# Optimizing a Trainium2 kernel written in Bass

```python
import math
import jax, jax.numpy as jnp
from jax import lax
import numpy as np

D_MODEL = 1024
BATCH = 1
SEQ = 256
DEPTH = 2

DA_HEADS = 4
DA_HEAD_DIM = 64
DA_QK_WIDTH = DA_HEADS * 2 * DA_HEAD_DIM
DA_V_WIDTH = DA_HEADS * 2 * DA_HEAD_DIM
MLA_HEADS = 8
MLA_Q_LORA = 384
MLA_KV_LORA = 256
MLA_NOPE = 64
MLA_ROPE = 32
MLA_V = 64
ROPE_THETA = 10000.0
SC_WIDTH = 512
SC_KERNEL = 3
CF_WIDTH = 512
CF_KERNEL = 31
N_BRANCHES = 4
FFN_DIM = 2816
FFN_KERNEL = 3
N_MOD = 6
Q_BLOCK = 128
NORM_EPS = 1e-6
LN_EPS = 1e-5
IN_SIZES = (DA_QK_WIDTH, DA_QK_WIDTH, DA_V_WIDTH,
            MLA_Q_LORA, MLA_KV_LORA, MLA_ROPE,
            SC_WIDTH, SC_WIDTH, SC_WIDTH,
            2 * CF_WIDTH,
            N_BRANCHES * D_MODEL)
IN_WIDTH = (3 * DA_QK_WIDTH + MLA_Q_LORA + MLA_KV_LORA + MLA_ROPE
            + 3 * SC_WIDTH + 2 * CF_WIDTH + N_BRANCHES * D_MODEL)


def rmsnorm(x, g):
    xf = x.astype(jnp.float32)
    y = xf * lax.rsqrt(jnp.mean(xf * xf, axis=-1, keepdims=True) + NORM_EPS)
    return (y * g.astype(jnp.float32)).astype(x.dtype)

def layernorm(x, g, b):
    xf = x.astype(jnp.float32)
    mu = jnp.mean(xf, axis=-1, keepdims=True)
    var = jnp.mean(jnp.square(xf - mu), axis=-1, keepdims=True)
    y = (xf - mu) * lax.rsqrt(var + LN_EPS)
    return (y * g.astype(jnp.float32) + b.astype(jnp.float32)).astype(x.dtype)

def causal_dwconv(x, w):
    k, ch = w.shape
    return lax.conv_general_dilated(
        x, w[:, None, :].astype(x.dtype), window_strides=(1,), padding=[(k - 1, 0)],
        dimension_numbers=('NWC', 'WIO', 'NWC'), feature_group_count=ch)

def rope_tables(positions):
    half = MLA_ROPE // 2
    inv_freq = ROPE_THETA ** (-jnp.arange(half, dtype=jnp.float32) / half)
    ang = positions.astype(jnp.float32)[:, :, None, None] * inv_freq
    return jnp.cos(ang), jnp.sin(ang)

def apply_rope(t, cos, sin):
    t1, t2 = jnp.split(t.astype(jnp.float32), 2, axis=-1)
    return jnp.concatenate([t1 * cos - t2 * sin, t2 * cos + t1 * sin], axis=-1).astype(t.dtype)

def to_blocks(t):
    b, s = t.shape[:2]
    return jnp.moveaxis(t.reshape((b, s // Q_BLOCK, Q_BLOCK) + t.shape[2:]), 1, 0)

def from_blocks(t):
    t = jnp.moveaxis(t, 0, 1)
    return t.reshape((t.shape[0], -1) + t.shape[3:])

def block_starts(s):
    return jnp.arange(s // Q_BLOCK, dtype=jnp.int32) * Q_BLOCK

def causal_probs(q_blk, k, q_start, scale):
    s = jnp.einsum('bqhd,bkhd->bhqk', q_blk, k).astype(jnp.float32) * scale
    q_pos = q_start + jnp.arange(q_blk.shape[1], dtype=jnp.int32)
    k_pos = jnp.arange(k.shape[1], dtype=jnp.int32)
    mask = k_pos[None, :] <= q_pos[:, None]
    return jax.nn.softmax(jnp.where(mask, s, -jnp.inf), axis=-1)

def differential_attention(q1, q2, k1, k2, v, lam):
    scale = DA_HEAD_DIM ** -0.5

    def one_block(args):
        q1b, q2b, st = args
        p = causal_probs(q1b, k1, st, scale) - lam * causal_probs(q2b, k2, st, scale)
        return jnp.einsum('bhqk,bkhd->bqhd', p.astype(v.dtype), v)

    out = lax.map(one_block, (to_blocks(q1), to_blocks(q2), block_starts(q1.shape[1])))
    return from_blocks(out)

def softmax_attention(q, k, v):
    scale = (MLA_NOPE + MLA_ROPE) ** -0.5

    def one_block(args):
        qb, st = args
        p = causal_probs(qb, k, st, scale)
        return jnp.einsum('bhqk,bkhd->bqhd', p.astype(v.dtype), v)

    out = lax.map(one_block, (to_blocks(q), block_starts(q.shape[1])))
    return from_blocks(out)

def token_mixing(x, shift, scale, cos, sin, layer_idx, g_pre, w_in,
                 lq1, lk1, lq2, lk2, g_subln, da_w_o,
                 g_cq, w_uq, g_ckv, w_ukv, mla_w_o,
                 sc_conv, sc_w_o,
                 cf_conv, cf_conv_b, cf_ln_g, cf_ln_b, cf_w_o,
                 w_mix_out, g_post):
    bsz, s, _ = x.shape
    h = rmsnorm(x, g_pre) * (1.0 + scale) + shift
    proj = h @ w_in
    split_idx = []
    acc = 0
    for size in IN_SIZES[:-1]:
        acc += size
        split_idx.append(acc)
    (da_q, da_k, da_v, mla_cq, mla_ckv, mla_kr,
     sc_u, sc_b, sc_c, cf_in, gates) = jnp.split(proj, split_idx, axis=-1)

    da_q = da_q.reshape(bsz, s, DA_HEADS, 2, DA_HEAD_DIM)
    da_k = da_k.reshape(bsz, s, DA_HEADS, 2, DA_HEAD_DIM)
    da_v = da_v.reshape(bsz, s, DA_HEADS, 2 * DA_HEAD_DIM)
    lam_init = 0.8 - 0.6 * math.exp(-0.3 * layer_idx)
    lam = (jnp.exp(jnp.sum(lq1.astype(jnp.float32) * lk1.astype(jnp.float32)))
           - jnp.exp(jnp.sum(lq2.astype(jnp.float32) * lk2.astype(jnp.float32))) + lam_init)
    ya = differential_attention(da_q[:, :, :, 0], da_q[:, :, :, 1],
                                da_k[:, :, :, 0], da_k[:, :, :, 1], da_v, lam)
    ya = rmsnorm(ya, g_subln) * (1.0 - lam_init)
    ya = ya.reshape(bsz, s, DA_V_WIDTH) @ da_w_o

    q = (rmsnorm(mla_cq, g_cq) @ w_uq).reshape(bsz, s, MLA_HEADS, MLA_NOPE + MLA_ROPE)
    q_nope, q_rope = jnp.split(q, [MLA_NOPE], axis=-1)
    q = jnp.concatenate([q_nope, apply_rope(q_rope, cos, sin)], axis=-1)
    kv = (rmsnorm(mla_ckv, g_ckv) @ w_ukv).reshape(bsz, s, MLA_HEADS, MLA_NOPE + MLA_V)
    k_nope, v_b = jnp.split(kv, [MLA_NOPE], axis=-1)
    k_rope = apply_rope(mla_kr[:, :, None, :], cos, sin)
    k = jnp.concatenate([k_nope, jnp.broadcast_to(k_rope, (bsz, s, MLA_HEADS, MLA_ROPE))], axis=-1)
    yb = softmax_attention(q, k, v_b).reshape(bsz, s, MLA_HEADS * MLA_V) @ mla_w_o

    yc = (sc_b * causal_dwconv(sc_c * sc_u, sc_conv)) @ sc_w_o

    cf_a, cf_g = jnp.split(cf_in, 2, axis=-1)
    u = cf_a * jax.nn.sigmoid(cf_g)
    u = causal_dwconv(u, cf_conv) + cf_conv_b
    u = jax.nn.silu(layernorm(u, cf_ln_g, cf_ln_b))
    yd = u @ cf_w_o

    g = jax.nn.sigmoid(gates).reshape(bsz, s, N_BRANCHES, D_MODEL)
    merged = g[:, :, 0] * ya + g[:, :, 1] * yb + g[:, :, 2] * yc + g[:, :, 3] * yd
    return rmsnorm(merged @ w_mix_out, g_post)

def channel_mixing(x, shift, scale, g_pre, w_up, ffn_conv, w_down, g_post):
    h = rmsnorm(x, g_pre) * (1.0 + scale) + shift
    a, b = jnp.split(h @ w_up, 2, axis=-1)
    y = (jax.nn.silu(causal_dwconv(a, ffn_conv)) * b) @ w_down
    return rmsnorm(y, g_post)

def first_inputs(seed: int = 0) -> dict:
    key = jax.random.key(seed)
    ks = iter(jax.random.split(key, 40))

    def nrm(shape, scale):
        return jax.random.normal(next(ks), shape, jnp.float32) * scale

    def gain(shape):
        return 1.0 + nrm(shape, 0.02)

    L = DEPTH
    return {
        "x": nrm((BATCH, SEQ, D_MODEL), 1.0),
        "c": nrm((BATCH, D_MODEL), 1.0),
        "positions": jnp.broadcast_to(jnp.arange(SEQ, dtype=jnp.int32), (BATCH, SEQ)),
        "w_ada": nrm((L, D_MODEL, N_MOD * D_MODEL), 0.5 * D_MODEL ** -0.5),
        "b_ada": nrm((L, N_MOD * D_MODEL), 0.01),
        "g_pre_mix": gain((L, D_MODEL)),
        "w_in": nrm((L, D_MODEL, IN_WIDTH), D_MODEL ** -0.5),
        "da_lam_q1": nrm((L, DA_HEAD_DIM), 0.1),
        "da_lam_k1": nrm((L, DA_HEAD_DIM), 0.1),
        "da_lam_q2": nrm((L, DA_HEAD_DIM), 0.1),
        "da_lam_k2": nrm((L, DA_HEAD_DIM), 0.1),
        "da_g_subln": gain((L, 2 * DA_HEAD_DIM)),
        "da_w_o": nrm((L, DA_V_WIDTH, D_MODEL), DA_V_WIDTH ** -0.5),
        "mla_g_cq": gain((L, MLA_Q_LORA)),
        "mla_w_uq": nrm((L, MLA_Q_LORA, MLA_HEADS * (MLA_NOPE + MLA_ROPE)), MLA_Q_LORA ** -0.5),
        "mla_g_ckv": gain((L, MLA_KV_LORA)),
        "mla_w_ukv": nrm((L, MLA_KV_LORA, MLA_HEADS * (MLA_NOPE + MLA_V)), MLA_KV_LORA ** -0.5),
        "mla_w_o": nrm((L, MLA_HEADS * MLA_V, D_MODEL), (MLA_HEADS * MLA_V) ** -0.5),
        "sc_conv": nrm((L, SC_KERNEL, SC_WIDTH), SC_KERNEL ** -0.5),
        "sc_w_o": nrm((L, SC_WIDTH, D_MODEL), SC_WIDTH ** -0.5),
        "cf_conv": nrm((L, CF_KERNEL, CF_WIDTH), CF_KERNEL ** -0.5),
        "cf_conv_b": nrm((L, CF_WIDTH), 0.01),
        "cf_ln_g": gain((L, CF_WIDTH)),
        "cf_ln_b": nrm((L, CF_WIDTH), 0.01),
        "cf_w_o": nrm((L, CF_WIDTH, D_MODEL), CF_WIDTH ** -0.5),
        "w_mix_out": nrm((L, D_MODEL, D_MODEL), D_MODEL ** -0.5),
        "g_post_mix": gain((L, D_MODEL)),
        "g_pre_ffn": gain((L, D_MODEL)),
        "w_up": nrm((L, D_MODEL, 2 * FFN_DIM), D_MODEL ** -0.5),
        "ffn_conv": nrm((L, FFN_KERNEL, FFN_DIM), FFN_KERNEL ** -0.5),
        "w_down": nrm((L, FFN_DIM, D_MODEL), FFN_DIM ** -0.5),
        "g_post_ffn": gain((L, D_MODEL)),
    }

def first_block(x, c, positions, w_ada, b_ada, g_pre_mix, w_in,
              da_lam_q1, da_lam_k1, da_lam_q2, da_lam_k2, da_g_subln, da_w_o,
              mla_g_cq, mla_w_uq, mla_g_ckv, mla_w_ukv, mla_w_o,
              sc_conv, sc_w_o,
              cf_conv, cf_conv_b, cf_ln_g, cf_ln_b, cf_w_o,
              w_mix_out, g_post_mix, g_pre_ffn, w_up, ffn_conv, w_down, g_post_ffn):
    cos, sin = rope_tables(positions)
    c_act = jax.nn.silu(c)
    for l in range(DEPTH):
        mod = (c_act @ w_ada[l] + b_ada[l])[:, None, :]
        shift1, scale1, gate1, shift2, scale2, gate2 = jnp.split(mod, N_MOD, axis=-1)
        x = x + gate1 * token_mixing(
            x, shift1, scale1, cos, sin, l, g_pre_mix[l], w_in[l],
            da_lam_q1[l], da_lam_k1[l], da_lam_q2[l], da_lam_k2[l], da_g_subln[l], da_w_o[l],
            mla_g_cq[l], mla_w_uq[l], mla_g_ckv[l], mla_w_ukv[l], mla_w_o[l],
            sc_conv[l], sc_w_o[l],
            cf_conv[l], cf_conv_b[l], cf_ln_g[l], cf_ln_b[l], cf_w_o[l],
            w_mix_out[l], g_post_mix[l])
        x = x + gate2 * channel_mixing(
            x, shift2, scale2, g_pre_ffn[l], w_up[l], ffn_conv[l], w_down[l], g_post_ffn[l])
    return x


DEPTH_2 = 4

N_MIXERS = 3
PLE_DIM = 256
D_FF = 2816
EPS = 1e-6
HG_HEADS = 8
HG_DK = D_MODEL // HG_HEADS
HG_DV = D_MODEL // HG_HEADS
HG_CHUNK = 64
ML_HEADS = 4
ML_DQK = D_MODEL // 2 // ML_HEADS
ML_DV = D_MODEL // ML_HEADS
ML_CHUNK = 64
ML_GATE_CAP = 15.0
SW_HEADS = 16
SW_KV_HEADS = 4
SW_GROUP = SW_HEADS // SW_KV_HEADS
SW_HD = 64
WINDOW = 128
SW_BLOCK = 128
N_A = (DEPTH_2 + 2) // 3
N_B = (DEPTH_2 + 1) // 3
N_C = DEPTH_2 // 3


def rmsnorm_2(x, gain):
    xf = x.astype(jnp.float32)
    y = xf * lax.rsqrt(jnp.mean(xf * xf, axis=-1, keepdims=True) + EPS)
    return (y * gain.astype(jnp.float32)).astype(x.dtype)

def swiglu(x, w_gu, w_down):
    g, u = jnp.split(x @ w_gu, 2, axis=-1)
    return (jax.nn.silu(g) * u) @ w_down

def to_chunks(t, L):
    B, T, H, d = t.shape
    return t.reshape(B, T // L, L, H, d).transpose(1, 0, 3, 2, 4)

def from_chunks(t):
    N, B, H, L, d = t.shape
    return t.transpose(1, 0, 3, 2, 4).reshape(B, N * L, H, d)

def gate_chunks(t, L):
    B, T, H = t.shape
    return t.reshape(B, T // L, L, H).transpose(1, 0, 3, 2)

def alibi_slopes(n_heads):
    return jnp.asarray([2.0 ** (-8.0 * (h + 1) / n_heads) for h in range(n_heads)], jnp.float32)

def hgrn2_mixer(x, lb, w_in, g_norm, w_out):
    B, T, _ = x.shape
    q, f, i, og = jnp.split(x @ w_in, 4, axis=-1)
    q = jax.nn.silu(q).astype(jnp.float32)
    f = f.astype(jnp.float32)
    lb = lb.astype(jnp.float32)
    log_f = jnp.logaddexp(jnp.log(lb), jnp.log1p(-lb) + jax.nn.log_sigmoid(f))
    k = (1.0 - lb) * jax.nn.sigmoid(-f)
    L = HG_CHUNK
    qc = to_chunks(q.reshape(B, T, HG_HEADS, HG_DK), L)
    kc = to_chunks(k.reshape(B, T, HG_HEADS, HG_DK), L)
    gc = to_chunks(log_f.reshape(B, T, HG_HEADS, HG_DK), L)
    vc = to_chunks(i.astype(jnp.float32).reshape(B, T, HG_HEADS, HG_DV), L)
    causal = jnp.tril(jnp.ones((L, L), bool))

    def step(S, inp):
        q_, k_, v_, g_ = inp
        b = jnp.cumsum(g_, axis=2)
        o_inter = jnp.einsum('bhtk,bhkv->bhtv', q_ * jnp.exp(b), S)
        diff = b[:, :, :, None, :] - b[:, :, None, :, :]
        decay = jnp.exp(jnp.where(causal[:, :, None], diff, -jnp.inf))
        A = jnp.einsum('bhtk,bhsk,bhtsk->bhts', q_, k_, decay)
        o_intra = jnp.einsum('bhts,bhsv->bhtv', A, v_)
        b_last = b[:, :, -1:, :]
        S_new = jnp.exp(b_last[:, :, 0, :])[..., None] * S + jnp.einsum(
            'bhsk,bhsv->bhkv', k_ * jnp.exp(b_last - b), v_)
        return S_new, o_inter + o_intra

    S0 = jnp.zeros((B, HG_HEADS, HG_DK, HG_DV), jnp.float32)
    _, o = lax.scan(step, S0, (qc, kc, vc, gc))
    o = rmsnorm_2(from_chunks(o), g_norm)
    o = o.reshape(B, T, D_MODEL).astype(x.dtype) * jax.nn.silu(og)
    return o @ w_out

def mlstm_mixer(x, w_qkvo, w_if, b_if, norm_g, w_out):
    B, T, _ = x.shape
    dqk_all = ML_HEADS * ML_DQK
    q, k, v, og = jnp.split(x @ w_qkvo, [dqk_all, 2 * dqk_all, 2 * dqk_all + D_MODEL], axis=-1)
    gates = (x @ w_if).astype(jnp.float32) + b_if.astype(jnp.float32)
    gates = ML_GATE_CAP * jnp.tanh(gates / ML_GATE_CAP)
    ig, fg = jnp.split(gates, 2, axis=-1)
    lf = jax.nn.log_sigmoid(fg)
    L = ML_CHUNK
    qc = to_chunks(q.astype(jnp.float32).reshape(B, T, ML_HEADS, ML_DQK), L)
    kc = to_chunks(k.astype(jnp.float32).reshape(B, T, ML_HEADS, ML_DQK), L) * (ML_DQK ** -0.5)
    vc = to_chunks(v.astype(jnp.float32).reshape(B, T, ML_HEADS, ML_DV), L)
    ic = gate_chunks(ig, L)
    fc = gate_chunks(lf, L)
    causal = jnp.tril(jnp.ones((L, L), bool))

    def step(carry, inp):
        C, n, m = carry
        q_, k_, v_, i_, f_ = inp
        b = jnp.cumsum(f_, axis=-1)
        log_intra = jnp.where(causal, b[..., :, None] - b[..., None, :] + i_[..., None, :], -jnp.inf)
        log_inter = b + m[..., None]
        m_t = jnp.maximum(jnp.max(log_intra, axis=-1), log_inter)
        w_intra = jnp.exp(log_intra - m_t[..., None])
        w_inter = jnp.exp(log_inter - m_t)
        scores = jnp.einsum('bhtk,bhsk->bhts', q_, k_) * w_intra
        num = w_inter[..., None] * jnp.einsum('bhtk,bhkv->bhtv', q_, C) + jnp.einsum('bhts,bhsv->bhtv', scores, v_)
        den = w_inter * jnp.einsum('bhtk,bhk->bht', q_, n) + jnp.sum(scores, axis=-1)
        h = num / jnp.maximum(jnp.abs(den), jnp.exp(-m_t))[..., None]
        b_L = b[..., -1]
        log_state = b_L + m
        log_src = b_L[..., None] - b + i_
        m_new = jnp.maximum(log_state, jnp.max(log_src, axis=-1))
        w_src = jnp.exp(log_src - m_new[..., None])
        decay = jnp.exp(log_state - m_new)
        C_new = decay[..., None, None] * C + jnp.einsum('bhsk,bhsv->bhkv', k_ * w_src[..., None], v_)
        n_new = decay[..., None] * n + jnp.einsum('bhs,bhsk->bhk', w_src, k_)
        return (C_new, n_new, m_new), h

    carry0 = (jnp.zeros((B, ML_HEADS, ML_DQK, ML_DV), jnp.float32),
              jnp.zeros((B, ML_HEADS, ML_DQK), jnp.float32),
              jnp.zeros((B, ML_HEADS), jnp.float32))
    _, h = lax.scan(step, carry0, (qc, kc, vc, ic, fc))
    h = rmsnorm_2(from_chunks(h), norm_g.reshape(ML_HEADS, ML_DV))
    h = h.reshape(B, T, D_MODEL).astype(x.dtype) * jax.nn.sigmoid(og)
    return h @ w_out

def swa_mixer(x, w_qkv, q_gain, k_gain, sinks, w_o):
    B, T, _ = x.shape
    nq = SW_HEADS * SW_HD
    nk = SW_KV_HEADS * SW_HD
    q, k, v = jnp.split(x @ w_qkv, [nq, nq + nk], axis=-1)
    q = rmsnorm_2(q.reshape(B, T, SW_HEADS, SW_HD), q_gain)
    k = rmsnorm_2(k.reshape(B, T, SW_KV_HEADS, SW_HD), k_gain)
    v = v.reshape(B, T, SW_KV_HEADS, SW_HD)
    nb = T // SW_BLOCK
    qb = q.reshape(B, nb, SW_BLOCK, SW_KV_HEADS, SW_GROUP, SW_HD)

    def band(t):
        tb = t.reshape(B, nb, SW_BLOCK, SW_KV_HEADS, SW_HD)
        prev = jnp.pad(tb, ((0, 0), (1, 0), (0, 0), (0, 0), (0, 0)))[:, :-1]
        return jnp.concatenate([prev, tb], axis=2)

    kk, vv = band(k), band(v)
    s = jnp.einsum('bnqkgd,bnskd->bnkgqs', qb, kk).astype(jnp.float32) * (SW_HD ** -0.5)
    qpos = jnp.arange(SW_BLOCK)
    kpos = jnp.arange(2 * SW_BLOCK) - SW_BLOCK
    dist = (qpos[:, None] - kpos[None, :]).astype(jnp.float32)
    blk_start = jnp.arange(nb) * SW_BLOCK
    valid = (dist >= 0) & (dist < WINDOW) & ((blk_start[:, None, None] + kpos[None, None, :]) >= 0)
    slopes = alibi_slopes(SW_HEADS).reshape(SW_KV_HEADS, SW_GROUP)
    s = s - slopes[:, :, None, None] * dist
    s = jnp.where(valid[None, :, None, None], s, -jnp.inf)
    sink = jnp.broadcast_to(sinks.astype(jnp.float32).reshape(SW_KV_HEADS, SW_GROUP)[:, :, None, None],
                            s.shape[:-1] + (1,))
    probs = jax.nn.softmax(jnp.concatenate([s, sink], axis=-1), axis=-1)[..., :-1]
    o = jnp.einsum('bnkgqs,bnskd->bnqkgd', probs.astype(vv.dtype), vv).reshape(B, T, nq)
    return o @ w_o

def second_inputs(seed: int = 0) -> dict:
    key = jax.random.key(seed)
    ks = jax.random.split(key, 24)
    f32 = jnp.float32

    def nrm(k, shape, fan_in):
        return jax.random.normal(k, shape, f32) * (fan_in ** -0.5)

    D = D_MODEL
    b_if = jnp.concatenate([
        0.1 * jax.random.normal(ks[11], (N_B, ML_HEADS), f32),
        jnp.linspace(3.0, 6.0, ML_HEADS, dtype=f32)[None, :] + 0.1 * jax.random.normal(ks[12], (N_B, ML_HEADS), f32),
    ], axis=-1)
    return {
        "x": jax.random.normal(ks[0], (BATCH, SEQ, D), f32),
        "p": jax.random.normal(ks[1], (DEPTH_2, BATCH, SEQ, PLE_DIM), f32),
        "norm_gains": 1.0 + 0.02 * jax.random.normal(ks[2], (DEPTH_2, 4, D), f32),
        "w_ffn_gu": nrm(ks[3], (DEPTH_2, 2, D, 2 * D_FF), D),
        "w_ffn_down": nrm(ks[4], (DEPTH_2, 2, D_FF, D), D_FF),
        "w_ple_gate": nrm(ks[5], (DEPTH_2, D, D), D),
        "w_ple_proj": nrm(ks[6], (DEPTH_2, PLE_DIM, D), PLE_DIM),
        "hg_lower_bounds": 0.5 * jax.random.normal(ks[7], (DEPTH_2, D), f32),
        "hg_w_in": nrm(ks[8], (N_A, D, 4 * D), D),
        "hg_g_norm": 1.0 + 0.02 * jax.random.normal(ks[9], (N_A, HG_DV), f32),
        "hg_w_out": nrm(ks[10], (N_A, D, D), D),
        "ml_w_qkvo": nrm(ks[13], (N_B, D, 2 * ML_HEADS * ML_DQK + 2 * D), D),
        "ml_w_if": nrm(ks[14], (N_B, D, 2 * ML_HEADS), D),
        "ml_b_if": b_if,
        "ml_norm": 1.0 + 0.02 * jax.random.normal(ks[15], (N_B, D), f32),
        "ml_w_out": nrm(ks[16], (N_B, D, D), D),
        "sw_w_qkv": nrm(ks[17], (N_C, D, (SW_HEADS + 2 * SW_KV_HEADS) * SW_HD), D),
        "sw_q_norm": 1.0 + 0.02 * jax.random.normal(ks[18], (N_C, SW_HD), f32),
        "sw_k_norm": 1.0 + 0.02 * jax.random.normal(ks[19], (N_C, SW_HD), f32),
        "sw_sinks": 0.5 * jax.random.normal(ks[20], (N_C, SW_HEADS), f32),
        "sw_w_o": nrm(ks[21], (N_C, SW_HEADS * SW_HD, D), SW_HEADS * SW_HD),
    }

def second_block(x, p, norm_gains, w_ffn_gu, w_ffn_down, w_ple_gate, w_ple_proj,
              hg_lower_bounds, hg_w_in, hg_g_norm, hg_w_out,
              ml_w_qkvo, ml_w_if, ml_b_if, ml_norm, ml_w_out,
              sw_w_qkv, sw_q_norm, sw_k_norm, sw_sinks, sw_w_o):
    lbs = jnp.cumsum(jax.nn.softmax(hg_lower_bounds.astype(jnp.float32), axis=0), axis=0)
    lbs = lbs - lbs[0:1]
    for layer in range(DEPTH_2):
        g = norm_gains[layer]
        h = x + 0.5 * swiglu(rmsnorm_2(x, g[0]), w_ffn_gu[layer, 0], w_ffn_down[layer, 0])
        xn = rmsnorm_2(h, g[1])
        kind = layer % N_MIXERS
        j = layer // N_MIXERS
        if kind == 0:
            mix = hgrn2_mixer(xn, lbs[layer], hg_w_in[j], hg_g_norm[j], hg_w_out[j])
        elif kind == 1:
            mix = mlstm_mixer(xn, ml_w_qkvo[j], ml_w_if[j], ml_b_if[j], ml_norm[j], ml_w_out[j])
        else:
            mix = swa_mixer(xn, sw_w_qkv[j], sw_q_norm[j], sw_k_norm[j], sw_sinks[j], sw_w_o[j])
        h = h + mix
        h = h + 0.5 * swiglu(rmsnorm_2(h, g[2]), w_ffn_gu[layer, 1], w_ffn_down[layer, 1])
        gate = jax.nn.sigmoid(rmsnorm_2(h, g[3]) @ w_ple_gate[layer])
        x = h + gate * (p[layer] @ w_ple_proj[layer])
    return x


def setup_inputs(seed=0):
    out = dict(first_inputs(seed))
    for name, value in second_inputs(seed + 1).items():
        if name != "x":
            out[name + "_2"] = value
    return out


def reference(
    x, c, positions, w_ada, b_ada, g_pre_mix, w_in, da_lam_q1, da_lam_k1, da_lam_q2, da_lam_k2,
    da_g_subln, da_w_o, mla_g_cq, mla_w_uq, mla_g_ckv, mla_w_ukv, mla_w_o, sc_conv, sc_w_o,
    cf_conv, cf_conv_b, cf_ln_g, cf_ln_b, cf_w_o, w_mix_out, g_post_mix, g_pre_ffn, w_up,
    ffn_conv, w_down, g_post_ffn, p_2, norm_gains_2, w_ffn_gu_2, w_ffn_down_2, w_ple_gate_2,
    w_ple_proj_2, hg_lower_bounds_2, hg_w_in_2, hg_g_norm_2, hg_w_out_2, ml_w_qkvo_2, ml_w_if_2,
    ml_b_if_2, ml_norm_2, ml_w_out_2, sw_w_qkv_2, sw_q_norm_2, sw_k_norm_2, sw_sinks_2,
    sw_w_o_2,
):
    x = first_block(
        x, c, positions, w_ada, b_ada, g_pre_mix, w_in, da_lam_q1, da_lam_k1, da_lam_q2,
        da_lam_k2, da_g_subln, da_w_o, mla_g_cq, mla_w_uq, mla_g_ckv, mla_w_ukv, mla_w_o,
        sc_conv, sc_w_o, cf_conv, cf_conv_b, cf_ln_g, cf_ln_b, cf_w_o, w_mix_out, g_post_mix,
        g_pre_ffn, w_up, ffn_conv, w_down, g_post_ffn,
    )
    return second_block(
        x, p_2, norm_gains_2, w_ffn_gu_2, w_ffn_down_2, w_ple_gate_2, w_ple_proj_2,
        hg_lower_bounds_2, hg_w_in_2, hg_g_norm_2, hg_w_out_2, ml_w_qkvo_2, ml_w_if_2,
        ml_b_if_2, ml_norm_2, ml_w_out_2, sw_w_qkv_2, sw_q_norm_2, sw_k_norm_2, sw_sinks_2,
        sw_w_o_2,
    )


_drawn_inputs = setup_inputs


def setup_inputs(seed=0):
    import zlib

    import numpy as np

    out = dict(_drawn_inputs(seed))
    spreads = {}
    factors = {'g_pre_mix': 3.205,
     'da_lam_q1': 4.409,
     'da_lam_k1': 3.784,
     'da_lam_q2': 6.914,
     'da_lam_k2': 4.092,
     'da_g_subln': 8.0,
     'mla_g_cq': 8.0,
     'mla_g_ckv': 8.0,
     'cf_conv_b': 8.0,
     'cf_ln_g': 8.0,
     'cf_ln_b': 42.404,
     'g_post_mix': 4.383,
     'g_pre_ffn': 3.864,
     'g_post_ffn': 5.083,
     'hg_lower_bounds_2': 3.101,
     'hg_g_norm_2': 4.939,
     'ml_norm_2': 8.0,
     'sw_q_norm_2': 8.0,
     'sw_k_norm_2': 22.756,
     'sw_sinks_2': 23.376}
    for name, (base, spread) in spreads.items():
        noise = np.random.default_rng([zlib.crc32(name.encode()), seed]).standard_normal(out[name].shape)
        drawn = base * np.exp(spread * noise) if base else spread * noise
        out[name] = __import__('jax').numpy.asarray(drawn.astype(out[name].dtype))
    for name, factor in factors.items():
        out[name] = (out[name] * factor).astype(out[name].dtype)
    return out
```

```python
import math
from contextlib import ExitStack

import numpy as np
import concourse.bass as bass
from concourse import mybir

F32 = mybir.dt.float32
F32R = mybir.dt.float32r
I32 = mybir.dt.int32
ALU = mybir.AluOpType
ACT = mybir.ActivationFunctionType
AX = mybir.AxisListType.X

D = 1024
T = 256
NC = 8
NF = 22
TILE = 2048
NEG = -1e30

PARAM_COLS = {}


def _plan_params():
    at = 0
    for name, n in [("c", 8), ("g_pre_mix", 16), ("b_ada", 96), ("lam", 8), ("da_g_subln", 2),
                    ("mla_g_cq", 6), ("mla_g_ckv", 4), ("sc_conv", 24), ("cf_conv", 248),
                    ("cf_conv_b", 8), ("cf_ln_g", 8), ("cf_ln_b", 8), ("g_post_mix", 16),
                    ("g_pre_ffn", 16), ("ffn_conv", 132), ("g_post_ffn", 16), ("norm_gains", 128),
                    ("hg_lb", 32), ("hg_g_norm", 2), ("ml_b_if", 2), ("ml_norm", 8),
                    ("sw_q_norm", 1), ("sw_k_norm", 1), ("sw_sinks", 16), ("w_if", 64)]:
        PARAM_COLS[name] = at
        at += n
    return at


NPAR = _plan_params()

CONST_COLS = {}


def _plan_consts():
    at = 0
    for name, n in [("ident", 128), ("ones", 128), ("ones64", 128), ("mask3", 384), ("dist3", 384),
                    ("maskT", 128), ("lev", 192), ("rot", 96), ("inv", 1), ("rst", 256)]:
        CONST_COLS[name] = at
        at += n
    return at


NCON = _plan_consts()


def constants():
    c = np.zeros((128, NCON), np.float32)

    def put(name, a):
        c[:a.shape[0], CONST_COLS[name]:CONST_COLS[name] + a.shape[1]] = a

    i = np.arange(128)
    put("ident", np.eye(128, dtype=np.float32))
    put("ones", np.ones((128, 128), np.float32))
    put("ones64", (i[:, None] // 64 == i[None, :] // 64).astype(np.float32))
    causal = np.where(i[None, :] <= i[:, None], 0.0, NEG)
    put("mask3", np.concatenate([causal, np.zeros((128, 128)), causal], 1))
    same = i[:, None] - i[None, :]
    prev = same + 128
    put("dist3", np.concatenate([np.where(same >= 0, same, -NEG * 1e3), np.where(prev < 128, prev, -NEG * 1e3),
                                 np.where(same >= 0, same, -NEG * 1e3)], 1))
    put("maskT", (i[None, :] >= i[:, None]).astype(np.float32))
    s = (i % 32)[:, None]
    t = np.arange(32)[None, :]
    lev = []
    for m in (16, 8, 4, 2, 1):
        lev.append((s // (2 * m) == t // (2 * m)) & (s % (2 * m) < m) & (t % (2 * m) >= m))
    lev.append(s == t)
    put("lev", np.concatenate(lev, 1).astype(np.float32))
    rot = np.zeros((128, 96), np.float32)
    for n in range(16):
        rot[80 + n, 64 + n] = -1.0
        rot[64 + n, 80 + n] = 1.0
    put("rot", rot)
    inv = np.zeros((128, 1), np.float32)
    f = (np.float32(10000.0) ** (-np.arange(16, dtype=np.float32) / np.float32(16))).astype(np.float32)
    inv[64:80, 0] = f
    inv[80:96, 0] = f
    put("inv", inv)
    put("rst", np.tile((np.arange(256) % 64 != 0).astype(np.float32), (128, 1)))
    return c


def tiles_kn(w, cols):
    k = w.shape[0] // 128
    return np.ascontiguousarray(w[:, cols].reshape(k, 128, len(cols)).transpose(1, 0, 2)).reshape(128, -1)


def _span(a, n):
    return list(range(a, a + n))


def plan_win():
    t = []
    for j in range(4):
        t.append(_span(3744 + 128 * j, 128) + _span(3744 + 512 + 128 * j, 128))
    for j in range(6):
        t.append(_span(256 * j, 256))
    for j in range(4):
        t.append(_span(2208 + 128 * j, 128) + _span(2208 + 1024 + 128 * j, 128))
    for j in range(2):
        t.append(_span(2208 + 512 + 256 * j, 256))
    for j in range(2):
        t.append(_span(1536 + 256 * j, 256))
    for j in range(16):
        t.append(_span(4768 + 256 * j, 256))
    return t


WIN = plan_win()
CF0, DA0, SCU0, SCB0, MLA0, GATE0 = 0, 4, 10, 14, 16, 18
TWO_PI = 2.0 * math.pi


class Queue:
    def __init__(self, sem, on=True):
        self.sem, self.n, self.ops, self.seen, self.on = sem, 0, [], {}, on

    def wait(self, *tokens):
        for t in tokens:
            if t is None:
                continue
            if isinstance(t, list):
                self.wait(*t)
                continue
            sem, v = t
            if v > 0 and self.seen.get(sem.name, 0) < v:
                self.seen[sem.name] = v
                self.ops.append(("w", sem, v))

    def op(self, fn, *after):
        self.wait(*after)
        self.n += 1
        self.ops.append(("i", fn, self.sem, 1))
        return (self.sem, self.n)

    def quiet(self, fn, *after):
        self.wait(*after)
        self.ops.append(("q", fn))

    def dma(self, fn, sem, *after):
        self.wait(*after)
        self.ops.append(("i", fn, sem, 16))

    def last(self):
        return (self.sem, self.n)

    def play(self, eng):
        for o in self.ops:
            if o[0] == "w":
                eng.wait_ge(o[1], o[2])
            elif o[0] == "i":
                o[1](eng).then_inc(o[2], o[3])
            else:
                o[1](eng)


class Buf:
    def __init__(self, ap):
        self.ap, self.free = ap, []


class Ring:

    def __init__(self, aps):
        self.bufs = [Buf(a) for a in aps]

    def get(self):
        return self.bufs.pop(0)

    def put(self, buf, *tokens):
        buf.free = [t for t in tokens]
        self.bufs.append(buf)


class Program:
    def __init__(self, nc, ctx, args, order, depth=2):
        self.nc, self.args, self.order, self.asked, self.ready = nc, args, order, 0, []
        self.depth = depth

        def sem(name):
            return ctx.enter_context(nc.semaphore(name))

        def sb(name, n, dt=F32):
            return ctx.enter_context(nc.sbuf_tensor(name, [128, n], dt))

        self.pe, self.act, self.dve, self.pool, self.sp = [Queue(sem("s_" + n)) for n in
                                                           ("pe", "act", "dve", "pool", "sp")]
        self.NL, self.NS = 3, 3
        self.land = sb("land", self.NL * TILE)
        self.whi = sb("whi", self.NS * TILE, F32R)
        self.wlo = sb("wlo", self.NS * TILE, F32R)
        self.s_land = [sem(f"s_land{i}") for i in range(self.NL)]
        self.s_misc = sem("s_misc")
        self.s_out = sem("s_out")
        self.s_p = [sem("s_p0"), sem("s_p1")]
        self.n_p = 0
        self.nload = 0
        self.nsplit = 0
        self.land_free = [[] for _ in range(self.NL)]
        self.land_use = [0] * self.NL
        self.split_free = [[] for _ in range(self.NS)]
        self.x = sb("x", NC * T)
        self.hh = sb("hh", NC * T, F32R)
        self.hl = sb("hl", NC * T, F32R)
        self.par = sb("par", NPAR)
        self.con = sb("con", NCON)
        self.fa = sb("fa", 11392)
        self.ra = sb("ra", 8704, F32R)
        self.attn = sb("attn", 1152)
        self.trig = sb("trig", 512)
        self.mod = sb("mod", 96)
        self.tmps = sb("tmps", 4 * 512)
        self.small = sb("small", 1024)
        self.ps = Ring([ctx.enter_context(nc.psum_tensor(f"ps{i}", [128, 512], F32)) for i in range(8)])
        self.cols = Ring([self.small[:, 600 + i * 16:616 + i * 16] for i in range(4)])
        self.tmp = Ring([self.tmps[:, i * 512:(i + 1) * 512] for i in range(4)])

    def P(self, name, j, rows=128):
        a = PARAM_COLS[name] + j
        return self.par[0:rows, a:a + 1]

    def C(self, name, a, n, p0=0, p1=128):
        a += CONST_COLS[name]
        return self.con[p0:p1, a:a + n]

    def _prepare(self):
        i = len(self.ready)
        name, n, split = self.order[i]
        s = self.nload % self.NL
        self.nload += 1
        self.land_use[s] += 1
        src = self.args[name][n]
        w = src.shape[1]
        dst = self.land[:, s * TILE:s * TILE + w]
        self.sp.dma(lambda e, d=dst, a=src: e.dma_start(d, a), self.s_land[s], *self.land_free[s])
        got = (self.s_land[s], 16 * self.land_use[s])
        if not split:
            self.ready.append((dst, None, got, s, None))
            self.land_free[s] = None
            return
        k = self.nsplit % self.NS
        self.nsplit += 1
        hi, lo = self.whi[:, k * TILE:k * TILE + w], self.wlo[:, k * TILE:k * TILE + w]
        t1 = self.act.op(lambda e, o=hi, a=dst: e.activation(o, a, ACT.Copy), got, *self.split_free[k])
        t2 = self.dve.op(lambda e, o=lo, a=dst, b=hi.bitcast(F32): e.tensor_tensor(o, a, b, ALU.subtract),
                         got, t1, *self.split_free[k])
        self.land_free[s] = [t1, t2]
        self.split_free[k] = None
        self.ready.append((hi, lo, t2, s, k))

    def weight(self, name, n, split=True):
        i = self.asked
        self.asked += 1
        assert self.order[i] == (name, n, split)
        top = min(i + self.depth, len(self.order))
        while len(self.ready) <= i or (len(self.ready) < top and self._room()):
            self._prepare()
        return self.ready[i]

    def _room(self):
        name, n, split = self.order[len(self.ready)]
        return self.land_free[self.nload % self.NL] is not None and (
            not split or self.split_free[self.nsplit % self.NS] is not None)

    def done(self, w, token):
        if w[4] is None:
            self.land_free[w[3]] = [token]
        else:
            self.split_free[w[4]] = [token]

    def mm3(self, out, wh, wl, xh, xl, first, last, skip=False, inc=False, after=()):
        pe = self.pe
        pe.wait(*after)
        pe.quiet(lambda e: e.matmul(out, wh, xh, start=first, stop=False, skip_group_check=skip))
        pe.quiet(lambda e: e.matmul(out, wh, xl, start=False, stop=False, skip_group_check=skip))
        fn = lambda e: e.matmul(out, wl, xh, start=False, stop=last, skip_group_check=skip)
        if inc:
            return pe.op(fn)
        pe.quiet(fn)

    def mm(self, out, lhsT, rhs, first=True, last=True, after=(), inc=True, skip=False):
        fn = lambda e: e.matmul(out, lhsT, rhs, start=first, stop=last, skip_group_check=skip)
        self.pe.wait(*after)
        if inc:
            return self.pe.op(fn)
        self.pe.quiet(fn)

    def xk(self, t, k):
        return t[:, k * T:(k + 1) * T]

    def v_tt(self, out, a, b, op, *after):
        return self.dve.op(lambda e: e.tensor_tensor(out, a, b, op), *after)

    def v_ts(self, out, a, s1, s2, op0, op1, *after):
        if op1 is None:
            return self.dve.op(lambda e: e.tensor_scalar(out, a, s1, None, op0), *after)
        return self.dve.op(lambda e: e.tensor_scalar(out, a, s1, s2, op0, op1), *after)

    def v_stt(self, out, a, s, b, op0, op1, *after):
        return self.dve.op(lambda e: e.scalar_tensor_tensor(out, a, s, b, op0, op1), *after)

    def v_copy(self, out, a, *after):
        return self.dve.op(lambda e: e.tensor_copy(out, a), *after)

    def a_act(self, out, a, f, *after, **kw):
        return self.act.op(lambda e: e.activation(out, a, f, **kw), *after)

    def split_act(self, hi, lo, src, *after):
        t1 = self.a_act(hi, src, ACT.Copy, *after)
        return t1, self.v_tt(lo, src, hi.bitcast(F32), ALU.subtract, t1, *after)

    def rsqrt(self, out, v, t):
        b = self.tmp.get()
        n = v.shape[1]
        p = v.shape[0]
        y, z = b.ap[0:p, 0:n], b.ap[0:p, 256:256 + n]
        t1 = self.a_act(y, v, ACT.Ln, t, *b.free)
        t1 = self.a_act(y, y, ACT.Exp, t1, scale=-0.5)
        t2 = self.v_tt(z, y, y, ALU.mult, t1, *b.free)
        t2 = self.v_tt(z, z, v, ALU.mult, t2)
        t2 = self.v_ts(z, z, -0.5, 1.5, ALU.mult, ALU.add, t2)
        t2 = self.v_tt(out, y, z, ALU.mult, t2)
        self.tmp.put(b, t1, t2)
        return t2

    def stats(self, src, n, dim, eps, out, vbuf, sq, after):
        t1 = self.a_act(sq[:, 0:n * T], src, ACT.Square, *after)
        b = self.tmp.get()
        t2 = self.dve.op(lambda e: e.tensor_reduce(
            b.ap[:, 0:T], sq[:, 0:n * T].rearrange("p (c t) -> p t c", c=n), AX, ALU.add), t1, *b.free)
        ps = self.ps.get()
        t3 = self.mm(ps.ap[:, 0:T], self.C("ones", 0, 128), b.ap[:, 0:T], after=[t2, *ps.free])
        self.tmp.put(b, t3)
        t4 = self.v_ts(vbuf, ps.ap[:, 0:T], 1.0 / dim, eps, ALU.mult, ALU.add, t3, *after)
        self.ps.put(ps, t4)
        return self.rsqrt(out, vbuf, t4), t1

    def group(self, w, kc, width, xh, xl, cols, out, after, m=128, per_k=None):
        wh, wl = w[0], w[1]
        for k in range(kc):
            a = k * width + cols
            ready = [w[2], *after] if k == 0 else []
            if per_k:
                ready = ready + [per_k[k]]
            tok = self.mm3(out, wh[:, a:a + m], wl[:, a:a + m], self.xk(xh, k), self.xk(xl, k),
                           k == 0, k == kc - 1, inc=k == kc - 1, after=ready)
        return tok

    def proj(self, name, n, kc, width, xh, xl, after, per_k=None):
        w = self.weight(name, n)
        out = []
        ng = (width + 127) // 128
        for j in range(0, ng, 2):
            ps = self.ps.get()
            for i in range(j, min(j + 2, ng)):
                tok = self.group(w, kc, width, xh, xl, i * 128, ps.ap[:, (i - j) * T:(i - j + 1) * T],
                                 [*ps.free, *after], per_k=per_k)
            out.append((ps, tok))
        self.done(w, tok)
        return out

    def split_gain(self, gname, g0, n, src, after, free=()):
        toks = []
        for k in range(n):
            s, g = self.xk(src, k), self.P(gname, g0 + k)
            h, l = self.xk(self.hh, k), self.xk(self.hl, k)
            t1 = self.a_act(h, s, ACT.Identity, *after, *free, scale=g)
            t2 = self.v_stt(l, s, g, h.bitcast(F32), ALU.mult, ALU.subtract, t1, *after, *free)
            toks.append(t2)
        return toks


def bc2(ap):
    return ap.unsqueeze(1).broadcast_to([ap.shape[0], 2, ap.shape[1]])


def v2(ap):
    return ap.rearrange("p (a t) -> p a t", a=2)


def load_small(g):
    a = g.args
    g.sp.dma(lambda e: e.dma_start(g.par[:, :], a["params"]), g.s_misc)
    g.sp.dma(lambda e: e.dma_start(g.con[:, :], a["consts"]), g.s_misc)
    g.sp.dma(lambda e: e.dma_start(g.x[:, :], a["xT"]), g.s_misc)
    return (g.s_misc, 48)


def modulation(g, lay, out, sg, after):
    t = g.a_act(sg, g.par[:, PARAM_COLS["c"]:PARAM_COLS["c"] + 8], ACT.Silu, *after)
    ps = g.ps.get()
    for j in range(24):
        w = g.weight("w_ada", lay * 24 + j, split=False)
        for i in range(2):
            for k in range(8):
                tok = g.mm(ps.ap[:, 2 * j + i:2 * j + i + 1], w[0][:, k * 256 + i * 128:k * 256 + i * 128 + 128],
                           sg[:, k:k + 1], first=k == 0, last=k == 7, after=[w[2], t, *ps.free] if k == 0 else (),
                           inc=k == 7)
        g.done(w, tok)
    a = PARAM_COLS["b_ada"] + lay * 48
    t = g.v_tt(out, ps.ap[:, 0:48], g.par[:, a:a + 48], ALU.add, tok, *after)
    g.ps.put(ps, t)
    return t


def modulated(g, gname, lay, mod, shift, scale, after):
    fa = g.fa
    xr, v, r = fa[:, 0:2048], g.small[:, 0:256], g.small[:, 256:512]
    A = g.small[:, 560:568]
    gc = PARAM_COLS[gname] + lay * 8
    t0 = g.v_ts(A, mod[:, scale:scale + 8], 1.0, None, ALU.add, None, *after)
    t0 = g.v_tt(A, A, g.par[:, gc:gc + 8], ALU.mult, t0)
    t1, tsq = g.stats(g.x[:, :], 8, D, 1e-6, r, v, xr, after)
    toks = []
    for k in range(8):
        s = g.xk(xr, k)
        t2 = g.v_tt(s, g.xk(g.x, k), r, ALU.mult, t1, tsq)
        t2 = g.v_ts(s, s, A[:, k:k + 1], mod[:, shift + k:shift + k + 1], ALU.mult, ALU.add, t2, t0)
        _, t3 = g.split_act(g.xk(g.hh, k), g.xk(g.hl, k), s, t2, g.pe.last())
        toks.append(t3)
    return toks


def add_normed(g, y, lay, gname, mod, gate, ty):
    v, r = g.small[:, 0:256], g.small[:, 256:512]
    B = g.small[:, 560:568]
    gc = PARAM_COLS[gname] + lay * 8
    t0 = g.v_tt(B, mod[:, gate:gate + 8], g.par[:, gc:gc + 8], ALU.mult, *ty)
    t1, tsq = g.stats(y, 8, D, 1e-6, r, v, g.fa[:, 2048:4096], ty)
    for k in range(8):
        s = g.xk(y, k)
        t2 = g.v_tt(s, s, r, ALU.mult, t1, tsq)
        t2 = g.v_stt(g.xk(g.x, k), s, B[:, k:k + 1], g.xk(g.x, k), ALU.mult, ALU.add, t2, t0)
    return t2


def conv3(g, out, src, name, j, step, after):
    t = g.v_ts(out, src[:, 2:258], g.P(name, j + 2 * step), None, ALU.mult, None, *after)
    t = g.v_stt(out, src[:, 1:257], g.P(name, j + step), out, ALU.mult, ALU.add, t)
    return g.v_stt(out, src[:, 0:256], g.P(name, j), out, ALU.mult, ALU.add, t)


def down_setup(g):
    return [g.ps.get() for _ in range(4)]


def down_pair(g, name, n, acc, yb, ty, first, last):
    w = g.weight(name, n)
    yh, yl = yb.ap
    for c in range(2):
        for m in range(8):
            bank = acc[m // 2]
            a = c * 1024 + m * 128
            f = first and c == 0
            tok = g.mm3(bank.ap[:, (m % 2) * T:(m % 2 + 1) * T], w[0][:, a:a + 128], w[1][:, a:a + 128],
                        g.xk(yh, c), g.xk(yl, c), f and m % 2 == 0, last and c == 1, skip=True,
                        inc=m == 7 or (last and c == 1 and m % 2 == 1),
                        after=[w[2], *ty, *(bank.free if f else [])])
            if last and c == 1 and m % 2 == 1:
                bank.ready = tok
    g.done(w, tok)
    return tok


def ffn(g, up, up0, down, dn0, per_k, chunk):
    acc = down_setup(g)
    R = [Buf((g.ra[:, i * 1024:i * 1024 + 512], g.ra[:, i * 1024 + 512:i * 1024 + 1024])) for i in range(3)]
    for b in R:
        b.free = [g.pe.last()]
    ready = []
    npair = NF // 2

    def do_down(p):
        b, t = ready.pop(0)
        tok = down_pair(g, down, dn0 + p, acc, b, t, p == 0, p == npair - 1)
        b.free = [tok]
        R.append(b)

    for p in range(npair):
        b = R.pop(0)
        toks = []
        for c in range(2):
            (ps, tok), = g.proj(up, up0 + 2 * p + c, 8, 256, g.hh, g.hl, [], per_k=per_k)
            toks.append(chunk(2 * p + c, ps, tok, g.xk(b.ap[0], c), g.xk(b.ap[1], c), b.free))
        ready.append((b, toks))
        if p >= 1:
            do_down(p - 1)
    do_down(npair - 1)
    return acc


def first_ffn(g, lay, mod, tmod):
    base = [g.pe.last(), g.act.last(), g.dve.last(), tmod]
    per_k = modulated(g, "g_pre_ffn", lay, mod, 24, 32, base)
    fa = g.fa
    A = [Buf(fa[:, 4096 + i * 512:4096 + i * 512 + 258]) for i in range(2)]
    S = [Buf(fa[:, 5120 + i * 256:5376 + i * 256]) for i in range(2)]
    for b in A:
        t = g.dve.op(lambda e, b=b: e.memset(b.ap[:, 0:2], 0.0), *base)
        b.free = [t]

    def chunk(j, ps, tok, yh, yl, free):
        a, s = A[j % 2].ap, S[j % 2].ap
        t = g.v_copy(a[:, 2:258], ps.ap[:, 0:T], tok, *A[j % 2].free)
        o = g.tmp.get()
        c1 = o.ap[:, 0:T]
        t = conv3(g, c1, a, "ffn_conv", lay * 66 + j, 22, [t, *o.free])
        A[j % 2].free = [t]
        t1 = g.a_act(s, c1, ACT.Silu, t)
        t2 = g.v_tt(o.ap[:, T:2 * T], s, ps.ap[:, T:2 * T], ALU.mult, t1, tok)
        g.ps.put(ps, t2)
        t3, t4 = g.split_act(yh, yl, o.ap[:, T:2 * T], t2, *free)
        g.tmp.put(o, t3, t4)
        return t4

    acc = ffn(g, "w_up", lay * 22, "w_down", lay * 11, per_k, chunk)
    y = fa[:, 0:2048]
    ty = []
    for i, b in enumerate(acc):
        t = g.v_copy(y[:, i * 512:(i + 1) * 512], b.ap[:, :], b.ready)
        g.ps.put(b, t)
        ty.append(t)
    return add_normed(g, y, lay, "g_post_ffn", mod, 40, ty)


def softmax3(g, S, E, tps, ps, bias, scale, sink=None, post=None):
    b = g.cols.get()
    mx, nm, sm, rs = b.ap[:, 0:2], b.ap[:, 2:4], b.ap[:, 4:6], b.ap[:, 6:8]
    es = b.ap[:, 8:10]
    if isinstance(bias, tuple):
        t = g.v_stt(S, bias[0], -bias[1], ps.ap[:, 0:384], ALU.mult, ALU.add, tps, *post)
    else:
        t = g.v_tt(S, ps.ap[:, 0:384], bias, ALU.add, tps, *post)
    g.ps.put(ps, t)
    t1 = g.dve.op(lambda e: e.tensor_reduce(mx[:, 0:1], S[:, 0:128], AX, ALU.max), t, *b.free)
    t1 = g.dve.op(lambda e: e.tensor_reduce(mx[:, 1:2], S[:, 128:384], AX, ALU.max), t, *b.free)
    if sink is not None:
        t1 = g.v_ts(mx, mx, sink, None, ALU.max, None, t1)
    t1 = g.v_ts(nm, mx, -scale, None, ALU.mult, None, t1)
    t2 = g.a_act(E[:, 0:128], S[:, 0:128], ACT.Exp, t1, *post, bias=nm[:, 0:1], scale=scale, accum_out=sm[:, 0:1])
    t2 = g.a_act(E[:, 128:384], S[:, 128:384], ACT.Exp, t1, *post, bias=nm[:, 1:2], scale=scale,
                 accum_out=sm[:, 1:2])
    if sink is not None:
        t3 = g.a_act(es[:, 0:1], sink, ACT.Exp, t1, bias=nm[:, 0:1], scale=scale)
        t3 = g.a_act(es[:, 1:2], sink, ACT.Exp, t1, bias=nm[:, 1:2], scale=scale)
        t2 = g.v_tt(sm, sm, es, ALU.add, t2, t3)
    t3 = g.dve.op(lambda e: e.reciprocal(rs, sm), t2)
    return b, rs, t3


def turn3(g, E, PT, t, after):
    ps = g.ps.get()
    for i in range(3):
        tok = g.pe.op(lambda e, i=i: e.transpose(ps.ap[:, i * 128:(i + 1) * 128], E[:, i * 128:(i + 1) * 128],
                                                 g.C("ident", 0, 128)), *t, *ps.free)
    t1 = g.v_copy(PT, ps.ap[:, 0:384], tok, *after)
    g.ps.put(ps, t1)
    return tok, t1


def sigmoid_psum(g, out, bank, tok, after):
    t = g.a_act(out, bank, ACT.Sigmoid, tok, *after)
    return t


def mix_first(g, lay, mod, tmod, out_tokens):
    fa, ra = g.fa, g.ra
    base = [g.pe.last(), g.act.last(), g.dve.last(), tmod, *out_tokens]
    lam_init = 0.8 - 0.6 * math.exp(-0.3 * lay)
    pl = g.small[:, 512:520]
    lc = PARAM_COLS["lam"] + lay * 4
    q = g.par[0:64, lc:lc + 4]
    tl = g.v_tt(pl[0:64, 0:1], q[:, 0:1], q[:, 1:2], ALU.mult, *base)
    tl = g.v_tt(pl[0:64, 1:2], q[:, 2:3], q[:, 3:4], ALU.mult, *base)
    ps = g.ps.get()
    tl = g.mm(ps.ap[:, 0:2], g.C("ones", 0, 128, 0, 64), pl[0:64, 0:2], after=[tl, *ps.free])
    tl = g.a_act(pl[:, 2:4], ps.ap[:, 0:2], ACT.Exp, tl, *base)
    g.ps.put(ps, tl)
    tl = g.v_tt(pl[:, 4:5], pl[:, 3:4], pl[:, 2:3], ALU.subtract, tl)
    tlam = g.v_ts(pl[:, 4:5], pl[:, 4:5], -lam_init, None, ALU.add, None, tl)
    nlam = pl[:, 4:5]

    per_k = modulated(g, "g_pre_mix", lay, mod, 0, 8, base)

    merged, Gb = fa[:, 0:2048], fa[:, 2048:4096]
    qT, kT, V = fa[:, 4096:5120], fa[:, 5120:6144], fa[:, 6144:7168]
    SCz, ya = fa[:, 7168:8200], fa[:, 8200:9224]
    cfu, cfv = fa[:, 9224:10368], fa[:, 10368:11392]
    cc, krb = fa[:, 2048:3328], fa[:, 3328:3584]
    Zh = [ra[:, i * 2048:i * 2048 + 1024] for i in range(3)]
    Zl = [ra[:, i * 2048 + 1024:i * 2048 + 2048] for i in range(3)]
    ch, cl = ra[:, 6144:7424], ra[:, 7424:8704]

    cu = cfu.rearrange("p (c t) -> p c t", c=4)
    tcu = []
    t0 = g.dve.op(lambda e: e.memset(cu[:, :, 0:30], 0.0), *per_k)
    for j in range(4):
        (ps, tok), = g.proj("w_in", lay * 34 + CF0 + j, 8, 256, g.hh, g.hl, [], per_k=per_k)
        b = g.tmp.get()
        t1 = g.a_act(b.ap[:, 0:T], ps.ap[:, T:2 * T], ACT.Sigmoid, tok, *b.free)
        t2 = g.v_tt(cu[:, j, 30:286], ps.ap[:, 0:T], b.ap[:, 0:T], ALU.mult, tok, t1)
        g.ps.put(ps, t1, t2)
        g.tmp.put(b, t2)
        tcu.append(t2)

    def conv_steps():
        for j in range(4):
            o = cfv[:, j * T:(j + 1) * T]
            t = g.v_ts(o, cu[:, j, 0:256], g.P("cf_conv", lay * 124 + j), g.P("cf_conv_b", lay * 4 + j),
                       ALU.mult, ALU.add, tcu[j], t0)
            for n in range(1, 31):
                t = g.v_stt(o, cu[:, j, n:n + 256], g.P("cf_conv", lay * 124 + 4 * n + j), o,
                            ALU.mult, ALU.add, t)
                if n % 6 == 0:
                    yield
            g.cf_tok = t

    tq = []
    for j in range(4):
        (ps, tok), = g.proj("w_in", lay * 34 + DA0 + j, 8, 256, g.hh, g.hl, [])
        dst = (qT if j < 2 else kT)[:, (j % 2) * 512:(j % 2) * 512 + 512]
        t = g.a_act(dst, ps.ap[:, :], ACT.Copy, tok, *per_k)
        g.ps.put(ps, t)
        tq.append(t)
    tv = []
    pv = [g.ps.get() for _ in range(2)]
    for j in range(2):
        w = g.weight("w_in", lay * 34 + DA0 + 4 + j)
        for tb in range(2):
            for k in range(8):
                xh = g.hh[:, k * T + tb * 128:k * T + tb * 128 + 128]
                xl = g.hl[:, k * T + tb * 128:k * T + tb * 128 + 128]
                wh, wl = w[0][:, k * 256:(k + 1) * 256], w[1][:, k * 256:(k + 1) * 256]
                tok = g.mm3(pv[tb].ap[:, j * 256:(j + 1) * 256], xh, xl, wh, wl, k == 0, k == 7, inc=k == 7,
                            after=[w[2], *pv[tb].free])
        g.done(w, tok)
    for tb in range(2):
        t = g.a_act(V[:, tb * 512:(tb + 1) * 512], pv[tb].ap[:, :], ACT.Copy, tok)
        g.ps.put(pv[tb], t)
        tv.append(t)

    conv = conv_steps()

    st = {}

    def sc_proj():
        z = SCz.rearrange("p (c t) -> p c t", c=4)
        st["z0"] = g.dve.op(lambda e: e.memset(z[:, :, 0:2], 0.0), *per_k)
        for j in range(4):
            (ps, tok), = g.proj("w_in", lay * 34 + SCU0 + j, 8, 256, g.hh, g.hl, [])
            b = g.tmp.get()
            t = g.a_act(b.ap[:, 0:T], ps.ap[:, 0:T], ACT.Copy, tok, *b.free)
            t = g.v_tt(z[:, j, 2:258], ps.ap[:, T:2 * T], b.ap[:, 0:T], ALU.mult, tok, t)
            g.ps.put(ps, t)
            g.tmp.put(b, t)
            st["z"] = t
            yield
        for j in range(2):
            (ps, tok), = g.proj("w_in", lay * 34 + SCB0 + j, 8, 256, g.hh, g.hl, [])
            for i in range(2):
                c = 2 * j + i
                b = g.tmp.get()
                t = conv3(g, b.ap[:, 0:T], z[:, c, :], "sc_conv", lay * 12 + c, 4, [st["z0"], st["z"], *b.free])
                t = g.v_tt(b.ap[:, 0:T], b.ap[:, 0:T], ps.ap[:, i * T:(i + 1) * T], ALU.mult, tok, t)
                t1, t2 = g.split_act(g.xk(Zh[0], c), g.xk(Zl[0], c), b.ap[:, 0:T], t)
                g.tmp.put(b, t1, t2)
            g.ps.put(ps, t)
            st["yc"] = t2
            yield

    def mla_proj():
        for j in range(2):
            (ps, tok), = g.proj("w_in", lay * 34 + MLA0 + j, 8, 256, g.hh, g.hl, [])
            t = g.v_copy(cc[:, j * 512:(j + 1) * 512], ps.ap[:, :], tok, *per_k)
            g.ps.put(ps, t)
            yield
        w = g.weight("w_mc", lay)
        ps = g.ps.get()
        tok = g.group(w, 8, 160, g.hh, g.hl, 0, ps.ap[:, 0:T], ps.free)
        tok = g.group(w, 8, 160, g.hh, g.hl, 64, ps.ap[0:96, T:2 * T], [], m=96)
        g.done(w, tok)
        t = g.v_copy(cc[:, 1024:1280], ps.ap[:, 0:T], tok)
        kr = st["kr"] = krb
        t2 = g.v_copy(kr[0:96, 0:T], ps.ap[0:96, T:2 * T], tok, *per_k)
        g.ps.put(ps, t2)
        st["cc"], st["krt"] = t, t2
        yield

    def merge(branch, z, wo, tz, gate_saved=None):
        zh, zl = z
        for n in range(2):
            held = g.weight(wo, lay * 2 + n)
            for i in range(2):
                pair = 2 * n + i
                dst = merged[:, pair * 512:(pair + 1) * 512]
                ps = g.ps.get()
                for c in range(2):
                    tok = g.group(held, 4, 512, zh, zl, i * 256 + c * 128, ps.ap[:, c * T:(c + 1) * T],
                                  [*ps.free, *tz])
                if i == 1:
                    g.done(held, tok)
                if gate_saved is None:
                    (pg, tg), = g.proj("w_in", lay * 34 + GATE0 + branch * 4 + pair, 8, 256, g.hh, g.hl, [])
                    b = g.tmp.get()
                    ts = g.a_act(b.ap[:, :], pg.ap[:, :], ACT.Sigmoid, tg, *b.free)
                    g.ps.put(pg, ts)
                    sg = b.ap[:, :]
                else:
                    b, sg, ts = None, gate_saved[0][:, pair * 512:(pair + 1) * 512], gate_saved[1]
                if branch == 2:
                    t = g.v_tt(dst, ps.ap[:, :], sg, ALU.mult, tok, ts, *per_k)
                    st[("merged", pair)] = t
                    if b:
                        g.tmp.put(b, t)
                else:
                    o = g.tmp.get()
                    t = g.v_tt(o.ap[:, :], ps.ap[:, :], sg, ALU.mult, tok, ts, *o.free)
                    t2 = g.v_tt(dst, dst, o.ap[:, :], ALU.add, t, st[("merged", pair)])
                    st[("merged", pair)] = t2
                    g.tmp.put(o, t2)
                    if b:
                        g.tmp.put(b, t)
                g.ps.put(ps, t)
                yield

    def gates_b():
        for j in range(4):
            (pg, tg), = g.proj("w_in", lay * 34 + GATE0 + 4 + j, 8, 256, g.hh, g.hl, [])
            st["gb"] = g.a_act(Gb[:, j * 512:(j + 1) * 512], pg.ap[:, :], ACT.Sigmoid, tg, *per_k)
            g.ps.put(pg, st["gb"])
            yield

    def chain(*gens):
        for x in gens:
            yield from (x() if callable(x) else x)

    def fill(*its):
        def step(n=1):
            for _ in range(n):
                for it in its:
                    next(it, None)
        return step

    def drain(it):
        for _ in it:
            pass

    work = chain(sc_proj, lambda: merge(2, (Zh[0], Zl[0]), "sc_w_o", [st["yc"]]), mla_proj)
    step = fill(conv, work)
    da_tmp = g.attn
    tya = []
    for h in range(4):
        hs = []
        for m in range(2):
            ps = g.ps.get()
            p0 = 64 * m
            tok = g.mm(ps.ap[:, 0:128], qT[p0:p0 + 64, h * T:h * T + 128], kT[p0:p0 + 64, h * T:h * T + 128],
                       after=[*tq, *ps.free], inc=False)
            tok = g.mm(ps.ap[:, 128:384], qT[p0:p0 + 64, h * T + 128:h * T + 256], kT[p0:p0 + 64, h * T:h * T + 256])
            Sb = da_tmp[:, m * 384:(m + 1) * 384]
            hs.append((Sb, *softmax3(g, Sb, Sb, tok, ps, g.C("mask3", 0, 384), 0.125,
                                     post=[g.pe.last() if h == 0 else st["tp"]])))
            step()
        (s1, b1, r1, t1), (s2, b2, r2, t2) = hs
        t2 = g.v_ts(r2, r2, nlam, None, ALU.mult, None, t2, tlam)
        for a, n, i in ((0, 128, 0), (128, 256, 1)):
            ta = g.v_ts(s1[:, a:a + n], s1[:, a:a + n], r1[:, i:i + 1], None, ALU.mult, None, t1)
            ta = g.v_stt(s1[:, a:a + n], s2[:, a:a + n], r2[:, i:i + 1], s1[:, a:a + n], ALU.mult, ALU.add, ta, t2)
        g.cols.put(b1, ta)
        g.cols.put(b2, ta)
        step()
        PT = da_tmp[:, 768:1152]
        st["tp"], tpt = turn3(g, s1, PT, [ta], [st["pv"]] if h else [g.pe.last()])
        ps = g.ps.get()
        g.mm(ps.ap[:, 0:256], V[:, h * 128:(h + 1) * 128], PT[:, 0:256], last=False, after=[tpt, *tv, *ps.free],
             inc=False)
        tok = st["pv"] = g.mm(ps.ap[:, 128:256], V[:, 512 + h * 128:512 + (h + 1) * 128], PT[:, 256:384], first=False)
        t = g.a_act(ya[:, h * T:(h + 1) * T], ps.ap[:, 0:T], ACT.Copy, tok, *per_k)
        g.ps.put(ps, t)
        tya.append(t)
        step()
    drain(work)
    drain(conv)

    def head_norm(src, n, gcol, gstep, eps, dim, extra, zh, zl, ones, after):
        for h in range(n):
            sq = g.tmp.get()
            s = src[:, h * T:(h + 1) * T]
            t = g.a_act(sq.ap[:, 0:T], s, ACT.Square, *after, *sq.free)
            ps = g.ps.get()
            t = g.mm(ps.ap[:, 0:T], ones, sq.ap[:, 0:T], after=[t, *ps.free])
            t = g.v_ts(sq.ap[:, T:2 * T], ps.ap[:, 0:T], 1.0 / dim, eps, ALU.mult, ALU.add, t)
            g.ps.put(ps, t)
            t = g.rsqrt(sq.ap[:, 0:T], sq.ap[:, T:2 * T], t)
            if extra is not None:
                t = g.v_ts(s, s, extra, None, ALU.mult, None, t)
            t = g.v_stt(s, s, gcol(h), sq.ap[:, 0:T], ALU.mult, ALU.mult, t)
            g.tmp.put(sq, t)
            t1, t2 = g.split_act(g.xk(zh, h), g.xk(zl, h), s, t)
        return [t1, t2]

    tza = head_norm(ya, 4, lambda h: g.P("da_g_subln", lay), 0, 1e-6, 128, 1.0 - lam_init, Zh[1], Zl[1],
                    g.C("ones", 0, 128), tya)

    v_, r_ = g.small[:, 0:256], g.small[:, 256:512]
    sqb = da_tmp[:, 0:768]
    tz = []
    for a, n, dim, gn, gl in ((0, 3, 384, "mla_g_cq", 3), (3, 2, 256, "mla_g_ckv", 2)):
        src = cc[:, a * T:(a + n) * T]
        t1, _ = g.stats(src, n, dim, 1e-6, r_, v_, sqb, [st["cc"], g.dve.last(), g.pe.last()])
        for k in range(n):
            s = cc[:, (a + k) * T:(a + k + 1) * T]
            t2 = g.v_stt(s, s, g.P(gn, lay * gl + k), r_, ALU.mult, ALU.mult, t1)
            _, t3 = g.split_act(g.xk(ch, a + k), g.xk(cl, a + k), s, t2, *per_k)
            tz.append(t3)
    mq, mk, mv = fa[:, 4096:6144], fa[:, 7168:9216], fa[:, 6144:7168]
    free = [g.pe.last(), g.dve.last(), g.act.last()]
    tmq = []
    cos, sin = g.trig[64:96, 0:256], g.trig[64:96, 256:512]

    def rope(dst, n, t, free):
        ps = g.ps.get()
        for i in range(n):
            tok = g.mm(ps.ap[0:96, i * T:(i + 1) * T], g.C("rot", 0, 96, 0, 96), dst[0:96, i * T:(i + 1) * T],
                       after=[t, *ps.free])
        b = g.tmp.get()
        o = b.ap[64:96, 0:n * T]
        d = dst[64:96, 0:n * T]
        cs, sn = (cos, sin) if n == 1 else (bc2(cos), bc2(sin))
        f = (lambda a: a) if n == 1 else v2
        t1 = g.v_tt(f(o), f(ps.ap[64:96, 0:n * T]), sn, ALU.mult, tok, *b.free, *g.trig_tok)
        g.ps.put(ps, t1)
        t2 = g.v_tt(f(d), f(d), cs, ALU.mult, tok)
        t3 = g.v_tt(d, d, o, ALU.add, t1, t2)
        g.tmp.put(b, t3)
        return t3

    for n in range(2):
        w = g.weight("mla_w_uq", lay * 2 + n)
        for i in range(2):
            ps = g.ps.get()
            for c in range(2):
                tok = g.group(w, 3, 384, ch, cl, (2 * i + c) * 96, ps.ap[0:96, c * T:(c + 1) * T],
                              [*ps.free, *tz], m=96)
            h = 4 * n + 2 * i
            t = g.a_act(mq[0:96, h * T:(h + 2) * T], ps.ap[0:96, :], ACT.Copy, tok, *free)
            g.ps.put(ps, t)
            tmq.append(rope(mq[:, h * T:(h + 2) * T], 2, t, free))
        g.done(w, tok)
    w = g.weight("mla_w_ukv", lay)
    c0h, c0l = ch[:, 3 * T:5 * T], cl[:, 3 * T:5 * T]
    tmk = []
    for i in range(4):
        ps = g.ps.get()
        for c in range(2):
            tok = g.group(w, 2, 1024, c0h, c0l, (2 * i + c) * 128, ps.ap[:, c * T:(c + 1) * T], ps.free)
        t = g.a_act(mk[0:64, 2 * i * T:(2 * i + 2) * T], ps.ap[0:64, :], ACT.Copy, tok, *free)
        g.ps.put(ps, t)
        tmk.append(t)
    tmv = []
    for tb in range(2):
        ps = g.ps.get()
        for k in range(2):
            xh, xl = [c0[:, k * T + tb * 128:k * T + tb * 128 + 128] for c0 in (c0h, c0l)]
            wh, wl = [a[:, k * 1024:(k + 1) * 1024].rearrange("p (h c) -> p h c", h=8)[:, :, 64:128] for a in (w[0], w[1])]
            tok = g.mm3(ps.ap[:, :].rearrange("p (h c) -> p h c", h=8), xh, xl, wh, wl, k == 0, k == 1, inc=k == 1,
                        after=ps.free)
        t = g.a_act(mv[:, tb * 512:(tb + 1) * 512], ps.ap[:, :], ACT.Copy, tok, *free)
        g.ps.put(ps, t)
        tmv.append(t)
    g.done(w, tok)
    kr = st["kr"]
    t = rope(kr, 1, st["krt"], [])
    for h in range(8):
        tkr = g.v_copy(mk[64:96, h * T:(h + 1) * T], kr[64:96, 0:T], t, *free)

    def cf_finish():
        sm, ve = g.small[:, 0:256], g.small[:, 256:512]
        b = g.tmp.get()
        t = g.dve.op(lambda e: e.tensor_reduce(b.ap[:, 0:T], cfv.rearrange("p (c t) -> p t c", c=4), AX, ALU.add),
                     g.cf_tok, *b.free)
        ps = g.ps.get()
        t = g.mm(ps.ap[:, 0:T], g.C("ones", 0, 128), b.ap[:, 0:T], after=[t, *ps.free])
        g.tmp.put(b, t)
        t = g.v_ts(sm, ps.ap[:, 0:T], 1.0 / 512, None, ALU.mult, None, t, g.act.last())
        g.ps.put(ps, t)
        for j in range(4):
            o = cfv[:, j * T:(j + 1) * T]
            t1 = g.v_tt(o, o, sm, ALU.subtract, t)
        yield
        t2, _ = g.stats(cfv, 4, 512, 1e-5, sm, ve, cfu, [t1, g.dve.last()])
        for j in range(4):
            o = cfv[:, j * T:(j + 1) * T]
            t3 = g.v_tt(o, o, sm, ALU.mult, t2)
            t3 = g.a_act(o, o, ACT.Silu, t3, scale=g.P("cf_ln_g", lay * 4 + j), bias=g.P("cf_ln_b", lay * 4 + j))
            _, t4 = g.split_act(g.xk(Zh[2], j), g.xk(Zl[2], j), o, t3, *per_k)
        st["cf"] = t4
        yield

    work = chain(cf_finish, gates_b, lambda: merge(0, (Zh[1], Zl[1]), "da_w_o", tza),
                 lambda: merge(3, (Zh[2], Zl[2]), "cf_w_o", [st["cf"]]))
    step = fill(work)
    tyb = []
    sc = 96 ** -0.5
    trn = [g.pe.last(), g.dve.last()]
    po = None
    for h in range(8):
        ps = g.ps.get()
        g.mm(ps.ap[:, 0:128], mq[0:96, h * T:h * T + 128], mk[0:96, h * T:h * T + 128],
             after=[*tmq, *tmk, tkr, *ps.free], inc=False)
        tok = g.mm(ps.ap[:, 128:384], mq[0:96, h * T + 128:(h + 1) * T], mk[0:96, h * T:(h + 1) * T])
        Sb = da_tmp[:, (h % 2) * 384:(h % 2 + 1) * 384]
        b, r, t = softmax3(g, Sb, Sb, tok, ps, g.C("mask3", 0, 384), sc, post=[trn if h < 2 else st[("tp", h - 2)]])
        for a, n, i in ((0, 128, 0), (128, 256, 1)):
            ta = g.v_ts(Sb[:, a:a + n], Sb[:, a:a + n], r[:, i:i + 1], None, ALU.mult, None, t)
        g.cols.put(b, ta)
        step()
        PT = da_tmp[:, 768:1152]
        st[("tp", h)], tpt = turn3(g, Sb, PT, [ta], [st["pv"]])
        p0 = 64 * (h % 2)
        if h % 2 == 0:
            po = g.ps.get()
        g.mm(po.ap[p0:p0 + 64, 0:256], mv[:, h * 64:(h + 1) * 64], PT[:, 0:256], last=False,
             after=[tpt, *tmv, *po.free], inc=False)
        tok = st["pv"] = g.mm(po.ap[p0:p0 + 64, 128:256], mv[:, 512 + h * 64:512 + (h + 1) * 64], PT[:, 256:384],
                              first=False)
        if h % 2:
            c = h // 2
            b = g.tmp.get()
            t = g.a_act(b.ap[:, 0:T], po.ap[:, 0:T], ACT.Copy, tok, *b.free)
            g.ps.put(po, t)
            t1, t2 = g.split_act(g.xk(Zh[0], c), g.xk(Zl[0], c), b.ap[:, 0:T], t, *trn)
            g.tmp.put(b, t1, t2)
            tyb += [t1, t2]
        step()
    drain(work)
    drain(merge(1, (Zh[0], Zl[0]), "mla_w_o", tyb, gate_saved=(Gb, st["gb"])))

    tm = []
    for k in range(8):
        _, t = g.split_act(g.xk(g.hh, k), g.xk(g.hl, k), g.xk(merged, k), st[("merged", k // 2)], g.pe.last())
        tm.append(t)
    y = fa[:, 4096:6144]
    ty = []
    for j in range(4):
        (ps, tok), = g.proj("w_mix_out", lay * 4 + j, 8, 256, g.hh, g.hl, [], per_k=tm)
        t = g.v_copy(y[:, j * 512:(j + 1) * 512], ps.ap[:, :], tok, g.pe.last())
        g.ps.put(ps, t)
        ty.append(t)
    return add_normed(g, y, lay, "g_post_mix", mod, 16, ty)


def tables(g, t0):
    pi = g.tmp.get()
    raw = pi.ap[64:96, 0:T].bitcast(I32)
    g.sp.dma(lambda e: e.dma_start(raw, g.args["positions"].broadcast_to([32, T])), g.s_p[0])
    g.n_p += 1
    p = pi.ap[64:96, T:2 * T]
    t = g.v_copy(p, raw, (g.s_p[0], 16))
    t = g.v_ts(p, p, g.C("inv", 0, 1, 64, 96), None, ALU.mult, None, t, t0)
    b = g.tmp.get()
    n, z = b.ap[64:96, 0:T], b.ap[64:96, T:2 * T]
    big = 12582912.0
    c1 = 6.28125
    c2 = float(np.float32(TWO_PI - c1))
    c3 = float(TWO_PI - c1 - float(np.float32(TWO_PI - c1)))
    for i, shift in ((0, 0.25), (1, 0.0)):
        t = g.v_ts(n, p, 1.0 / TWO_PI, shift, ALU.mult, ALU.add, t)
        t = g.v_ts(n, n, big, None, ALU.add, None, t)
        t = g.v_ts(n, n, big, None, ALU.subtract, None, t)
        t = g.v_stt(z, n, -c1, p, ALU.mult, ALU.add, t)
        t = g.v_stt(z, n, -c2, z, ALU.mult, ALU.add, t)
        t = g.v_stt(z, n, -c3, z, ALU.mult, ALU.add, t)
        if i == 0:
            t = g.v_ts(z, z, math.pi / 2, None, ALU.add, None, t)
        t = g.v_ts(z, z, 3.1415925, -3.1415925, ALU.min, ALU.max, t)
        t = g.a_act(g.trig[64:96, i * T:(i + 1) * T], z, ACT.Sin, t)
    g.tmp.put(pi, t)
    g.tmp.put(b, t)
    g.trig_tok = [t]


def second_norm(g, layer, which, after):
    v, r = g.small[:, 0:256], g.small[:, 256:512]
    per_k = g.split_gain("norm_gains", (layer * 4 + which) * 8, 8, g.x, after, [g.pe.last()])
    sq = g.fa[:, 0:2048]
    tr, _ = g.stats(g.x[:, :], 8, D, 1e-6, r, v, sq, [*after, g.pe.last(), g.act.last(), g.dve.last()])
    return per_k, r, tr


def second_ffn(g, layer, half, tx):
    per_k, r, tr = second_norm(g, layer, 2 * half, [tx])

    def chunk(j, ps, tok, yh, yl, free):
        a = g.tmp.get()
        t = g.v_tt(v2(a.ap[:, :]), v2(ps.ap[:, :]), bc2(r), ALU.mult, tok, tr, *a.free)
        g.ps.put(ps, t)
        b = g.tmp.get()
        t1 = g.a_act(b.ap[:, 0:T], a.ap[:, 0:T], ACT.Silu, t, *b.free)
        t2 = g.v_tt(b.ap[:, T:2 * T], b.ap[:, 0:T], a.ap[:, T:2 * T], ALU.mult, t1)
        g.tmp.put(a, t2)
        t3, t4 = g.split_act(yh, yl, b.ap[:, T:2 * T], t2, *free)
        g.tmp.put(b, t3, t4)
        return t4

    i = layer * 2 + half
    acc = ffn(g, "w_gu", i * 22, "w_dn", i * 11, per_k, chunk)
    la = g.act.last()
    for n, b in enumerate(acc):
        s = g.x[:, n * 512:(n + 1) * 512]
        t = g.v_stt(s, b.ap[:, :], 0.5, s, ALU.mult, ALU.add, b.ready, la)
        g.ps.put(b, t)
    return t


def out_add(g, name, n0, zh, zl, tz):
    la = g.act.last()
    for j in range(4):
        (ps, tok), = g.proj(name, n0 + j, 8, 256, zh, zl, [], per_k=tz)
        s = g.x[:, j * 512:(j + 1) * 512]
        t = g.v_tt(s, s, ps.ap[:, :], ALU.add, tok, la)
        g.ps.put(ps, t)
    return t


def evac_scaled(g, out, ps, tok, r, tr, *after):
    t = g.v_tt(v2(out), v2(ps.ap[:, :]), bc2(r), ALU.mult, tok, tr, *after)
    g.ps.put(ps, t)
    return t


def token_factor(g, r, tr):
    rc = g.small[:, 520:522]
    ps = g.ps.get()
    for tb in range(2):
        tok = g.pe.op(lambda e, tb=tb: e.transpose(ps.ap[:, tb * 128:(tb + 1) * 128], r[:, tb * 128:(tb + 1) * 128],
                                                   g.C("ident", 0, 128)), tr, *ps.free)
    for tb in range(2):
        t = g.v_copy(rc[:, tb:tb + 1], ps.ap[:, tb * 128:tb * 128 + 1], tok)
    g.ps.put(ps, t)
    return rc, t


def token_major(g, name, ns, width, offs, banks, per_k):
    for j, n in enumerate(ns):
        w = g.weight(name, n)
        for tb in range(2):
            ps = banks[tb]
            for k in range(8):
                a = k * T + tb * 128
                tok = g.mm3(ps.ap[:, j * width:(j + 1) * width], g.hh[:, a:a + 128], g.hl[:, a:a + 128],
                            w[0][:, k * width:(k + 1) * width], w[1][:, k * width:(k + 1) * width],
                            k == 0, k == 7, inc=k == 7, after=[w[2], *ps.free, per_k[k]])
        g.done(w, tok)
    return tok


def hgrn(g, layer, j, tx):
    per_k, r, tr = second_norm(g, layer, 1, [tx])
    rc, trc = token_factor(g, r, tr)
    fa = g.fa
    q, k, b = fa[:, 0:1024], fa[:, 1024:2048], fa[:, 2048:3072]
    Qa, Ka = fa[:, 3072:4096], fa[:, 4096:5120]
    Dv = fa[:, 5120:6144]
    AT = fa[:, 6144:7680]
    V = fa[:, 7680:8704]
    o = fa[:, 8704:10752]
    A32 = fa[:, 10752:11008]
    base = [g.pe.last(), g.act.last(), g.dve.last()]
    L = g.attn[:, 0:96]
    lb, oml, zf = L[:, 64:72], L[:, 72:80], L[:, 80:88]
    if layer == 0:
        tl = g.dve.op(lambda e: e.memset(lb, 0.0), *base)
        tl = g.dve.op(lambda e: e.memset(oml, 1.0), *base)
        tl = g.dve.op(lambda e: e.memset(zf, 1.0), *base)
    else:
        c = PARAM_COLS["hg_lb"]
        raw = g.par[:, c:c + 32]
        mx, s = L[:, 88:96], L[:, 32:40]
        t = g.dve.op(lambda e: e.tensor_reduce(mx, raw.rearrange("p (l c) -> p c l", l=4), AX, ALU.max), *base)
        t = g.v_tt(L[:, 0:32].rearrange("p (l c) -> p l c", l=4), raw.rearrange("p (l c) -> p l c", l=4),
                   mx.unsqueeze(1).broadcast_to([128, 4, 8]), ALU.subtract, t)
        t = g.a_act(L[:, 0:32], L[:, 0:32], ACT.Exp, t)
        t = g.v_tt(s, L[:, 8:16], L[:, 16:24], ALU.add, t)
        t = g.v_tt(s, s, L[:, 24:32], ALU.add, t) if layer == 3 else t
        t = g.v_tt(L[:, 40:48], s, L[:, 0:8], ALU.add, t)
        t = g.dve.op(lambda e: e.reciprocal(L[:, 48:56], L[:, 40:48]), t)
        t = g.v_tt(lb, s, L[:, 48:56], ALU.mult, t)
        t = g.v_tt(oml, L[:, 0:8], L[:, 48:56], ALU.mult, t)
        tl = g.v_ts(zf, lb, 2.0 ** -60, None, ALU.is_lt, None, t)
    t_at = g.dve.op(lambda e: e.memset(AT, 0.0), *base)
    AT4 = AT.rearrange("p (h c) -> p h c", h=4)
    tO = []
    for gr in range(2):
        tq, tb_ = [], []
        for n in range(2):
            (ps, tok), = g.proj("hg_in", j * 16 + gr * 2 + n, 8, 256, g.hh, g.hl, [], per_k=per_k)
            a = g.tmp.get()
            t = evac_scaled(g, a.ap[:, :], ps, tok, r, tr, *a.free)
            t = g.a_act(q[:, n * 512:(n + 1) * 512], a.ap[:, :], ACT.Silu, t, *base)
            g.tmp.put(a, t)
            tq.append(t)
        for n in range(2):
            (ps, tok), = g.proj("hg_in", j * 16 + 4 + gr * 2 + n, 8, 256, g.hh, g.hl, [])
            f = g.tmp.get()
            t = evac_scaled(g, f.ap[:, :], ps, tok, r, tr, *f.free)
            e_ = g.tmp.get()
            tc = g.v_ts(e_.ap[:, :], f.ap[:, :], -80.0, None, ALU.max, None, t, *e_.free)
            t = g.a_act(e_.ap[:, :], e_.ap[:, :], ACT.Exp, tc, scale=-1.0)
            s = g.tmp.get()
            ts = g.v_ts(s.ap[:, :], e_.ap[:, :], 1.0, None, ALU.add, None, t, *s.free)
            ts = g.dve.op(lambda e, s=s: e.reciprocal(s.ap[:, :], s.ap[:, :]), ts)
            for c in range(2):
                hd = gr * 4 + n * 2 + c
                w = slice(c * T, (c + 1) * T)
                kk = k[:, (2 * n + c) * T:(2 * n + c + 1) * T]
                t = g.v_stt(kk, e_.ap[:, w], oml[:, hd:hd + 1], s.ap[:, w], ALU.mult, ALU.mult, ts, tl, *base)
                tu = g.v_ts(s.ap[:, w], s.ap[:, w], oml[:, hd:hd + 1], lb[:, hd:hd + 1], ALU.mult, ALU.add, t)
                tf = g.v_ts(f.ap[:, w], f.ap[:, w], 60 * math.log(2.0), 0.0, ALU.add, ALU.min, tc)
                tu = g.v_ts(s.ap[:, w], s.ap[:, w], 2.0 ** -60, None, ALU.max, None, tu)
                tu = g.a_act(s.ap[:, w], s.ap[:, w], ACT.Ln, tu)
                tu = g.v_stt(f.ap[:, w], f.ap[:, w], zf[:, hd:hd + 1], s.ap[:, w], ALU.mult, ALU.add, tu, tf)
                bb = b[:, (2 * n + c) * T:(2 * n + c + 1) * T]
                tu = g.dve.op(lambda e, bb=bb, ff=f.ap[:, w]: e.tensor_tensor_scan(
                    bb, g.C("rst", 0, 256), ff, 0.0, ALU.mult, ALU.add), tu, *base)
            for x_ in (f, e_, s):
                g.tmp.put(x_, tu, t)
            tb_.append(tu)
        banks = [g.ps.get() for _ in range(2)]
        tok = token_major(g, "hg_in", [j * 16 + 8 + gr * 2, j * 16 + 9 + gr * 2], 256, None, banks, per_k)
        tv = []
        for tb in range(2):
            t = g.v_ts(V[:, tb * 512:(tb + 1) * 512], banks[tb].ap[:, :], rc[:, tb:tb + 1], None, ALU.mult, None,
                       tok, trc, *base)
            g.ps.put(banks[tb], t)
            tv.append(t)

        def v3(a, n):
            return a.rearrange("p (n m) -> p n m", m=n)

        b64 = v3(b, 64)
        last = b64[:, :, 63:64].broadcast_to([128, 16, 64])
        t = g.a_act(Qa, b, ACT.Exp, *tb_, *base)
        tQ = g.v_tt(Qa, Qa, q, ALU.mult, t, *tq)
        t = g.v_tt(v3(Ka, 64), last, b64, ALU.subtract, *base, *tb_)
        t = g.a_act(Ka, Ka, ACT.Exp, t)
        tK = g.v_tt(Ka, Ka, k, ALU.mult, t)
        eb = g.cols.get()
        tE = g.a_act(eb.ap[:, 0:16].unsqueeze(2), b64[:, :, 63:64], ACT.Exp, *tb_, *eb.free)

        ps = g.ps.get()
        for h in range(4):
            for sb in range(2):
                a = h * T + sb * 128
                tok = g.mm(ps.ap[0:64, h * 128 + sb * 64:h * 128 + sb * 64 + 64], Ka[:, a:a + 64], Qa[:, a + 64:a + 128],
                           after=[tQ, tK, *ps.free], inc=h == 3)
        av = AT4.rearrange("p h (s t) -> p h s t", t=128)
        tA = []
        for sb in range(2):
            t = g.a_act(AT4[0:64, :, sb * 256 + 64:sb * 256 + 128],
                        ps.ap[0:64, :].rearrange("p (h s t) -> p h s t", h=4, s=2)[:, :, sb, :], ACT.Copy, tok, t_at)
            tA.append(t)
        g.ps.put(ps, t)
        q3 = v3(Qa, 64).rearrange("p (h c) m -> p h c m", c=4)
        k3 = v3(Ka, 64).rearrange("p (h c) m -> p h c m", c=4)
        e4 = eb.ap[:, 0:16].rearrange("p (h c) -> p h c", c=4)
        t1 = g.v_tt(q3[:, :, 3, :], q3[:, :, 3, :], e4[:, :, 2:3].broadcast_to([128, 4, 64]), ALU.mult, tok, tE)
        t2 = g.v_tt(k3[:, :, 0, :], k3[:, :, 0, :], e4[:, :, 1:2].broadcast_to([128, 4, 64]), ALU.mult, tok, tE)
        g.cols.put(eb, t2)
        ps = g.ps.get()
        for h in range(4):
            tok = g.mm(ps.ap[:, h * 128:(h + 1) * 128], Ka[:, h * T:h * T + 128], Qa[:, h * T + 128:h * T + 256],
                       after=[t1, t2, *ps.free], inc=h == 3)
        t = g.a_act(AT4[:, :, 128:256], ps.ap[:, :].rearrange("p (h t) -> p h t", h=4), ACT.Copy, tok, t_at)
        tA.append(t)
        g.ps.put(ps, t)
        tfree = [g.pe.last()]
        tacc = None
        for lv, m in enumerate((32, 16, 8, 4, 2, 1, 0)):
            if m:
                b3, d3, qq, kk = v3(b, 2 * m), v3(Dv, 2 * m), v3(q, 2 * m), v3(k, 2 * m)
                n = 1024 // (2 * m)
                ref = b3[:, :, m - 1:m].broadcast_to([128, n, m])
                t1 = g.v_tt(d3[:, :, m:2 * m], b3[:, :, m:2 * m], ref, ALU.subtract, *tfree)
                t1 = g.v_tt(d3[:, :, 0:m], ref, b3[:, :, 0:m], ALU.subtract, *tfree)
                t = g.a_act(Dv, Dv, ACT.Exp, t1)
                t1 = g.v_tt(d3[:, :, m:2 * m], d3[:, :, m:2 * m], qq[:, :, m:2 * m], ALU.mult, t)
                t1 = g.v_tt(d3[:, :, 0:m], d3[:, :, 0:m], kk[:, :, 0:m], ALU.mult, t)
            ps = g.ps.get()
            if m == 32:
                for h in range(4):
                    for c in range(4):
                        a = h * T + c * 64
                        p0 = 64 * (c % 2)
                        col = h * 64 + (c // 2) * 32
                        tok = g.mm(ps.ap[p0:p0 + 32, col:col + 32], Dv[:, a:a + 32], Dv[:, a + 32:a + 64],
                                   after=[t1, *ps.free], inc=h == 3 and c == 3)
                for c in range(2):
                    p0 = 64 * c
                    for sb in range(2):
                        t = g.a_act(AT4[p0:p0 + 32, :, sb * 256 + p0 + 32:sb * 256 + p0 + 64],
                                    ps.ap[p0:p0 + 32, 0:256].rearrange("p (h s t) -> p h s t", h=4, s=2)[:, :, sb, :],
                                    ACT.Copy, tok, t_at)
                        tA.append(t)
                g.ps.put(ps, t)
            else:
                lhs, rhs = (Dv, Dv) if m else (k, q)
                for h in range(4):
                    for jb in range(8):
                        a = h * T + jb * 32
                        p0 = 32 * (jb % 4)
                        col = h * 64 + (jb // 4) * 32
                        tok = g.mm(ps.ap[p0:p0 + 32, col:col + 32], lhs[:, a:a + 32], rhs[:, a:a + 32],
                                   after=[t1, *ps.free], inc=h == 3 and jb == 7)
                mask = g.C("lev", (lv - 1) * 32, 32).unsqueeze(1).broadcast_to([128, 8, 32])
                pv = ps.ap[:, 0:256].rearrange("p (n t) -> p n t", t=32)
                av = A32.rearrange("p (n t) -> p n t", t=32)
                if lv == 1:
                    tacc = g.v_tt(av, pv, mask, ALU.mult, tok, *tA)
                    g.ps.put(ps, tacc)
                else:
                    a = g.tmp.get()
                    t = g.v_tt(a.ap[:, 0:256].rearrange("p (n t) -> p n t", t=32), pv, mask, ALU.mult, tok, *a.free)
                    g.ps.put(ps, t)
                    tacc = g.v_tt(A32, A32, a.ap[:, 0:256], ALU.add, t, tacc)
                    g.tmp.put(a, tacc)
            tfree = [g.pe.last()]
        for c in range(4):
            p0 = 32 * c
            for sb in range(2):
                t = g.a_act(AT4[p0:p0 + 32, :, sb * 256 + p0:sb * 256 + p0 + 32],
                            A32[p0:p0 + 32, :].rearrange("p (h s t) -> p h s t", h=4, s=2)[:, :, sb, :],
                            ACT.Copy, tacc, t_at)
        tA.append(t)
        for hp in range(2):
            ps = g.ps.get()
            for c in range(2):
                h = 2 * hp + c
                g.mm(ps.ap[:, c * T:c * T + 256], V[:, h * 128:(h + 1) * 128], AT4[:, h, 0:256], last=False,
                     after=[*tA, *tv, *ps.free], inc=False)
                tok = g.mm(ps.ap[:, c * T + 128:c * T + 256], V[:, 512 + h * 128:512 + (h + 1) * 128],
                           AT4[:, h, 256:384], first=False)
            hh = gr * 4 + 2 * hp
            t = g.v_copy(o[:, hh * T:(hh + 2) * T], ps.ap[:, :], tok, *base)
            g.ps.put(ps, t)
            tO.append(t)
        base = [g.pe.last(), g.act.last(), g.dve.last()]
        t_at = base[0]
    zh, zl = g.ra[:, 0:2048], g.ra[:, 2048:4096]
    tz = []
    rr = g.attn[:, 128:1152]
    for n in range(4):
        (ps, tok), = g.proj("hg_in", j * 16 + 12 + n, 8, 256, g.hh, g.hl, [])
        og = g.tmp.get()
        t = evac_scaled(g, og.ap[:, :], ps, tok, r, tr, *og.free)
        tg = g.a_act(og.ap[:, :], og.ap[:, :], ACT.Silu, t)
        s = o[:, n * 512:(n + 1) * 512]
        toks = norm_heads(g, s, 2, 1, 128, lambda c: g.P("hg_g_norm", j), g.C("ones", 0, 128), [tO[n]])
        t = g.v_tt(s, s, og.ap[:, :], ALU.mult, tg, *toks)
        g.tmp.put(og, t)
        t1, t2 = g.split_act(zh[:, n * 512:(n + 1) * 512], zl[:, n * 512:(n + 1) * 512], s, t, *base)
        tz += [t2, t2]
    return out_add(g, "hg_out", j * 4, zh, zl, tz)


def norm_heads(g, s, n, per, dim, gcol, ones, after):
    toks = []
    for h in range(n // per):
        sq = g.tmp.get()
        w = slice(h * per * T, (h + 1) * per * T)
        t = g.a_act(sq.ap[:, 0:per * T], s[:, w], ACT.Square, *after, *sq.free)
        ps = g.ps.get()
        for c in range(per):
            tok = g.mm(ps.ap[:, 0:T], ones, sq.ap[:, c * T:(c + 1) * T], first=c == 0, last=c == per - 1,
                       after=[t, *ps.free])
        v = sq.ap[:, T:2 * T]
        t = g.v_ts(v, ps.ap[:, 0:T], 1.0 / dim, 1e-6, ALU.mult, ALU.add, tok)
        g.ps.put(ps, t)
        t = g.rsqrt(sq.ap[:, 0:T], v, t)
        for c in range(per):
            a = s[:, (h * per + c) * T:(h * per + c + 1) * T]
            t1 = g.v_stt(a, a, gcol(h * per + c), sq.ap[:, 0:T], ALU.mult, ALU.mult, t)
        g.tmp.put(sq, t1)
        toks.append(t1)
    return toks


def mlstm(g, tx):
    per_k, r, tr = second_norm(g, 1, 1, [tx])
    rc, trc = token_factor(g, r, tr)
    fa = g.fa
    q, k = fa[:, 0:1024], fa[:, 1024:2048]
    V = fa[:, 2048:4096]
    h_ = fa[:, 4096:6144]
    W, AT = fa[:, 6144:6528], fa[:, 6528:6912]
    rows = fa[0:4, 6912:8960]
    em = fa[:, 8960:9216]
    dn = fa[:, 9216:9472]
    base = [g.pe.last(), g.act.last(), g.dve.last()]
    ps = g.ps.get()
    c0 = PARAM_COLS["w_if"]
    for i in range(2):
        for kk in range(8):
            w = g.par[:, c0 + kk * 8 + i * 4:c0 + kk * 8 + i * 4 + 4]
            out = ps.ap[0:4, i * T:(i + 1) * T]
            g.mm(out, w, g.xk(g.hh, kk).bitcast(F32), first=kk == 0, last=False, inc=False, after=[per_k[kk], *ps.free])
            tok = g.mm(out, w, g.xk(g.hl, kk).bitcast(F32), first=False, last=kk == 7)
    G, X1, Lc, A, CM, NM = [rows[:, i * T:(i + 1) * T] for i in (0, 2, 3, 4, 5, 6)]
    ig, fg = rows[:, 0:T], rows[:, T:2 * T]
    t = g.v_tt(v2(rows[:, 0:512]), v2(ps.ap[0:4, :]), bc2(r[0:4, :]), ALU.mult, tok, tr, *base)
    g.ps.put(ps, t)
    for i, a in enumerate((ig, fg)):
        t = g.v_ts(a, a, g.P("ml_b_if", i, 4), None, ALU.add, None, t)
    t = g.a_act(rows[:, 0:512], rows[:, 0:512], ACT.Tanh, t, scale=1.0 / 15)
    t = g.v_ts(rows[:, 0:512], rows[:, 0:512], 15.0, None, ALU.mult, None, t)
    t = g.a_act(X1, fg, ACT.Exp, t, scale=-1.0)
    t = g.v_ts(X1, X1, 1.0, None, ALU.add, None, t)
    t = g.a_act(X1, X1, ACT.Ln, t)
    t = g.dve.op(lambda e: e.tensor_tensor_scan(Lc, g.C("ones", 0, 1, 0, 4).broadcast_to([4, T]), X1, 0.0,
                                                ALU.mult, ALU.add), t)
    t = g.v_tt(A, ig, Lc, ALU.add, t)
    t = g.dve.op(lambda e: e.tensor_tensor_scan(CM, A, A, 0.0, ALU.max, ALU.max), t)
    t = g.v_tt(NM, Lc, CM, ALU.subtract, t)
    ac = g.small[:, 528:536]
    ps = g.ps.get()
    for sb in range(2):
        tok = g.pe.op(lambda e, sb=sb, ps=ps: e.transpose(ps.ap[:, sb * 4:sb * 4 + 4], A[:, sb * 128:(sb + 1) * 128],
                                                   g.C("ident", 0, 4, 0, 4)), t, *ps.free)
    tac = g.v_copy(ac, ps.ap[:, 0:8], tok)
    g.ps.put(ps, tac)
    tq = []
    for n in range(4):
        (ps, tok), = g.proj("ml_in", n, 8, 256, g.hh, g.hl, [])
        dst = (q if n < 2 else k)[:, (n % 2) * 512:(n % 2) * 512 + 512]
        tq.append(evac_scaled(g, dst, ps, tok, r, tr, *base))
    tv = []
    for n in range(2):
        banks = [g.ps.get() for _ in range(2)]
        tok = token_major(g, "ml_in", [4 + 2 * n, 5 + 2 * n], 256, None, banks, per_k)
        for tb in range(2):
            t = g.v_ts(V[:, tb * 1024 + n * 512:tb * 1024 + (n + 1) * 512], banks[tb].ap[:, :], rc[:, tb:tb + 1], None,
                       ALU.mult, None, tok, trc, *base)
            g.ps.put(banks[tb], t)
            tv.append(t)
    th = []
    for h in range(4):
        ps = g.ps.get()
        s_ = g.C("ident", h, 1, 0, 4).broadcast_to([4, 128])
        tok = g.mm(ps.ap[:, 0:T], s_, CM, after=[tac, *ps.free])
        tok = g.mm(ps.ap[:, T:2 * T], s_, NM)
        free = [g.pe.last(), g.dve.last()]
        t = g.v_ts(W[:, 0:256], ps.ap[:, 0:256], ac[:, h:h + 1], 0.0, ALU.subtract, ALU.max, tok, *base)
        t = g.v_ts(W[:, 256:384], ps.ap[:, 128:256], ac[:, 4 + h:5 + h], 0.0, ALU.subtract, ALU.max, tok, *base)
        te = g.a_act(em, ps.ap[:, T:2 * T], ACT.Exp, tok, t, *free)
        g.ps.put(ps, t, te)
        t = g.a_act(W, W, ACT.Exp, t, scale=-1.0)
        for a in (0, 256):
            t = g.v_tt(W[:, a:a + 128], W[:, a:a + 128], g.C("maskT", 0, 128), ALU.mult, t)
        ps = g.ps.get()
        tok = g.mm(ps.ap[:, 0:256], k[:, h * T:h * T + 128], q[:, h * T:(h + 1) * T], after=[*tq, *ps.free])
        tok = g.mm(ps.ap[:, 256:384], k[:, h * T + 128:(h + 1) * T], q[:, h * T + 128:(h + 1) * T])
        t = g.v_stt(AT, ps.ap[:, 0:384], 128 ** -0.5, W, ALU.mult, ALU.mult, tok, t, *free)
        g.ps.put(ps, t)
        ps, pd = g.ps.get(), g.ps.get()
        g.mm(pd.ap[:, 0:256], g.C("ones", 0, 128), AT[:, 0:256], last=False, inc=False, after=[t, *pd.free])
        tokd = g.mm(pd.ap[:, 128:256], g.C("ones", 0, 128), AT[:, 256:384], first=False)
        for c in range(2):
            a = h * 256 + c * 128
            g.mm(ps.ap[:, c * T:c * T + 256], V[:, a:a + 128], AT[:, 0:256], last=False, inc=False,
                 after=[*tv, *ps.free])
            tok = g.mm(ps.ap[:, c * T + 128:c * T + 256], V[:, 1024 + a:1024 + a + 128], AT[:, 256:384], first=False)
        t = g.a_act(dn, pd.ap[:, 0:256], ACT.Abs, tokd, *free)
        g.ps.put(pd, t)
        t = g.v_tt(dn, dn, em, ALU.max, t, te)
        t = g.dve.op(lambda e: e.reciprocal(dn, dn), t)
        t = g.v_tt(v2(h_[:, 2 * h * T:(2 * h + 2) * T]), v2(ps.ap[:, :]), bc2(dn), ALU.mult, t, tok, *base)
        g.ps.put(ps, t)
        th.append(t)
    zh, zl = g.ra[:, 0:2048], g.ra[:, 2048:4096]
    tz = []
    for n in range(4):
        (ps, tok), = g.proj("ml_in", 8 + n, 8, 256, g.hh, g.hl, [])
        og = g.tmp.get()
        t = evac_scaled(g, og.ap[:, :], ps, tok, r, tr, *og.free)
        tg = g.a_act(og.ap[:, :], og.ap[:, :], ACT.Sigmoid, t)
        s = h_[:, n * 512:(n + 1) * 512]
        toks = norm_heads(g, s, 2, 2, 256, lambda c, n=n: g.P("ml_norm", 2 * n + c), g.C("ones", 0, 128), [th[n]])
        t = g.v_tt(s, s, og.ap[:, :], ALU.mult, tg, *toks)
        g.tmp.put(og, t)
        t1, t2 = g.split_act(zh[:, n * 512:(n + 1) * 512], zl[:, n * 512:(n + 1) * 512], s, t, *base)
        tz += [t2, t2]
    return out_add(g, "ml_out", 0, zh, zl, tz)


def swa(g, tx):
    per_k, r, tr = second_norm(g, 2, 1, [tx])
    rc, trc = token_factor(g, r, tr)
    fa = g.fa
    q, k = fa[:, 0:2048], fa[:, 2048:3072]
    V = fa[:, 3072:3584]
    o = fa[:, 3584:5632]
    base = [g.pe.last(), g.act.last(), g.dve.last()]
    tq = []
    gq = g.small[:, 540:541]
    t0 = g.v_ts(gq, g.P("sw_q_norm", 0), 0.125, None, ALU.mult, None, *base)
    for n in range(4):
        (ps, tok), = g.proj("sw_in", n, 8, 256, g.hh, g.hl, [], per_k=per_k)
        t = evac_scaled(g, q[:, n * 512:(n + 1) * 512], ps, tok, r, tr, *base)
        tq += norm_heads(g, q[:, n * 512:(n + 1) * 512], 2, 1, 64, lambda c: gq, g.C("ones64", 0, 128), [t, t0])
    for n in range(2):
        (ps, tok), = g.proj("sw_in", 4 + n, 8, 256, g.hh, g.hl, [])
        t = evac_scaled(g, k[:, n * 512:(n + 1) * 512], ps, tok, r, tr, *base)
        tq += norm_heads(g, k[:, n * 512:(n + 1) * 512], 2, 1, 64, lambda c: g.P("sw_k_norm", 0),
                         g.C("ones64", 0, 128), [t])
    banks = [g.ps.get() for _ in range(2)]
    tok = token_major(g, "sw_in", [6], 256, None, banks, per_k)
    tv = []
    for tb in range(2):
        t = g.v_ts(V[:, tb * 256:(tb + 1) * 256], banks[tb].ap[:, 0:256], rc[:, tb:tb + 1], None, ALU.mult, None,
                   tok, trc, *base)
        g.ps.put(banks[tb], t)
        tv.append(t)
    A = g.attn
    tps = [g.pe.last(), g.pe.last()]
    tpv = g.pe.last()
    zh, zl = g.ra[:, 0:2048], g.ra[:, 2048:4096]
    tz = []
    for h in range(16):
        c, p0, gk = h // 2, 64 * (h % 2), h // 4
        ps = g.ps.get()
        g.mm(ps.ap[:, 0:128], q[p0:p0 + 64, c * T:c * T + 128], k[p0:p0 + 64, gk * T:gk * T + 128],
             after=[*tq, *ps.free], inc=False)
        tok = g.mm(ps.ap[:, 128:384], q[p0:p0 + 64, c * T + 128:(c + 1) * T], k[p0:p0 + 64, gk * T:(gk + 1) * T])
        S = A[:, (h % 2) * 384:(h % 2 + 1) * 384]
        slope = 2.0 ** (-8.0 * (h + 1) / 16)
        b, rs, t = softmax3(g, S, S, tok, ps, (g.C("dist3", 0, 384), slope), 1.0, sink=g.P("sw_sinks", h),
                            post=[tps[h % 2]])
        for a, n, i in ((0, 128, 0), (128, 256, 1)):
            ta = g.v_ts(S[:, a:a + n], S[:, a:a + n], rs[:, i:i + 1], None, ALU.mult, None, t)
        g.cols.put(b, ta)
        PT = A[:, 768:1152]
        tps[h % 2], tpt = turn3(g, S, PT, [ta], [tpv])
        if h % 2 == 0:
            po = g.ps.get()
        g.mm(po.ap[p0:p0 + 64, 0:256], V[:, gk * 64:(gk + 1) * 64], PT[:, 0:256], last=False, inc=False,
             after=[tpt, *tv, *po.free])
        tpv = g.mm(po.ap[p0:p0 + 64, 128:256], V[:, 256 + gk * 64:256 + (gk + 1) * 64], PT[:, 256:384], first=False)
        if h % 2:
            oo = o[:, c * T:(c + 1) * T]
            t = g.v_copy(oo, po.ap[:, 0:256], tpv, *base)
            g.ps.put(po, t)
            t1, t2 = g.split_act(g.xk(zh, c), g.xk(zl, c), oo, t, *base)
            tz.append(t2)
    return out_add(g, "sw_out", 0, zh, zl, tz)


def ple(g, layer, tx):
    per_k, r, tr = second_norm(g, layer, 3, [tx])
    gate = g.fa[:, 2048:4096]
    base = [g.pe.last(), g.act.last(), g.dve.last()]
    pt = g.fa[:, 4096:4608]
    ph, pl = g.ra[:, 0:512], g.ra[:, 512:1024]
    g.sp.dma(lambda e: e.dma_start(pt, g.args["pT"][layer]), g.s_p[1], *base)
    t1, t2 = g.split_act(ph, pl, pt, (g.s_p[1], 16 * (layer + 1)), *base)
    tp = [t1, t2]
    tg = []
    for j in range(4):
        (ps, tok), = g.proj("ple_gate", layer * 4 + j, 8, 256, g.hh, g.hl, [], per_k=per_k)
        s = gate[:, j * 512:(j + 1) * 512]
        t = evac_scaled(g, s, ps, tok, r, tr, *base)
        tg.append(g.a_act(s, s, ACT.Sigmoid, t))
    w = g.weight("ple_proj", layer)
    for j in range(4):
        ps = g.ps.get()
        for c in range(2):
            tok = g.group(w, 2, 1024, ph, pl, (2 * j + c) * 128, ps.ap[:, c * T:(c + 1) * T], [*tp, *ps.free])
        s = gate[:, j * 512:(j + 1) * 512]
        t = g.v_tt(s, s, ps.ap[:, :], ALU.mult, tok, tg[j])
        g.ps.put(ps, t)
        xs = g.x[:, j * 512:(j + 1) * 512]
        t = g.v_tt(xs, xs, s, ALU.add, t, base[1])
    g.done(w, tok)
    return t


STAGES = ["mix0", "ffn0", "mix1", "ffn1"] + [f"{a}{n}" for n in range(4) for a in ("h1_", "mx_", "h2_", "pl_")]


def emit(g, start=0, stop=99):
    t0 = load_small(g)
    g.dve.wait(t0)
    g.act.wait(t0)
    g.pe.wait(t0)
    tx = t0
    tables(g, t0)
    for lay in range(2):
        if start <= 2 * lay + 1 and 2 * lay < stop:
            tmod = modulation(g, lay, g.mod[:, 0:48], g.small[:, 570:578],
                              [g.pe.last(), g.act.last(), g.dve.last()])
        if start <= 2 * lay < stop:
            tx = mix_first(g, lay, g.mod, tmod, [])
        if start <= 2 * lay + 1 < stop:
            tx = first_ffn(g, lay, g.mod, tmod)
    for layer in range(4):
        s = 4 + 4 * layer
        if start <= s < stop:
            tx = second_ffn(g, layer, 0, tx)
        if start <= s + 1 < stop:
            tx = [lambda: hgrn(g, layer, layer // 3, tx), lambda: mlstm(g, tx), lambda: swa(g, tx)][layer % 3]()
        if start <= s + 2 < stop:
            tx = second_ffn(g, layer, 1, tx)
        if start <= s + 3 < stop:
            tx = ple(g, layer, tx)
    g.sp.dma(lambda e: e.dma_start(g.args["out"], g.x[:, :]), g.s_out, tx)
    g.sp.wait((g.s_out, 16))


def build(nc: bass.Bass, args, order, start=0, stop=99):
    with ExitStack() as ctx:
        g = Program(nc, ctx, args, order)
        emit(g, start, stop)
        block = ctx.enter_context(nc.Block())

        @block.sync
        def _(eng):
            g.sp.play(eng)

        @block.scalar
        def _(eng):
            g.act.play(eng)

        @block.vector
        def _(eng):
            g.dve.play(eng)

        @block.tensor
        def _(eng):
            g.pe.play(eng)

        @block.gpsimd
        def _(eng):
            g.pool.play(eng)


def cols(v):
    v = np.asarray(v)
    return v.reshape(-1, 128).T


def rows_to(v, n=128):
    a = np.zeros((128, v.shape[1]), np.float32)
    a[:v.shape[0]] = v
    return a


def layout(i):
    par = [cols(i["c"]), cols(i["g_pre_mix"]), cols(i["b_ada"]),
           rows_to(np.stack([i[n][l] for l in range(2) for n in ("da_lam_q1", "da_lam_k1", "da_lam_q2", "da_lam_k2")], 1)),
           cols(i["da_g_subln"]), cols(i["mla_g_cq"]), cols(i["mla_g_ckv"]), cols(i["sc_conv"]), cols(i["cf_conv"]),
           cols(i["cf_conv_b"]), cols(i["cf_ln_g"]), cols(i["cf_ln_b"]), cols(i["g_post_mix"]), cols(i["g_pre_ffn"]),
           cols(i["ffn_conv"]), cols(i["g_post_ffn"]), cols(i["norm_gains_2"]), cols(i["hg_lower_bounds_2"]),
           cols(i["hg_g_norm_2"]), rows_to(np.asarray(i["ml_b_if_2"]).reshape(2, 4).T), cols(i["ml_norm_2"]),
           np.concatenate([np.asarray(i["sw_q_norm_2"]).T] * 2, 0), np.concatenate([np.asarray(i["sw_k_norm_2"]).T] * 2, 0),
           np.broadcast_to(np.asarray(i["sw_sinks_2"]), (128, 16)),
           np.asarray(i["ml_w_if_2"])[0].reshape(8, 128, 8).transpose(1, 0, 2).reshape(128, 64)]
    par = np.concatenate([np.asarray(p) for p in par], 1)
    assert par.shape == (128, NPAR)

    def kn(ws, n, plan=None):
        return np.stack([tiles_kn(w, c) for w in ws for c in (plan or [_span(a, n) for a in range(0, w.shape[1], n)])])

    dup = [sum([_span(1024 + 64 * (2 * a + b // 2), 64) for b in range(4)], []) for a in range(2)]
    gu = [_span(128 * a, 128) + _span(2816 + 128 * a, 128) for a in range(22)]

    def ko(ws):
        return np.stack([np.ascontiguousarray(w[a:a + 256].reshape(2, 128, 1024).transpose(1, 0, 2)).reshape(128, 2048)
                         for w in ws for a in range(0, 2816, 256)])

    out = {
        "params": par, "consts": constants(), "positions": np.asarray(i["positions"]),
        "xT": np.ascontiguousarray(np.asarray(i["x"])[0].T.reshape(8, 128, 256).transpose(1, 0, 2)).reshape(128, 2048),
        "pT": np.ascontiguousarray(np.asarray(i["p_2"])[:, 0].transpose(0, 2, 1).reshape(4, 2, 128, 256)
                                   .transpose(0, 2, 1, 3)).reshape(4, 128, 512),
        "w_ada": kn(i["w_ada"], 256), "w_in": kn(i["w_in"], 0, WIN),
        "w_mc": kn(i["w_in"], 0, [_span(2048, 160)]),
        "da_w_o": kn(i["da_w_o"], 512), "mla_w_o": kn(i["mla_w_o"], 512), "sc_w_o": kn(i["sc_w_o"], 512),
        "cf_w_o": kn(i["cf_w_o"], 512), "mla_w_uq": kn(i["mla_w_uq"], 384), "mla_w_ukv": kn(i["mla_w_ukv"], 1024),
        "w_mix_out": kn(i["w_mix_out"], 256), "w_up": kn(i["w_up"], 0, gu), "w_down": ko(i["w_down"]),
        "w_gu": kn(np.asarray(i["w_ffn_gu_2"]).reshape(8, 1024, 5632), 0, gu),
        "w_dn": ko(np.asarray(i["w_ffn_down_2"]).reshape(8, 2816, 1024)),
        "ple_gate": kn(i["w_ple_gate_2"], 256), "ple_proj": kn(i["w_ple_proj_2"], 1024),
        "hg_in": kn(i["hg_w_in_2"], 256), "hg_out": kn(i["hg_w_out_2"], 256),
        "ml_in": kn(i["ml_w_qkvo_2"], 256), "ml_out": kn(i["ml_w_out_2"], 256),
        "sw_in": kn(i["sw_w_qkv_2"], 0, [_span(256 * a, 256) for a in range(4)] + dup + [_span(1280, 256)]), "sw_out": kn(i["sw_w_o_2"], 256),
    }
    return out


def weight_order(start=0, stop=99):
    out = []

    def add(name, *ns, split=True):
        out.extend((name, n, split) for n in ns)

    def ffn_tiles(up, up0, down, dn0):
        for p in range(NF // 2):
            add(up, up0 + 2 * p, up0 + 2 * p + 1)
            if p:
                add(down, dn0 + p - 1)
        add(down, dn0 + NF // 2 - 1)

    def merge_tiles(lay, wo, branch):
        for n in range(2):
            add(wo, lay * 2 + n)
            if branch is not None:
                add("w_in", *[lay * 34 + GATE0 + 4 * branch + 2 * n + i for i in range(2)])

    for lay in range(2):
        if start <= 2 * lay + 1 and 2 * lay < stop:
            add("w_ada", *range(lay * 24, lay * 24 + 24), split=False)
        if start <= 2 * lay < stop:
            w = lay * 34
            add("w_in", *range(w, w + MLA0))
            merge_tiles(lay, "sc_w_o", 2)
            add("w_in", w + MLA0, w + MLA0 + 1)
            add("w_mc", lay)
            add("mla_w_uq", 2 * lay, 2 * lay + 1)
            add("mla_w_ukv", lay)
            add("w_in", *range(w + GATE0 + 4, w + GATE0 + 8))
            merge_tiles(lay, "da_w_o", 0)
            merge_tiles(lay, "cf_w_o", 3)
            merge_tiles(lay, "mla_w_o", None)
            add("w_mix_out", *range(4 * lay, 4 * lay + 4))
        if start <= 2 * lay + 1 < stop:
            ffn_tiles("w_up", lay * 22, "w_down", lay * 11)
    for layer in range(4):
        s = 4 + 4 * layer
        j = layer // 3
        if start <= s < stop:
            ffn_tiles("w_gu", layer * 44, "w_dn", layer * 22)
        if start <= s + 1 < stop:
            if layer % 3 == 0:
                for a in (0, 2):
                    add("hg_in", *[16 * j + a + n for n in (0, 1, 4, 5, 8, 9)])
                add("hg_in", *range(16 * j + 12, 16 * j + 16))
                add("hg_out", *range(4 * j, 4 * j + 4))
            elif layer == 1:
                add("ml_in", *range(12))
                add("ml_out", *range(4))
            else:
                add("sw_in", *range(7))
                add("sw_out", *range(4))
        if start <= s + 2 < stop:
            ffn_tiles("w_gu", layer * 44 + 22, "w_dn", layer * 22 + 11)
        if start <= s + 3 < stop:
            add("ple_gate", *range(layer * 4, layer * 4 + 4))
            add("ple_proj", layer)
    return out


def kernel(**inputs):
    import concourse.bacc as _bacc
    from concourse.bass_utils import run_bass_kernel_spmd as _run

    arrays = layout({k: np.asarray(v) for k, v in inputs.items()})
    nc = _bacc.Bacc("TRN2", target_bir_lowering=False, num_devices=1)
    args = {k: nc.dram_tensor(k, v.shape, mybir.dt.from_np(v.dtype), kind="ExternalInput").ap() for k, v in arrays.items()}
    args["out"] = nc.dram_tensor("out", (128, 2048), F32, kind="ExternalOutput").ap()
    build(nc, args, weight_order())
    r = _run(nc, [arrays], core_ids=[0])
    o = r.results[0]["out"]
    return np.ascontiguousarray(o.reshape(128, 8, 256).transpose(1, 0, 2).reshape(1024, 256).T)[None]
```

```python
import math
from contextlib import ExitStack

import numpy as np
import concourse.bass as bass
from concourse import mybir

F32 = mybir.dt.float32
F32R = mybir.dt.float32r
I32 = mybir.dt.int32
ALU = mybir.AluOpType
ACT = mybir.ActivationFunctionType
AX = mybir.AxisListType.X

D = 1024
T = 256
NC = 8
NF = 22
TILE = 2048
NEG = -1e30

PARAM_COLS = {}


def _plan_params():
    at = 0
    for name, n in [("c", 8), ("g_pre_mix", 16), ("b_ada", 96), ("lam", 8), ("da_g_subln", 2),
                    ("mla_g_cq", 6), ("mla_g_ckv", 4), ("sc_conv", 24), ("cf_conv", 248),
                    ("cf_conv_b", 8), ("cf_ln_g", 8), ("cf_ln_b", 8), ("g_post_mix", 16),
                    ("g_pre_ffn", 16), ("ffn_conv", 132), ("g_post_ffn", 16), ("norm_gains", 128),
                    ("hg_lb", 32), ("hg_g_norm", 2), ("ml_b_if", 2), ("ml_norm", 8),
                    ("sw_q_norm", 1), ("sw_k_norm", 1), ("sw_sinks", 16), ("w_if", 64)]:
        PARAM_COLS[name] = at
        at += n
    return at


NPAR = _plan_params()

CONST_COLS = {}


def _plan_consts():
    at = 0
    for name, n in [("ident", 128), ("ones", 128), ("ones64", 128), ("mask3", 384), ("dist3", 384),
                    ("maskT", 128), ("lev", 192), ("rot", 96), ("inv", 1), ("rst", 256)]:
        CONST_COLS[name] = at
        at += n
    return at


NCON = _plan_consts()


def constants():
    c = np.zeros((128, NCON), np.float32)

    def put(name, a):
        c[:a.shape[0], CONST_COLS[name]:CONST_COLS[name] + a.shape[1]] = a

    i = np.arange(128)
    put("ident", np.eye(128, dtype=np.float32))
    put("ones", np.ones((128, 128), np.float32))
    put("ones64", (i[:, None] // 64 == i[None, :] // 64).astype(np.float32))
    causal = np.where(i[None, :] <= i[:, None], 0.0, NEG)
    put("mask3", np.concatenate([causal, np.zeros((128, 128)), causal], 1))
    same = i[:, None] - i[None, :]
    prev = same + 128
    put("dist3", np.concatenate([np.where(same >= 0, same, -NEG * 1e3), np.where(prev < 128, prev, -NEG * 1e3),
                                 np.where(same >= 0, same, -NEG * 1e3)], 1))
    put("maskT", (i[None, :] >= i[:, None]).astype(np.float32))
    s = (i % 32)[:, None]
    t = np.arange(32)[None, :]
    lev = []
    for m in (16, 8, 4, 2, 1):
        lev.append((s // (2 * m) == t // (2 * m)) & (s % (2 * m) < m) & (t % (2 * m) >= m))
    lev.append(s == t)
    put("lev", np.concatenate(lev, 1).astype(np.float32))
    rot = np.zeros((128, 96), np.float32)
    for n in range(16):
        rot[80 + n, 64 + n] = -1.0
        rot[64 + n, 80 + n] = 1.0
    put("rot", rot)
    inv = np.zeros((128, 1), np.float32)
    f = (np.float32(10000.0) ** (-np.arange(16, dtype=np.float32) / np.float32(16))).astype(np.float32)
    inv[64:80, 0] = f
    inv[80:96, 0] = f
    put("inv", inv)
    put("rst", np.tile((np.arange(256) % 64 != 0).astype(np.float32), (128, 1)))
    return c


def tiles_kn(w, cols):
    k = w.shape[0] // 128
    return np.ascontiguousarray(w[:, cols].reshape(k, 128, len(cols)).transpose(1, 0, 2)).reshape(128, -1)


def _span(a, n):
    return list(range(a, a + n))


def plan_win():
    t = []
    for j in range(4):
        t.append(_span(3744 + 128 * j, 128) + _span(3744 + 512 + 128 * j, 128))
    for j in range(6):
        t.append(_span(256 * j, 256))
    for j in range(4):
        t.append(_span(2208 + 128 * j, 128) + _span(2208 + 1024 + 128 * j, 128))
    for j in range(2):
        t.append(_span(2208 + 512 + 256 * j, 256))
    for j in range(2):
        t.append(_span(1536 + 256 * j, 256))
    for j in range(16):
        t.append(_span(4768 + 256 * j, 256))
    return t


WIN = plan_win()
CF0, DA0, SCU0, SCB0, MLA0, GATE0 = 0, 4, 10, 14, 16, 18
TWO_PI = 2.0 * math.pi


class Queue:
    def __init__(self, sem, on=True):
        self.sem, self.n, self.ops, self.seen, self.on = sem, 0, [], {}, on

    def wait(self, *tokens):
        for t in tokens:
            if t is None:
                continue
            if isinstance(t, list):
                self.wait(*t)
                continue
            sem, v = t
            if v > 0 and self.seen.get(sem.name, 0) < v:
                self.seen[sem.name] = v
                self.ops.append(("w", sem, v))

    def op(self, fn, *after):
        self.wait(*after)
        self.n += 1
        self.ops.append(("i", fn, self.sem, 1))
        return (self.sem, self.n)

    def quiet(self, fn, *after):
        self.wait(*after)
        self.ops.append(("q", fn))

    def dma(self, fn, sem, *after):
        self.wait(*after)
        self.ops.append(("i", fn, sem, 16))

    def last(self):
        return (self.sem, self.n)

    def play(self, eng):
        for o in self.ops:
            if o[0] == "w":
                eng.wait_ge(o[1], o[2])
            elif o[0] == "i":
                o[1](eng).then_inc(o[2], o[3])
            else:
                o[1](eng)


class Buf:
    def __init__(self, ap):
        self.ap, self.free = ap, []


class Ring:

    def __init__(self, aps):
        self.bufs = [Buf(a) for a in aps]

    def get(self):
        return self.bufs.pop(0)

    def put(self, buf, *tokens):
        buf.free = [t for t in tokens]
        self.bufs.append(buf)


class Program:
    def __init__(self, nc, ctx, args, order, depth=3):
        self.nc, self.args, self.order, self.asked, self.ready = nc, args, order, 0, []
        self.depth = depth

        def sem(name):
            return ctx.enter_context(nc.semaphore(name))

        def sb(name, n, dt=F32):
            return ctx.enter_context(nc.sbuf_tensor(name, [128, n], dt))

        self.pe, self.act, self.dve, self.pool, self.sp = [Queue(sem("s_" + n)) for n in
                                                           ("pe", "act", "dve", "pool", "sp")]
        self.NL, self.NS = 3, 3
        self.land = sb("land", self.NL * TILE)
        self.whi = sb("whi", self.NS * TILE, F32R)
        self.wlo = sb("wlo", self.NS * TILE, F32R)
        self.s_land = [sem(f"s_land{i}") for i in range(self.NL)]
        self.s_misc = sem("s_misc")
        self.s_con = sem("s_con")
        self.s_out = sem("s_out")
        self.s_p = [sem("s_p0"), sem("s_p1")]
        self.n_p = 0
        self.t_mod = [None, None]
        self.sc = sb("sc", 8)
        self.nload = 0
        self.nsplit = 0
        self.land_free = [[] for _ in range(self.NL)]
        self.land_use = [0] * self.NL
        self.split_free = [[] for _ in range(self.NS)]
        self.x = sb("x", NC * T)
        self.hh = sb("hh", NC * T, F32R)
        self.hl = sb("hl", NC * T, F32R)
        self.par = sb("par", NPAR)
        self.con = sb("con", NCON)
        self.attn = sb("attn", 1152)
        self.sring = Ring([self.attn[:, i * 384:(i + 1) * 384] for i in range(3)])
        self.trig = sb("trig", 512)
        self.mod = sb("mod", 96)
        self.tmps = sb("tmps", 4 * 512)
        self.small = sb("small", 1024)
        self.ps = Ring([ctx.enter_context(nc.psum_tensor(f"ps{i}", [128, 512], F32)) for i in range(8)])
        self.cols = Ring([self.small[:, 600 + i * 16:616 + i * 16] for i in range(4)])
        self.tmp = Ring([self.tmps[:, i * 512:(i + 1) * 512] for i in range(4)])

    def scope(self, ctx, n, fa, ra):
        self.fa = ctx.enter_context(self.nc.sbuf_tensor(f"fa{n}", [128, fa], F32))
        self.ra = ctx.enter_context(self.nc.sbuf_tensor(f"ra{n}", [128, ra], F32R))

    def P(self, name, j, rows=128):
        a = PARAM_COLS[name] + j
        return self.par[0:rows, a:a + 1]

    def C(self, name, a, n, p0=0, p1=128):
        a += CONST_COLS[name]
        return self.con[p0:p1, a:a + n]

    def _prepare(self):
        i = len(self.ready)
        name, n, split = self.order[i]
        s = self.nload % self.NL
        self.nload += 1
        self.land_use[s] += 1
        src = self.args[name][n]
        w = src.shape[1]
        dst = self.land[:, s * TILE:s * TILE + w]
        self.sp.dma(lambda e, d=dst, a=src: e.dma_start(d, a), self.s_land[s], *self.land_free[s])
        got = (self.s_land[s], 16 * self.land_use[s])
        if not split:
            self.ready.append((dst, None, got, s, None))
            self.land_free[s] = None
            return
        k = self.nsplit % self.NS
        self.nsplit += 1
        hi, lo = self.whi[:, k * TILE:k * TILE + w], self.wlo[:, k * TILE:k * TILE + w]
        t1 = self.act.op(lambda e, o=hi, a=dst: e.activation(o, a, ACT.Copy), got, *self.split_free[k])
        t2 = self.dve.op(lambda e, o=lo, a=dst, b=hi.bitcast(F32): e.tensor_tensor(o, a, b, ALU.subtract),
                         got, t1, *self.split_free[k])
        self.land_free[s] = [t1, t2]
        self.split_free[k] = None
        self.ready.append((hi, lo, t2, s, k))

    def weight(self, name, n, split=True):
        i = self.asked
        self.asked += 1
        assert self.order[i] == (name, n, split)
        top = min(i + self.depth, len(self.order))
        while len(self.ready) <= i or (len(self.ready) < top and self._room()):
            self._prepare()
        return self.ready[i]

    def _room(self):
        name, n, split = self.order[len(self.ready)]
        return self.land_free[self.nload % self.NL] is not None and (
            not split or self.split_free[self.nsplit % self.NS] is not None)

    def done(self, w, token):
        if w[4] is None:
            self.land_free[w[3]] = [token]
        else:
            self.split_free[w[4]] = [token]

    def mm3(self, out, wh, wl, xh, xl, first, last, skip=False, inc=False, after=()):
        pe = self.pe
        pe.wait(*after)
        pe.quiet(lambda e: e.matmul(out, wh, xh, start=first, stop=False, skip_group_check=skip))
        pe.quiet(lambda e: e.matmul(out, wh, xl, start=False, stop=False, skip_group_check=skip))
        fn = lambda e: e.matmul(out, wl, xh, start=False, stop=last, skip_group_check=skip)
        if inc:
            return pe.op(fn)
        pe.quiet(fn)

    def mm(self, out, lhsT, rhs, first=True, last=True, after=(), inc=True, skip=False):
        fn = lambda e: e.matmul(out, lhsT, rhs, start=first, stop=last, skip_group_check=skip)
        self.pe.wait(*after)
        if inc:
            return self.pe.op(fn)
        self.pe.quiet(fn)

    def xk(self, t, k):
        return t[:, k * T:(k + 1) * T]

    def v_tt(self, out, a, b, op, *after):
        return self.dve.op(lambda e: e.tensor_tensor(out, a, b, op), *after)

    def p_tt(self, out, a, b, op, *after):
        return self.pool.op(lambda e: e.tensor_tensor(out, a, b, op), *after)

    def v_ts(self, out, a, s1, s2, op0, op1, *after):
        if op1 is None:
            return self.dve.op(lambda e: e.tensor_scalar(out, a, s1, None, op0), *after)
        return self.dve.op(lambda e: e.tensor_scalar(out, a, s1, s2, op0, op1), *after)

    def v_stt(self, out, a, s, b, op0, op1, *after):
        return self.dve.op(lambda e: e.scalar_tensor_tensor(out, a, s, b, op0, op1), *after)

    def v_copy(self, out, a, *after):
        return self.dve.op(lambda e: e.tensor_copy(out, a), *after)

    def a_act(self, out, a, f, *after, **kw):
        return self.act.op(lambda e: e.activation(out, a, f, **kw), *after)

    def split_act(self, hi, lo, src, *after):
        t1 = self.a_act(hi, src, ACT.Copy, *after)
        return t1, self.v_tt(lo, src, hi.bitcast(F32), ALU.subtract, t1, *after)

    def rsqrt(self, out, v, t):
        b = self.tmp.get()
        n = v.shape[1]
        p = v.shape[0]
        y, z = b.ap[0:p, 0:n], b.ap[0:p, 256:256 + n]
        t1 = self.a_act(y, v, ACT.Ln, t, *b.free)
        t1 = self.a_act(y, y, ACT.Exp, t1, scale=-0.5)
        t2 = self.v_tt(z, y, y, ALU.mult, t1, *b.free)
        t2 = self.v_stt(z, z, -0.5, v, ALU.mult, ALU.mult, t2)
        t2 = self.v_stt(out, z, 1.5, y, ALU.add, ALU.mult, t2)
        self.tmp.put(b, t1, t2)
        return t2

    def stats(self, src, n, dim, eps, out, vbuf, sq, after):
        t1, finish = self.stats_later(src, n, dim, eps, out, vbuf, sq, after)
        return finish(), t1

    def stats_later(self, src, n, dim, eps, out, vbuf, sq, after):
        t1 = self.a_act(sq[:, 0:n * T], src, ACT.Square, *after)
        b = self.tmp.get()
        t2 = self.dve.op(lambda e: e.tensor_reduce(
            b.ap[:, 0:T], sq[:, 0:n * T].rearrange("p (c t) -> p t c", c=n), AX, ALU.add), t1, *b.free)

        def finish():
            ps = self.ps.get()
            t3 = self.mm(ps.ap[:, 0:T], self.C("ones", 0, 128), b.ap[:, 0:T], after=[t2, *ps.free])
            self.tmp.put(b, t3)
            t4 = self.v_ts(vbuf, ps.ap[:, 0:T], 1.0 / dim, eps, ALU.mult, ALU.add, t3, *after)
            self.ps.put(ps, t4)
            return self.rsqrt(out, vbuf, t4)

        return t1, finish

    def group(self, w, kc, width, xh, xl, cols, out, after, m=128, per_k=None):
        wh, wl = w[0], w[1]
        for k in range(kc):
            a = k * width + cols
            ready = [w[2], *after] if k == 0 else []
            if per_k:
                ready = ready + [per_k[k]]
            tok = self.mm3(out, wh[:, a:a + m], wl[:, a:a + m], self.xk(xh, k), self.xk(xl, k),
                           k == 0, k == kc - 1, inc=k == kc - 1, after=ready)
        return tok

    def proj(self, name, n, kc, width, xh, xl, after, per_k=None):
        w = self.weight(name, n)
        out = []
        ng = (width + 127) // 128
        for j in range(0, ng, 2):
            ps = self.ps.get()
            for i in range(j, min(j + 2, ng)):
                tok = self.group(w, kc, width, xh, xl, i * 128, ps.ap[:, (i - j) * T:(i - j + 1) * T],
                                 [*ps.free, *after], per_k=per_k)
            out.append((ps, tok))
        self.done(w, tok)
        return out

    def split_gain(self, gname, g0, n, src, after, free=()):
        toks = []
        for k in range(n):
            s, g = self.xk(src, k), self.P(gname, g0 + k)
            h, l = self.xk(self.hh, k), self.xk(self.hl, k)
            t1 = self.a_act(h, s, ACT.Identity, *after, *free, scale=g)
            t2 = self.v_stt(l, s, g, h.bitcast(F32), ALU.mult, ALU.subtract, t1, *after, *free)
            toks.append(t2)
        return toks


class Later:

    def __init__(self, fn):
        self.fn, self.token = fn, None

    def get(self):
        if self.token is None:
            self.token = self.fn()
        return self.token


def bc2(ap):
    return ap.unsqueeze(1).broadcast_to([ap.shape[0], 2, ap.shape[1]])


def v2(ap):
    return ap.rearrange("p (a t) -> p a t", a=2)


def sigmoid(g, out, src, *after):
    t1 = g.a_act(out, src, ACT.Exp, *after, scale=-1.0)
    t = g.v_ts(out, out, 1.0, None, ALU.add, None, t1)
    return g.dve.op(lambda e: e.reciprocal(out, out), t), t1


def exp_silu(g, out, src, tmp, after):
    t, _ = sigmoid(g, tmp, src, *after)
    return g.v_tt(out, src, tmp, ALU.mult, t)


def load_small(g):
    a = g.args
    g.sp.dma(lambda e: e.dma_start(g.par[:, :], a["params"]), g.s_misc)
    g.act.dma(lambda e: e.dma_start(g.x[:, :], a["xT"]), g.s_misc)
    g.act.dma(lambda e: e.dma_start(g.con[:, :], a["consts"]), g.s_con)
    return (g.s_misc, 32), (g.s_con, 16)


def modulation_tile(g, lay, j):
    w = g.weight("w_ada", lay * 24 + j, split=False)
    wt = w[0]
    if lay == 0 and j < 8:
        ps = g.ps.get()
        for i in range(2):
            for k in range(8):
                tok = g.mm(ps.ap[:, i:i + 1], wt[:, k * 256 + i * 128:k * 256 + i * 128 + 128], g.sc[:, k:k + 1],
                           first=k == 0, last=k == 7, after=[w[2], g.t_sc, *ps.free] if k == 0 else (), inc=k == 7)
    else:
        t = g.p_tt(wt.rearrange("p (k n) -> p k n", k=8), wt.rearrange("p (k n) -> p k n", k=8),
                   g.sc[:, 0:8].unsqueeze(2).broadcast_to([128, 8, 256]), ALU.mult, w[2], g.t_sc)
        for n in (1024, 512, 256):
            t = g.p_tt(wt[:, 0:n], wt[:, 0:n], wt[:, n:2 * n], ALU.add, t)
        ps = g.ps.get()
        for i in range(2):
            tok = g.mm(ps.ap[:, i:i + 1], wt[:, i * 128:i * 128 + 128], g.C("ones", 0, 1), after=[t, *ps.free])
    g.done(w, tok)
    a = PARAM_COLS["b_ada"] + lay * 48 + 2 * j
    c = lay * 48 + 2 * j
    t = g.v_tt(g.mod[:, c:c + 2], ps.ap[:, 0:2], g.par[:, a:a + 2], ALU.add, tok)
    g.ps.put(ps, t)
    g.t_mod[lay] = t


ADA_IN_MIX = [2, 2, 2, 2, 2, 2, 1, 1, 1, 1]


def modulated(g, gname, lay, mod, shift, scale, after):
    fa = g.fa
    xr, v, r = fa[:, 0:2048], g.small[:, 0:256], g.small[:, 256:512]
    A = g.small[:, 560:568]
    gc = PARAM_COLS[gname] + lay * 8
    t0 = g.v_ts(A, mod[:, scale:scale + 8], 1.0, None, ALU.add, None, *after)
    t0 = g.v_tt(A, A, g.par[:, gc:gc + 8], ALU.mult, t0)
    t1, tsq = g.stats(g.x[:, :], 8, D, 1e-6, r, v, xr, after)
    toks = []
    for k in range(8):
        s = g.xk(xr, k)
        t2 = g.v_tt(s, g.xk(g.x, k), r, ALU.mult, t1, tsq)
        t2 = g.v_ts(s, s, A[:, k:k + 1], mod[:, shift + k:shift + k + 1], ALU.mult, ALU.add, t2, t0)
        _, t3 = g.split_act(g.xk(g.hh, k), g.xk(g.hl, k), s, t2, g.pe.last())
        toks.append(t3)
    return toks


def add_normed(g, y, lay, gname, mod, gate, ty):
    v, r = g.small[:, 0:256], g.small[:, 256:512]
    B = g.small[:, 560:568]
    gc = PARAM_COLS[gname] + lay * 8
    t0 = g.v_tt(B, mod[:, gate:gate + 8], g.par[:, gc:gc + 8], ALU.mult, *ty)
    t1, tsq = g.stats(y, 8, D, 1e-6, r, v, g.fa[:, 2048:4096], ty)
    for k in range(8):
        s = g.xk(y, k)
        t2 = g.v_tt(s, s, r, ALU.mult, t1, tsq)
        t2 = g.v_stt(g.xk(g.x, k), s, B[:, k:k + 1], g.xk(g.x, k), ALU.mult, ALU.add, t2, t0)
    return t2


def conv3(g, out, src, name, j, step, after):
    t = g.v_ts(out, src[:, 2:258], g.P(name, j + 2 * step), None, ALU.mult, None, *after)
    t = g.v_stt(out, src[:, 1:257], g.P(name, j + step), out, ALU.mult, ALU.add, t)
    return g.v_stt(out, src[:, 0:256], g.P(name, j), out, ALU.mult, ALU.add, t)


def down_setup(g):
    return [g.ps.get() for _ in range(4)]


def down_pair(g, name, n, acc, yb, ty, first, last):
    w = g.weight(name, n)
    yh, yl = yb.ap
    for c in range(2):
        for m in range(8):
            bank = acc[m // 2]
            a = c * 1024 + m * 128
            f = first and c == 0
            tok = g.mm3(bank.ap[:, (m % 2) * T:(m % 2 + 1) * T], w[0][:, a:a + 128], w[1][:, a:a + 128],
                        g.xk(yh, c), g.xk(yl, c), f and m % 2 == 0, last and c == 1, skip=True,
                        inc=m == 7 or (last and c == 1 and m % 2 == 1),
                        after=[w[2], *ty, *(bank.free if f else [])])
            if last and c == 1 and m % 2 == 1:
                bank.ready = tok
    g.done(w, tok)
    return tok


def ffn(g, up, up0, down, dn0, per_k, chunk, side=None):
    acc = down_setup(g)
    R = [Buf((g.ra[:, i * 1024:i * 1024 + 512], g.ra[:, i * 1024 + 512:i * 1024 + 1024])) for i in range(3)]
    for b in R:
        b.free = [g.pe.last()]
    ready = []
    npair = NF // 2

    def do_down(p):
        b, t = ready.pop(0)
        tok = down_pair(g, down, dn0 + p, acc, b, t, p == 0, p == npair - 1)
        b.free = [tok]
        R.append(b)

    for p in range(npair):
        b = R.pop(0)
        toks = []
        for c in range(2):
            (ps, tok), = g.proj(up, up0 + 2 * p + c, 8, 256, g.hh, g.hl, [], per_k=per_k)
            toks.append(chunk(2 * p + c, ps, tok, g.xk(b.ap[0], c), g.xk(b.ap[1], c), b.free))
            if side:
                side(2 * p + c)
        ready.append((b, toks))
        if p >= 1:
            do_down(p - 1)
    if side:
        side(22)
        side(23)
    do_down(npair - 1)
    return acc


def first_ffn(g, lay, mod):
    base = [g.pe.last(), g.act.last(), g.dve.last(), g.t_mod[lay]]
    per_k = modulated(g, "g_pre_ffn", lay, mod, 24, 32, base)
    fa = g.fa
    A = [Buf(fa[:, 4096 + i * 512:4096 + i * 512 + 258]) for i in range(2)]
    S = [Buf(fa[:, 5120 + i * 256:5376 + i * 256]) for i in range(2)]
    for b in A:
        t = g.dve.op(lambda e, b=b: e.memset(b.ap[:, 0:2], 0.0), *base)
        b.free = [t]

    def chunk(j, ps, tok, yh, yl, free):
        a, s = A[j % 2].ap, S[j % 2].ap
        t = g.v_copy(a[:, 2:258], ps.ap[:, 0:T], tok, *A[j % 2].free)
        o = g.tmp.get()
        c1 = o.ap[:, 0:T]
        t = conv3(g, c1, a, "ffn_conv", lay * 66 + j, 22, [t, *o.free])
        A[j % 2].free = [t]
        t1 = g.a_act(s, c1, ACT.Silu, t)
        t2 = g.v_tt(o.ap[:, T:2 * T], s, ps.ap[:, T:2 * T], ALU.mult, t1, tok)
        g.ps.put(ps, t2)
        t3, t4 = g.split_act(yh, yl, o.ap[:, T:2 * T], t2, *free)
        g.tmp.put(o, t3, t4)
        return t4

    acc = ffn(g, "w_up", lay * 22, "w_down", lay * 11, per_k, chunk,
              (lambda j: modulation_tile(g, 1, j)) if lay == 0 else None)
    y = fa[:, 0:2048]
    ty = []
    for i, b in enumerate(acc):
        t = g.v_copy(y[:, i * 512:(i + 1) * 512], b.ap[:, :], b.ready)
        g.ps.put(b, t)
        ty.append(t)
    return add_normed(g, y, lay, "g_post_ffn", mod, 40, ty)


def softmax3(g, u, tps, ps, bias, scale, sink=None):
    b = g.cols.get()
    S = u.ap[:, 0:384]
    mx, nm, sm, es = b.ap[:, 0:2], b.ap[:, 2:4], b.ap[:, 4:6], b.ap[:, 8:10]
    if isinstance(bias, tuple):
        t = g.v_stt(S, bias[0], -bias[1], ps.ap[:, 0:384], ALU.mult, ALU.add, tps, *u.free)
    else:
        t = g.v_tt(S, ps.ap[:, 0:384], bias, ALU.add, tps, *u.free)
    g.ps.put(ps, t)
    t1 = g.dve.op(lambda e: e.tensor_reduce(mx[:, 0:1], S[:, 0:128], AX, ALU.max), t, *b.free)
    t1 = g.dve.op(lambda e: e.tensor_reduce(mx[:, 1:2], S[:, 128:384], AX, ALU.max), t, *b.free)
    if sink is not None:
        t1 = g.v_ts(mx, mx, sink, None, ALU.max, None, t1)
    t1 = g.v_ts(nm, mx, -scale, None, ALU.mult, None, t1)
    if sink is not None:
        t3 = g.v_ts(es, nm, sink, None, ALU.add, None, t1)
    g.a_act(S[:, 0:128], S[:, 0:128], ACT.Exp, t1, bias=nm[:, 0:1], scale=scale, accum_out=sm[:, 0:1])
    t2 = g.a_act(S[:, 128:384], S[:, 128:384], ACT.Exp, t1, bias=nm[:, 1:2], scale=scale, accum_out=sm[:, 1:2])
    if sink is not None:
        t2 = g.a_act(es, es, ACT.Exp, t3)
    return b, t2, sink is not None


def softmax3_end(g, state):
    b, t, sink = state
    sm, rs, es = b.ap[:, 4:6], b.ap[:, 6:8], b.ap[:, 8:10]
    if sink:
        t = g.v_tt(sm, sm, es, ALU.add, t)
    return rs, g.dve.op(lambda e: e.reciprocal(rs, sm), t)


def softmax3_scale(g, u, state):
    rs, t = softmax3_end(g, state)
    S = u.ap[:, 0:384]
    for a, n, i in ((0, 128, 0), (128, 256, 1)):
        ta = g.v_ts(S[:, a:a + n], S[:, a:a + n], rs[:, i:i + 1], None, ALU.mult, None, t)
    g.cols.put(state[0], ta)
    return ta


def turn3(g, E, t):
    ps = g.ps.get()
    b = g.tmp.get()
    for i in range(3):
        tok = g.pe.op(lambda e, i=i: e.transpose(ps.ap[:, i * 128:(i + 1) * 128], E[:, i * 128:(i + 1) * 128],
                                                 g.C("ident", 0, 128)), *t, *ps.free)
    t1 = g.v_copy(b.ap[:, 0:384], ps.ap[:, 0:384], tok, *b.free)
    g.ps.put(ps, t1)
    return b, tok, t1


def pipelined(n, stages, step):
    last = len(stages) - 1
    for h in range(n + last):
        for i in range(last, -1, -1):
            if 0 <= h - i < n:
                stages[i](h - i)
        step()


def mix_first(g, lay, mod):
    fa, ra = g.fa, g.ra
    base = [g.pe.last(), g.act.last(), g.dve.last(), g.t_mod[lay]]

    def side(n):
        if lay == 0:
            a = 8 + sum(ADA_IN_MIX[:n])
            for j in range(a, a + ADA_IN_MIX[n]):
                modulation_tile(g, 0, j)

    lam_init = 0.8 - 0.6 * math.exp(-0.3 * lay)
    pl = g.small[:, 512:520]
    lc = PARAM_COLS["lam"] + lay * 4
    q = g.par[0:64, lc:lc + 4]
    tl = g.v_tt(pl[0:64, 0:1], q[:, 0:1], q[:, 1:2], ALU.mult, *base)
    tl = g.v_tt(pl[0:64, 1:2], q[:, 2:3], q[:, 3:4], ALU.mult, *base)
    ps = g.ps.get()
    tl = g.mm(ps.ap[:, 0:2], g.C("ones", 0, 128, 0, 64), pl[0:64, 0:2], after=[tl, *ps.free])
    tl = g.a_act(pl[:, 2:4], ps.ap[:, 0:2], ACT.Exp, tl, *base)
    g.ps.put(ps, tl)
    tl = g.v_tt(pl[:, 4:5], pl[:, 3:4], pl[:, 2:3], ALU.subtract, tl)
    tlam = g.v_ts(pl[:, 4:5], pl[:, 4:5], -lam_init, None, ALU.add, None, tl)
    nlam = pl[:, 4:5]

    per_k = modulated(g, "g_pre_mix", lay, mod, 0, 8, base)

    merged, Gb = fa[:, 0:2048], fa[:, 2048:4096]
    qT, kT, V = fa[:, 4096:5120], fa[:, 5120:6144], fa[:, 6144:7168]
    SCz, ya = fa[:, 7168:8200], fa[:, 8200:9224]
    cfu, cfv = fa[:, 9224:10368], fa[:, 10368:11392]
    cc, krb = fa[:, 2048:3328], fa[:, 3328:3584]
    Zh = [ra[:, i * 2048:i * 2048 + 1024] for i in range(3)]
    Zl = [ra[:, i * 2048 + 1024:i * 2048 + 2048] for i in range(3)]
    ch, cl = ra[:, 6144:7424], ra[:, 7424:8704]

    cu = cfu.rearrange("p (c t) -> p c t", c=4)
    tcu = []
    t0 = g.dve.op(lambda e: e.memset(cu[:, :, 0:30], 0.0), *per_k)
    for j in range(4):
        (ps, tok), = g.proj("w_in", lay * 34 + CF0 + j, 8, 256, g.hh, g.hl, [], per_k=per_k)
        b = g.tmp.get()
        t1, _ = sigmoid(g, b.ap[:, 0:T], ps.ap[:, T:2 * T], tok, *b.free)
        t2 = g.v_tt(cu[:, j, 30:286], ps.ap[:, 0:T], b.ap[:, 0:T], ALU.mult, tok, t1)
        g.ps.put(ps, t1, t2)
        g.tmp.put(b, t2)
        tcu.append(t2)
        side(j)

    def conv_steps():
        for j in range(4):
            o = cfv[:, j * T:(j + 1) * T]
            t = g.v_ts(o, cu[:, j, 0:256], g.P("cf_conv", lay * 124 + j), g.P("cf_conv_b", lay * 4 + j),
                       ALU.mult, ALU.add, tcu[j], t0)
            for n in range(1, 31):
                t = g.v_stt(o, cu[:, j, n:n + 256], g.P("cf_conv", lay * 124 + 4 * n + j), o,
                            ALU.mult, ALU.add, t)
                if n % 6 == 0:
                    yield
            g.cf_tok = t

    tq = []
    for j in range(4):
        (ps, tok), = g.proj("w_in", lay * 34 + DA0 + j, 8, 256, g.hh, g.hl, [])
        dst = (qT if j < 2 else kT)[:, (j % 2) * 512:(j % 2) * 512 + 512]
        t = g.a_act(dst, ps.ap[:, :], ACT.Copy, tok, *per_k)
        g.ps.put(ps, t)
        tq.append(t)
        side(4 + j)
    tv = []
    pv = [g.ps.get() for _ in range(2)]
    for j in range(2):
        w = g.weight("w_in", lay * 34 + DA0 + 4 + j)
        for tb in range(2):
            for k in range(8):
                xh = g.hh[:, k * T + tb * 128:k * T + tb * 128 + 128]
                xl = g.hl[:, k * T + tb * 128:k * T + tb * 128 + 128]
                wh, wl = w[0][:, k * 256:(k + 1) * 256], w[1][:, k * 256:(k + 1) * 256]
                tok = g.mm3(pv[tb].ap[:, j * 256:(j + 1) * 256], xh, xl, wh, wl, k == 0, k == 7, inc=k == 7,
                            after=[w[2], *pv[tb].free])
        g.done(w, tok)
        side(8 + j)
    for tb in range(2):
        t = g.a_act(V[:, tb * 512:(tb + 1) * 512], pv[tb].ap[:, :], ACT.Copy, tok)
        g.ps.put(pv[tb], t)
        tv.append(t)

    conv = conv_steps()

    st = {}

    def sc_proj():
        z = SCz.rearrange("p (c t) -> p c t", c=4)
        st["z0"] = g.dve.op(lambda e: e.memset(z[:, :, 0:2], 0.0), *per_k)
        for j in range(4):
            (ps, tok), = g.proj("w_in", lay * 34 + SCU0 + j, 8, 256, g.hh, g.hl, [])
            b = g.tmp.get()
            t = g.a_act(b.ap[:, 0:T], ps.ap[:, 0:T], ACT.Copy, tok, *b.free)
            t = g.v_tt(z[:, j, 2:258], ps.ap[:, T:2 * T], b.ap[:, 0:T], ALU.mult, tok, t)
            g.ps.put(ps, t)
            g.tmp.put(b, t)
            st["z"] = t
            yield
        for j in range(2):
            (ps, tok), = g.proj("w_in", lay * 34 + SCB0 + j, 8, 256, g.hh, g.hl, [])
            for i in range(2):
                c = 2 * j + i
                b = g.tmp.get()
                t = conv3(g, b.ap[:, 0:T], z[:, c, :], "sc_conv", lay * 12 + c, 4, [st["z0"], st["z"], *b.free])
                t = g.v_tt(b.ap[:, 0:T], b.ap[:, 0:T], ps.ap[:, i * T:(i + 1) * T], ALU.mult, tok, t)
                t1, t2 = g.split_act(g.xk(Zh[0], c), g.xk(Zl[0], c), b.ap[:, 0:T], t)
                g.tmp.put(b, t1, t2)
            g.ps.put(ps, t)
            st["yc"] = t2
            yield

    def mla_proj():
        for j in range(2):
            (ps, tok), = g.proj("w_in", lay * 34 + MLA0 + j, 8, 256, g.hh, g.hl, [])
            t = g.v_copy(cc[:, j * 512:(j + 1) * 512], ps.ap[:, :], tok, *per_k)
            g.ps.put(ps, t)
            yield
        w = g.weight("w_mc", lay)
        ps = g.ps.get()
        tok = g.group(w, 8, 160, g.hh, g.hl, 0, ps.ap[:, 0:T], ps.free)
        tok = g.group(w, 8, 160, g.hh, g.hl, 64, ps.ap[0:96, T:2 * T], [], m=96)
        g.done(w, tok)
        t = g.v_copy(cc[:, 1024:1280], ps.ap[:, 0:T], tok)
        kr = st["kr"] = krb
        t2 = g.v_copy(kr[0:96, 0:T], ps.ap[0:96, T:2 * T], tok, *per_k)
        g.ps.put(ps, t2)
        st["cc"], st["krt"] = t, t2
        yield

    def merge(branch, z, wo, tz, gate_saved=None):
        zh, zl = z
        for n in range(2):
            held = g.weight(wo, lay * 2 + n)
            for i in range(2):
                pair = 2 * n + i
                dst = merged[:, pair * 512:(pair + 1) * 512]
                ps = g.ps.get()
                for c in range(2):
                    tok = g.group(held, 4, 512, zh, zl, i * 256 + c * 128, ps.ap[:, c * T:(c + 1) * T],
                                  [*ps.free, *tz])
                if i == 1:
                    g.done(held, tok)
                if gate_saved is None:
                    (pg, tg), = g.proj("w_in", lay * 34 + GATE0 + branch * 4 + pair, 8, 256, g.hh, g.hl, [])
                    b = g.tmp.get()
                    ts, tr_ = sigmoid(g, b.ap[:, :], pg.ap[:, :], tg, *b.free)
                    g.ps.put(pg, tr_)
                    sg = b.ap[:, :]
                else:
                    b, sg, ts = None, gate_saved[0][:, pair * 512:(pair + 1) * 512], gate_saved[1]
                if branch == 2:
                    t = g.v_tt(dst, ps.ap[:, :], sg, ALU.mult, tok, ts, *per_k)
                    st[("merged", pair)] = t
                    if b:
                        g.tmp.put(b, t)
                else:
                    o = g.tmp.get()
                    t = g.v_tt(o.ap[:, :], ps.ap[:, :], sg, ALU.mult, tok, ts, *o.free)
                    t2 = g.v_tt(dst, dst, o.ap[:, :], ALU.add, t, st[("merged", pair)])
                    st[("merged", pair)] = t2
                    g.tmp.put(o, t2)
                    if b:
                        g.tmp.put(b, t)
                g.ps.put(ps, t)
                yield

    def gates_b():
        for j in range(4):
            (pg, tg), = g.proj("w_in", lay * 34 + GATE0 + 4 + j, 8, 256, g.hh, g.hl, [])
            st["gb"], tr_ = sigmoid(g, Gb[:, j * 512:(j + 1) * 512], pg.ap[:, :], tg, *per_k)
            g.ps.put(pg, tr_)
            yield

    def chain(*gens):
        for x in gens:
            yield from (x() if callable(x) else x)

    def fill(*its):
        def step(n=1):
            for _ in range(n):
                for it in its:
                    next(it, None)
        return step

    def drain(it):
        for _ in it:
            pass

    work = chain(sc_proj, lambda: merge(2, (Zh[0], Zl[0]), "sc_w_o", [st["yc"]]), mla_proj)
    step = fill(conv, work)
    tya, held = [], {}

    def da_scores(h):
        hs = []
        for m in range(2):
            ps = g.ps.get()
            p0 = 64 * m
            tok = g.mm(ps.ap[:, 0:128], qT[p0:p0 + 64, h * T:h * T + 128], kT[p0:p0 + 64, h * T:h * T + 128],
                       after=[*tq, *ps.free], inc=False)
            tok = g.mm(ps.ap[:, 128:384], qT[p0:p0 + 64, h * T + 128:h * T + 256], kT[p0:p0 + 64, h * T:h * T + 256])
            u = (g.tmp if m else g.sring).get()
            hs.append((u, softmax3(g, u, tok, ps, g.C("mask3", 0, 384), 0.125)))
        held[h] = hs

    def da_combine(h):
        (u1, st1), (u2, st2) = held[h]
        s1, s2 = u1.ap, u2.ap
        r1, t1 = softmax3_end(g, st1)
        r2, t2 = softmax3_end(g, st2)
        t2 = g.v_ts(r2, r2, nlam, None, ALU.mult, None, t2, tlam)
        for a, n, i in ((0, 128, 0), (128, 256, 1)):
            ta = g.v_ts(s1[:, a:a + n], s1[:, a:a + n], r1[:, i:i + 1], None, ALU.mult, None, t1)
            ta = g.v_stt(s1[:, a:a + n], s2[:, a:a + n], r2[:, i:i + 1], s1[:, a:a + n], ALU.mult, ALU.add, ta, t2)
        g.cols.put(st1[0], ta)
        g.cols.put(st2[0], ta)
        g.tmp.put(u2, ta)
        held[h] = (u1, ta)

    def turn(h):
        u, ta = held[h]
        pt, tE, tpt = turn3(g, u.ap, [ta])
        g.sring.put(u, tE)
        held[h] = (pt, tpt)

    def da_values(h):
        pt, tpt = held.pop(h)
        ps = g.ps.get()
        g.mm(ps.ap[:, 0:256], V[:, h * 128:(h + 1) * 128], pt.ap[:, 0:256], last=False, after=[tpt, *tv, *ps.free],
             inc=False)
        tok = g.mm(ps.ap[:, 128:256], V[:, 512 + h * 128:512 + (h + 1) * 128], pt.ap[:, 256:384], first=False)
        g.tmp.put(pt, tok)
        t = g.a_act(ya[:, h * T:(h + 1) * T], ps.ap[:, 0:T], ACT.Copy, tok, *per_k)
        g.ps.put(ps, t)
        tya.append(t)

    pipelined(4, [da_scores, da_combine, turn, da_values], lambda: step(2))
    drain(work)
    drain(conv)

    def head_norm(src, n, gcol, gstep, eps, dim, extra, zh, zl, ones, after):
        for h in range(n):
            sq = g.tmp.get()
            s = src[:, h * T:(h + 1) * T]
            t = g.a_act(sq.ap[:, 0:T], s, ACT.Square, *after, *sq.free)
            ps = g.ps.get()
            t = g.mm(ps.ap[:, 0:T], ones, sq.ap[:, 0:T], after=[t, *ps.free])
            t = g.v_ts(sq.ap[:, T:2 * T], ps.ap[:, 0:T], 1.0 / dim, eps, ALU.mult, ALU.add, t)
            g.ps.put(ps, t)
            t = g.rsqrt(sq.ap[:, 0:T], sq.ap[:, T:2 * T], t)
            if extra is not None:
                t = g.v_ts(s, s, extra, None, ALU.mult, None, t)
            t = g.v_stt(s, s, gcol(h), sq.ap[:, 0:T], ALU.mult, ALU.mult, t)
            g.tmp.put(sq, t)
            t1, t2 = g.split_act(g.xk(zh, h), g.xk(zl, h), s, t)
        return [t1, t2]

    tza = head_norm(ya, 4, lambda h: g.P("da_g_subln", lay), 0, 1e-6, 128, 1.0 - lam_init, Zh[1], Zl[1],
                    g.C("ones", 0, 128), tya)

    v_, r_ = g.small[:, 0:256], g.small[:, 256:512]
    sqb = g.attn[:, 0:768]
    tz = []
    for a, n, dim, gn, gl in ((0, 3, 384, "mla_g_cq", 3), (3, 2, 256, "mla_g_ckv", 2)):
        src = cc[:, a * T:(a + n) * T]
        t1, _ = g.stats(src, n, dim, 1e-6, r_, v_, sqb, [st["cc"], g.dve.last(), g.pe.last(), g.act.last()])
        for k in range(n):
            s = cc[:, (a + k) * T:(a + k + 1) * T]
            t2 = g.v_stt(s, s, g.P(gn, lay * gl + k), r_, ALU.mult, ALU.mult, t1)
            _, t3 = g.split_act(g.xk(ch, a + k), g.xk(cl, a + k), s, t2, *per_k)
            tz.append(t3)
    mq, mk, mv = fa[:, 4096:6144], fa[:, 7168:9216], fa[:, 6144:7168]
    free = [g.pe.last(), g.dve.last(), g.act.last()]
    tmq = []
    cos, sin = g.trig[64:96, 0:256], g.trig[64:96, 256:512]

    def rope(dst, n, t, free):
        ps = g.ps.get()
        for i in range(n):
            tok = g.mm(ps.ap[0:96, i * T:(i + 1) * T], g.C("rot", 0, 96, 0, 96), dst[0:96, i * T:(i + 1) * T],
                       after=[t, *ps.free])
        b = g.tmp.get()
        o = b.ap[64:96, 0:n * T]
        d = dst[64:96, 0:n * T]
        cs, sn = (cos, sin) if n == 1 else (bc2(cos), bc2(sin))
        f = (lambda a: a) if n == 1 else v2
        t1 = g.v_tt(f(o), f(ps.ap[64:96, 0:n * T]), sn, ALU.mult, tok, *b.free, *g.trig_tok)
        g.ps.put(ps, t1)
        t2 = g.v_tt(f(d), f(d), cs, ALU.mult, tok)
        t3 = g.v_tt(d, d, o, ALU.add, t1, t2)
        g.tmp.put(b, t3)
        return t3

    for n in range(2):
        w = g.weight("mla_w_uq", lay * 2 + n)
        for i in range(2):
            ps = g.ps.get()
            for c in range(2):
                tok = g.group(w, 3, 384, ch, cl, (2 * i + c) * 96, ps.ap[0:96, c * T:(c + 1) * T],
                              [*ps.free, *tz], m=96)
            h = 4 * n + 2 * i
            t = g.a_act(mq[0:96, h * T:(h + 2) * T], ps.ap[0:96, :], ACT.Copy, tok, *free)
            g.ps.put(ps, t)
            tmq.append(rope(mq[:, h * T:(h + 2) * T], 2, t, free))
        g.done(w, tok)
    w = g.weight("mla_w_ukv", lay)
    c0h, c0l = ch[:, 3 * T:5 * T], cl[:, 3 * T:5 * T]
    tmk = []
    for i in range(4):
        ps = g.ps.get()
        for c in range(2):
            tok = g.group(w, 2, 1024, c0h, c0l, (2 * i + c) * 128, ps.ap[:, c * T:(c + 1) * T], ps.free)
        t = g.a_act(mk[0:64, 2 * i * T:(2 * i + 2) * T], ps.ap[0:64, :], ACT.Copy, tok, *free)
        g.ps.put(ps, t)
        tmk.append(t)
    tmv = []
    for tb in range(2):
        ps = g.ps.get()
        for k in range(2):
            xh, xl = [c0[:, k * T + tb * 128:k * T + tb * 128 + 128] for c0 in (c0h, c0l)]
            wh, wl = [a[:, k * 1024:(k + 1) * 1024].rearrange("p (h c) -> p h c", h=8)[:, :, 64:128] for a in (w[0], w[1])]
            tok = g.mm3(ps.ap[:, :].rearrange("p (h c) -> p h c", h=8), xh, xl, wh, wl, k == 0, k == 1, inc=k == 1,
                        after=ps.free)
        t = g.a_act(mv[:, tb * 512:(tb + 1) * 512], ps.ap[:, :], ACT.Copy, tok, *free)
        g.ps.put(ps, t)
        tmv.append(t)
    g.done(w, tok)
    kr = st["kr"]
    t = rope(kr, 1, st["krt"], [])
    for h in range(8):
        tkr = g.v_copy(mk[64:96, h * T:(h + 1) * T], kr[64:96, 0:T], t, *free)

    def cf_finish():
        sm, ve = g.small[:, 0:256], g.small[:, 256:512]
        b = g.tmp.get()
        t = g.dve.op(lambda e: e.tensor_reduce(b.ap[:, 0:T], cfv.rearrange("p (c t) -> p t c", c=4), AX, ALU.add),
                     g.cf_tok, *b.free)
        ps = g.ps.get()
        t = g.mm(ps.ap[:, 0:T], g.C("ones", 0, 128), b.ap[:, 0:T], after=[t, *ps.free])
        g.tmp.put(b, t)
        t = g.v_ts(sm, ps.ap[:, 0:T], 1.0 / 512, None, ALU.mult, None, t, g.act.last())
        g.ps.put(ps, t)
        for j in range(4):
            o = cfv[:, j * T:(j + 1) * T]
            t1 = g.v_tt(o, o, sm, ALU.subtract, t)
        yield
        t2, _ = g.stats(cfv, 4, 512, 1e-5, sm, ve, cfu, [t1, g.dve.last()])
        for j in range(4):
            o = cfv[:, j * T:(j + 1) * T]
            t3 = g.v_tt(o, o, sm, ALU.mult, t2)
            t3 = g.v_ts(o, o, g.P("cf_ln_g", lay * 4 + j), g.P("cf_ln_b", lay * 4 + j), ALU.mult, ALU.add, t3)
            t3 = exp_silu(g, o, o, cfu[:, 0:T], [t3])
            _, t4 = g.split_act(g.xk(Zh[2], j), g.xk(Zl[2], j), o, t3, *per_k)
        st["cf"] = t4
        yield

    work = chain(cf_finish, gates_b, lambda: merge(0, (Zh[1], Zl[1]), "da_w_o", tza),
                 lambda: merge(3, (Zh[2], Zl[2]), "cf_w_o", [st["cf"]]))
    step = fill(work)
    tyb = []
    sc = 96 ** -0.5
    trn = [g.pe.last(), g.dve.last()]
    for u in g.sring.bufs:
        u.free = trn
    po = {}

    def mla_scores(h):
        ps = g.ps.get()
        g.mm(ps.ap[:, 0:128], mq[0:96, h * T:h * T + 128], mk[0:96, h * T:h * T + 128],
             after=[*tmq, *tmk, tkr, *ps.free], inc=False)
        tok = g.mm(ps.ap[:, 128:384], mq[0:96, h * T + 128:(h + 1) * T], mk[0:96, h * T:(h + 1) * T])
        u = g.sring.get()
        held[h] = (u, softmax3(g, u, tok, ps, g.C("mask3", 0, 384), sc))

    def scale(h):
        u, state = held[h]
        held[h] = (u, softmax3_scale(g, u, state))

    def mla_values(h):
        pt, tpt = held.pop(h)
        p0 = 64 * (h % 2)
        if h % 2 == 0:
            po[0] = g.ps.get()
        o = po[0]
        g.mm(o.ap[p0:p0 + 64, 0:256], mv[:, h * 64:(h + 1) * 64], pt.ap[:, 0:256], last=False,
             after=[tpt, *tmv, *o.free], inc=False)
        tok = g.mm(o.ap[p0:p0 + 64, 128:256], mv[:, 512 + h * 64:512 + (h + 1) * 64], pt.ap[:, 256:384], first=False)
        g.tmp.put(pt, tok)
        if h % 2:
            c = h // 2
            b = g.tmp.get()
            t = g.a_act(b.ap[:, 0:T], o.ap[:, 0:T], ACT.Copy, tok, *b.free)
            g.ps.put(o, t)
            t1, t2 = g.split_act(g.xk(Zh[0], c), g.xk(Zl[0], c), b.ap[:, 0:T], t, *trn)
            g.tmp.put(b, t1, t2)
            tyb.extend([t1, t2])

    pipelined(8, [mla_scores, scale, turn, mla_values], step)
    drain(work)
    drain(merge(1, (Zh[0], Zl[0]), "mla_w_o", tyb, gate_saved=(Gb, st["gb"])))

    tm = []
    for k in range(8):
        _, t = g.split_act(g.xk(g.hh, k), g.xk(g.hl, k), g.xk(merged, k), st[("merged", k // 2)], g.pe.last())
        tm.append(t)
    y = fa[:, 4096:6144]
    ty = []
    for j in range(4):
        (ps, tok), = g.proj("w_mix_out", lay * 4 + j, 8, 256, g.hh, g.hl, [], per_k=tm)
        t = g.v_copy(y[:, j * 512:(j + 1) * 512], ps.ap[:, :], tok, g.pe.last())
        g.ps.put(ps, t)
        ty.append(t)
    return add_normed(g, y, lay, "g_post_mix", mod, 16, ty)


def tables(g, t0):
    pi = g.tmp.get()
    raw = pi.ap[64:96, 0:T].bitcast(I32)
    g.sp.dma(lambda e: e.dma_start(raw, g.args["positions"].broadcast_to([32, T])), g.s_p[0])
    g.n_p += 1
    p = pi.ap[64:96, T:2 * T]
    t = g.v_copy(p, raw, (g.s_p[0], 16))
    t = g.v_ts(p, p, g.C("inv", 0, 1, 64, 96), None, ALU.mult, None, t, t0)
    b = g.tmp.get()
    n, z = b.ap[64:96, 0:T], b.ap[64:96, T:2 * T]
    big = 12582912.0
    c1 = 6.28125
    c2 = float(np.float32(TWO_PI - c1))
    c3 = float(TWO_PI - c1 - float(np.float32(TWO_PI - c1)))
    for i, shift in ((0, 0.25), (1, 0.0)):
        t = g.v_ts(n, p, 1.0 / TWO_PI, shift, ALU.mult, ALU.add, t)
        t = g.v_ts(n, n, big, None, ALU.add, None, t)
        t = g.v_ts(n, n, big, None, ALU.subtract, None, t)
        t = g.v_stt(z, n, -c1, p, ALU.mult, ALU.add, t)
        t = g.v_stt(z, n, -c2, z, ALU.mult, ALU.add, t)
        t = g.v_stt(z, n, -c3, z, ALU.mult, ALU.add, t)
        if i == 0:
            t = g.v_ts(z, z, math.pi / 2, None, ALU.add, None, t)
        t = g.v_ts(z, z, 3.1415925, -3.1415925, ALU.min, ALU.max, t)
        t = g.a_act(g.trig[64:96, i * T:(i + 1) * T], z, ACT.Sin, t)
    g.tmp.put(pi, t)
    g.tmp.put(b, t)
    g.trig_tok = [t]


def second_norm(g, layer, which, after):
    v, r = g.small[:, 0:256], g.small[:, 256:512]
    per_k = g.split_gain("norm_gains", (layer * 4 + which) * 8, 8, g.x, after, [g.pe.last()])
    sq = g.fa[:, 13056:15104]
    _, finish = g.stats_later(g.x[:, :], 8, D, 1e-6, r, v, sq, [*after, g.pe.last(), g.act.last(), g.dve.last()])
    return per_k, r, Later(finish)


def second_ffn(g, layer, half, tx):
    per_k, r, tr = second_norm(g, layer, 2 * half, [tx])

    def chunk(j, ps, tok, yh, yl, free):
        tr.get()
        a = g.tmp.get()
        t = g.v_tt(v2(a.ap[:, :]), v2(ps.ap[:, :]), bc2(r), ALU.mult, tok, tr.get(), *a.free)
        g.ps.put(ps, t)
        b = g.tmp.get()
        t1 = g.a_act(b.ap[:, 0:T], a.ap[:, 0:T], ACT.Silu, t, *b.free)
        t2 = g.v_tt(b.ap[:, T:2 * T], b.ap[:, 0:T], a.ap[:, T:2 * T], ALU.mult, t1)
        g.tmp.put(a, t2)
        t3, t4 = g.split_act(yh, yl, b.ap[:, T:2 * T], t2, *free)
        g.tmp.put(b, t3, t4)
        return t4

    i = layer * 2 + half
    acc = ffn(g, "w_gu", i * 22, "w_dn", i * 11, per_k, chunk)
    la = g.act.last()
    for n, b in enumerate(acc):
        s = g.x[:, n * 512:(n + 1) * 512]
        t = g.v_stt(s, b.ap[:, :], 0.5, s, ALU.mult, ALU.add, b.ready, la)
        g.ps.put(b, t)
    return t


def out_add(g, name, n0, zh, zl, tz):
    la = g.act.last()
    for j in range(4):
        (ps, tok), = g.proj(name, n0 + j, 8, 256, zh, zl, [], per_k=tz)
        s = g.x[:, j * 512:(j + 1) * 512]
        t = g.v_tt(s, s, ps.ap[:, :], ALU.add, tok, la)
        g.ps.put(ps, t)
    return t


def evac_scaled(g, out, ps, tok, r, tr, *after):
    t = g.v_tt(v2(out), v2(ps.ap[:, :]), bc2(r), ALU.mult, tok, tr.get(), *after)
    g.ps.put(ps, t)
    return t


def token_factor(g, r, tr):
    rc = g.small[:, 520:522]
    ps = g.ps.get()
    for tb in range(2):
        tok = g.pe.op(lambda e, tb=tb: e.transpose(ps.ap[:, tb * 128:(tb + 1) * 128], r[:, tb * 128:(tb + 1) * 128],
                                                   g.C("ident", 0, 128)), tr.get(), *ps.free)
    for tb in range(2):
        t = g.v_copy(rc[:, tb:tb + 1], ps.ap[:, tb * 128:tb * 128 + 1], tok)
    g.ps.put(ps, t)
    return rc, t


def token_major(g, name, ns, width, j0, banks, per_k):
    for j, n in enumerate(ns, j0):
        w = g.weight(name, n)
        for tb in range(2):
            ps = banks[tb]
            for k in range(8):
                a = k * T + tb * 128
                tok = g.mm3(ps.ap[:, j * width:(j + 1) * width], g.hh[:, a:a + 128], g.hl[:, a:a + 128],
                            w[0][:, k * width:(k + 1) * width], w[1][:, k * width:(k + 1) * width],
                            k == 0, k == 7, inc=k == 7, after=[w[2], *ps.free, per_k[k]])
        g.done(w, tok)
    return tok


def hgrn(g, layer, j, tx):
    per_k, r, tr = second_norm(g, layer, 1, [tx])
    fa = g.fa
    G = [None, None]
    G[0] = [fa[:, 0:1024], fa[:, 1024:2048], fa[:, 2048:3072], fa[:, 3072:4096]]
    G[1] = [fa[:, 4096:5120], fa[:, 5120:6144], fa[:, 6144:7168], fa[:, 7168:8192]]
    Qa, Ka = fa[:, 8192:9216], fa[:, 9216:10240]
    DD = [fa[:, 10240:11264], g.attn[:, 128:1152]]
    AT = fa[:, 11264:12800]
    A32 = fa[:, 12800:13056]
    o = fa[:, 13056:15104]
    base = [g.pe.last(), g.act.last(), g.dve.last()]
    L = g.attn[:, 0:96]
    lb, oml, zf = L[:, 64:72], L[:, 72:80], L[:, 80:88]
    if layer == 0:
        tl = g.dve.op(lambda e: e.memset(lb, 0.0), *base)
        tl = g.dve.op(lambda e: e.memset(oml, 1.0), *base)
        tl = g.dve.op(lambda e: e.memset(zf, 1.0), *base)
    else:
        c = PARAM_COLS["hg_lb"]
        raw = g.par[:, c:c + 32]
        mx, s = L[:, 88:96], L[:, 32:40]
        t = g.dve.op(lambda e: e.tensor_reduce(mx, raw.rearrange("p (l c) -> p c l", l=4), AX, ALU.max), *base)
        t = g.v_tt(L[:, 0:32].rearrange("p (l c) -> p l c", l=4), raw.rearrange("p (l c) -> p l c", l=4),
                   mx.unsqueeze(1).broadcast_to([128, 4, 8]), ALU.subtract, t)
        t = g.a_act(L[:, 0:32], L[:, 0:32], ACT.Exp, t)
        t = g.v_tt(s, L[:, 8:16], L[:, 16:24], ALU.add, t)
        t = g.v_tt(s, s, L[:, 24:32], ALU.add, t) if layer == 3 else t
        t = g.v_tt(L[:, 40:48], s, L[:, 0:8], ALU.add, t)
        t = g.dve.op(lambda e: e.reciprocal(L[:, 48:56], L[:, 40:48]), t)
        t = g.v_tt(lb, s, L[:, 48:56], ALU.mult, t)
        t = g.v_tt(oml, L[:, 0:8], L[:, 48:56], ALU.mult, t)
        tl = g.v_ts(zf, lb, 2.0 ** -60, None, ALU.is_lt, None, t)
    t_at = g.pool.op(lambda e: e.memset(AT, 0.0), *base)
    AT4 = AT.rearrange("p (h c) -> p h c", h=4)
    st = [{}, {}]
    tO = []

    def project(gr):
        q, k, b, V = G[gr]
        x = st[gr]
        x["q"], x["b"], x["v"] = [], [], []
        for n in range(2):
            (ps, tok), = g.proj("hg_in", j * 16 + gr * 2 + n, 8, 256, g.hh, g.hl, [], per_k=per_k)
            a = g.tmp.get()
            t = evac_scaled(g, a.ap[:, :], ps, tok, r, tr, *a.free)
            u = g.tmp.get()
            t = exp_silu(g, q[:, n * 512:(n + 1) * 512], a.ap[:, :], u.ap[:, :], [t, *u.free, *base])
            g.tmp.put(a, t)
            g.tmp.put(u, t)
            x["q"].append(t)
            yield
        for n in range(2):
            (ps, tok), = g.proj("hg_in", j * 16 + 4 + gr * 2 + n, 8, 256, g.hh, g.hl, [])
            f = g.tmp.get()
            t = evac_scaled(g, f.ap[:, :], ps, tok, r, tr, *f.free)
            e_ = g.tmp.get()
            tc = g.v_ts(e_.ap[:, :], f.ap[:, :], -80.0, None, ALU.max, None, t, *e_.free)
            t = g.a_act(e_.ap[:, :], e_.ap[:, :], ACT.Exp, tc, scale=-1.0)
            tf = g.v_ts(f.ap[:, :], f.ap[:, :], 60 * math.log(2.0), 0.0, ALU.add, ALU.min, tc)
            s = g.tmp.get()
            ts = g.v_ts(s.ap[:, :], e_.ap[:, :], 1.0, None, ALU.add, None, t, *s.free)
            ts = g.dve.op(lambda e, s=s: e.reciprocal(s.ap[:, :], s.ap[:, :]), ts)
            for c in range(2):
                hd = gr * 4 + n * 2 + c
                w = slice(c * T, (c + 1) * T)
                kk = k[:, (2 * n + c) * T:(2 * n + c + 1) * T]
                t = g.v_stt(kk, e_.ap[:, w], oml[:, hd:hd + 1], s.ap[:, w], ALU.mult, ALU.mult, ts, tl, *base)
                tu = g.v_ts(s.ap[:, w], s.ap[:, w], oml[:, hd:hd + 1], lb[:, hd:hd + 1], ALU.mult, ALU.add, t)
            tu = g.v_ts(s.ap[:, :], s.ap[:, :], 2.0 ** -60, None, ALU.max, None, tu)
            tu = g.a_act(s.ap[:, :], s.ap[:, :], ACT.Ln, tu)
            for c in range(2):
                hd = gr * 4 + n * 2 + c
                w = slice(c * T, (c + 1) * T)
                tw = g.v_stt(f.ap[:, w], f.ap[:, w], zf[:, hd:hd + 1], s.ap[:, w], ALU.mult, ALU.add, tu, tf)
                bb = b[:, (2 * n + c) * T:(2 * n + c + 1) * T]
                tw = g.dve.op(lambda e, bb=bb, ff=f.ap[:, w]: e.tensor_tensor_scan(
                    bb, g.C("rst", 0, 256), ff, 0.0, ALU.mult, ALU.add), tw, *base)
            for x_ in (f, e_, s):
                g.tmp.put(x_, tw, t)
            x["b"].append(tw)
            x["k"] = t
            yield
        rc, trc = token_factor(g, r, tr) if gr == 0 else st[0]["rc"]
        x["rc"] = (rc, trc)
        banks = [g.ps.get() for _ in range(2)]
        for n in range(2):
            tok = token_major(g, "hg_in", [j * 16 + 8 + gr * 2 + n], 256, n, banks, per_k)
            if n == 0:
                yield
        for tb in range(2):
            t = g.v_ts(V[:, tb * 512:(tb + 1) * 512], banks[tb].ap[:, :], rc[:, tb:tb + 1], None, ALU.mult, None,
                       tok, trc, *base)
            g.ps.put(banks[tb], t)
            x["v"].append(t)
        yield

    def v3(a, n):
        return a.rearrange("p (n m) -> p n m", m=n)

    def scan(gr):
        nonlocal t_at
        q, k, b, V = G[gr]
        x = st[gr]
        tb_, tq = x["b"], x["q"]
        free = [g.pe.last(), g.act.last(), g.dve.last()]
        b64 = v3(b, 64)
        last = b64[:, :, 63:64].broadcast_to([128, 16, 64])
        t = g.a_act(Qa, b, ACT.Exp, *tb_, *free)
        tQ = g.v_tt(Qa, Qa, q, ALU.mult, t, *tq)
        t = g.p_tt(v3(Ka, 64), last, b64, ALU.subtract, *free, *tb_)
        t = g.a_act(Ka, Ka, ACT.Exp, t)
        tK = g.p_tt(Ka, Ka, k, ALU.mult, t, x["k"])
        eb = g.cols.get()
        tE = g.a_act(eb.ap[:, 0:16].unsqueeze(2), b64[:, :, 63:64], ACT.Exp, *tb_, *eb.free)
        levels = (32, 16, 8, 4, 2, 1, 0)
        made = {}
        dfree = [list(free), list(free)]

        def make(lv):
            m = levels[lv]
            if m == 0:
                made[lv] = (k, q, [x["k"], *tq])
                return
            Dv = DD[lv % 2]
            b3, d3, qq, kk = v3(b, 2 * m), v3(Dv, 2 * m), v3(q, 2 * m), v3(k, 2 * m)
            n = 1024 // (2 * m)
            ref = b3[:, :, m - 1:m].broadcast_to([128, n, m])
            t1 = g.v_tt(d3[:, :, m:2 * m], b3[:, :, m:2 * m], ref, ALU.subtract, *dfree[lv % 2], *tb_)
            t2 = g.p_tt(d3[:, :, 0:m], ref, b3[:, :, 0:m], ALU.subtract, *dfree[lv % 2], *tb_)
            t = g.a_act(Dv, Dv, ACT.Exp, t1, t2)
            made[lv] = (Dv, d3, qq, kk, m, t)

        def finish_make(lv):
            if levels[lv] == 0:
                return
            Dv, d3, qq, kk, m, t = made[lv]
            t1 = g.v_tt(d3[:, :, m:2 * m], d3[:, :, m:2 * m], qq[:, :, m:2 * m], ALU.mult, t)
            t2 = g.p_tt(d3[:, :, 0:m], d3[:, :, 0:m], kk[:, :, 0:m], ALU.mult, t)
            made[lv] = (Dv, Dv, [t1, t2])

        make(0)
        make(1)
        yield
        ps = g.ps.get()
        for h in range(4):
            for sb in range(2):
                a = h * T + sb * 128
                tok = g.mm(ps.ap[0:64, h * 128 + sb * 64:h * 128 + sb * 64 + 64], Ka[:, a:a + 64], Qa[:, a + 64:a + 128],
                           after=[tQ, tK, *ps.free], inc=h == 3)
        tA = []
        for sb in range(2):
            t = g.a_act(AT4[0:64, :, sb * 256 + 64:sb * 256 + 128],
                        ps.ap[0:64, :].rearrange("p (h s t) -> p h s t", h=4, s=2)[:, :, sb, :], ACT.Copy, tok, t_at)
            tA.append(t)
        g.ps.put(ps, t)
        q3 = v3(Qa, 64).rearrange("p (h c) m -> p h c m", c=4)
        k3 = v3(Ka, 64).rearrange("p (h c) m -> p h c m", c=4)
        e4 = eb.ap[:, 0:16].rearrange("p (h c) -> p h c", c=4)
        t1 = g.v_tt(q3[:, :, 3, :], q3[:, :, 3, :], e4[:, :, 2:3].broadcast_to([128, 4, 64]), ALU.mult, tok, tE)
        t2 = g.v_tt(k3[:, :, 0, :], k3[:, :, 0, :], e4[:, :, 1:2].broadcast_to([128, 4, 64]), ALU.mult, tok, tE)
        g.cols.put(eb, t2)
        finish_make(0)
        yield
        ps = g.ps.get()
        for h in range(4):
            tok = g.mm(ps.ap[:, h * 128:(h + 1) * 128], Ka[:, h * T:h * T + 128], Qa[:, h * T + 128:h * T + 256],
                       after=[t1, t2, *ps.free], inc=h == 3)
        t = g.a_act(AT4[:, :, 128:256], ps.ap[:, :].rearrange("p (h t) -> p h t", h=4), ACT.Copy, tok, t_at)
        tA.append(t)
        g.ps.put(ps, t)
        tacc = None
        for lv, m in enumerate(levels):
            lhs, rhs, ready = made.pop(lv)
            ps = g.ps.get()
            if m == 32:
                for h in range(4):
                    for c in range(4):
                        a = h * T + c * 64
                        p0 = 64 * (c % 2)
                        col = h * 64 + (c // 2) * 32
                        tok = g.mm(ps.ap[p0:p0 + 32, col:col + 32], lhs[:, a:a + 32], rhs[:, a + 32:a + 64],
                                   after=[*ready, *ps.free], inc=h == 3 and c == 3)
            else:
                for h in range(4):
                    for jb in range(8):
                        a = h * T + jb * 32
                        p0 = 32 * (jb % 4)
                        col = h * 64 + (jb // 4) * 32
                        tok = g.mm(ps.ap[p0:p0 + 32, col:col + 32], lhs[:, a:a + 32], rhs[:, a:a + 32],
                                   after=[*ready, *ps.free], inc=h == 3 and jb == 7)
            dfree[lv % 2] = [tok]
            if lv + 1 < len(levels):
                finish_make(lv + 1)
            if lv + 2 < len(levels):
                make(lv + 2)
            if m == 32:
                for c in range(2):
                    p0 = 64 * c
                    for sb in range(2):
                        t = g.a_act(AT4[p0:p0 + 32, :, sb * 256 + p0 + 32:sb * 256 + p0 + 64],
                                    ps.ap[p0:p0 + 32, 0:256].rearrange("p (h s t) -> p h s t", h=4, s=2)[:, :, sb, :],
                                    ACT.Copy, tok, t_at)
                        tA.append(t)
                g.ps.put(ps, t)
            else:
                mask = g.C("lev", (lv - 1) * 32, 32).unsqueeze(1).broadcast_to([128, 8, 32])
                pv = ps.ap[:, 0:256].rearrange("p (n t) -> p n t", t=32)
                av = A32.rearrange("p (n t) -> p n t", t=32)
                if lv == 1:
                    tacc = g.v_tt(av, pv, mask, ALU.mult, tok, *tA, *free)
                    g.ps.put(ps, tacc)
                else:
                    a = g.tmp.get()
                    t = g.v_tt(a.ap[:, 0:256].rearrange("p (n t) -> p n t", t=32), pv, mask, ALU.mult, tok, *a.free)
                    g.ps.put(ps, t)
                    tacc = g.v_tt(A32, A32, a.ap[:, 0:256], ALU.add, t, tacc)
                    g.tmp.put(a, tacc)
            yield
        for c in range(4):
            p0 = 32 * c
            for sb in range(2):
                t = g.a_act(AT4[p0:p0 + 32, :, sb * 256 + p0:sb * 256 + p0 + 32],
                            A32[p0:p0 + 32, :].rearrange("p (h s t) -> p h s t", h=4, s=2)[:, :, sb, :],
                            ACT.Copy, tacc, t_at)
        tA.append(t)
        yield
        for hp in range(2):
            ps = g.ps.get()
            for c in range(2):
                h = 2 * hp + c
                g.mm(ps.ap[:, c * T:c * T + 256], V[:, h * 128:(h + 1) * 128], AT4[:, h, 0:256], last=False,
                     after=[*tA, *x["v"], *ps.free], inc=False)
                tok = g.mm(ps.ap[:, c * T + 128:c * T + 256], V[:, 512 + h * 128:512 + (h + 1) * 128],
                           AT4[:, h, 256:384], first=False)
            hh = gr * 4 + 2 * hp
            t = g.v_copy(o[:, hh * T:(hh + 2) * T], ps.ap[:, :], tok, *base)
            g.ps.put(ps, t)
            tO.append(t)
        t_at = tok
        yield

    og = fa[:, 0:2048]
    tg = []

    def gates():
        dead = [g.pe.last(), g.act.last(), g.dve.last(), g.pool.last()]
        for n in range(4):
            (ps, tok), = g.proj("hg_in", j * 16 + 12 + n, 8, 256, g.hh, g.hl, [])
            s = og[:, n * 512:(n + 1) * 512]
            tg.append(silu_gate(g, s, evac_scaled(g, s, ps, tok, r, tr, *dead)))
            yield

    zh, zl = g.ra[:, 0:2048], g.ra[:, 2048:4096]
    tz = []

    def tail(n):
        s = o[:, n * 512:(n + 1) * 512]
        end = norm_heads(g, s, 1, 128, lambda c: g.P("hg_g_norm", j), g.C("ones", 0, 128), [tO[n]])
        yield
        t = end()
        t = g.v_tt(s, s, og[:, n * 512:(n + 1) * 512], ALU.mult, tg[n], t)
        t1, t2 = g.split_act(zh[:, n * 512:(n + 1) * 512], zl[:, n * 512:(n + 1) * 512], s, t, *base)
        tz.extend([t2, t2])
        yield

    for _ in project(0):
        pass
    other = project(1)
    for i, _ in enumerate(scan(0)):
        next(other, None)
    for _ in other:
        pass
    other = gates()
    for i, _ in enumerate(scan(1)):
        if i % 2 == 0:
            next(other, None)
    for _ in other:
        pass
    ends = [tail(n) for n in range(4)]
    for n in range(5):
        if n < 4:
            next(ends[n])
        if n:
            next(ends[n - 1])
    return out_add(g, "hg_out", j * 4, zh, zl, tz)


def silu_gate(g, og, t):
    u = g.tmp.get()
    t = exp_silu(g, og, og, u.ap[:, :], [t, *u.free])
    g.tmp.put(u, t)
    return t


def sigmoid_gate(g, og, t):
    return sigmoid(g, og, og, t)[0]


def gated_tail(g, name, n0, o, to, per, dim, gcol, gate, zh, zl, r, tr, base):
    tz = []
    for n in range(4):
        s = o[:, n * 512:(n + 1) * 512]
        end = norm_heads(g, s, per, dim, lambda c, n=n: gcol(n, c), g.C("ones", 0, 128), [to[n]])
        (ps, tok), = g.proj(name, n0 + n, 8, 256, g.hh, g.hl, [])
        t = end()
        og = g.tmp.get()
        tg = gate(g, og.ap[:, :], evac_scaled(g, og.ap[:, :], ps, tok, r, tr, *og.free))
        t = g.v_tt(s, s, og.ap[:, :], ALU.mult, tg, t)
        g.tmp.put(og, t)
        t1, t2 = g.split_act(zh[:, n * 512:(n + 1) * 512], zl[:, n * 512:(n + 1) * 512], s, t, *base)
        tz += [t2, t2]
    return tz


def norm_heads(g, s, per, dim, gcol, ones, after):
    sq = g.tmp.get()
    t = g.a_act(sq.ap[:, :], s, ACT.Square, *after, *sq.free)

    def finish():
        n = 512 // per
        ps = g.ps.get()
        for c in range(2):
            if per == 1:
                tok = g.mm(ps.ap[:, c * T:(c + 1) * T], ones, sq.ap[:, c * T:(c + 1) * T], after=[t, *ps.free])
            else:
                tok = g.mm(ps.ap[:, 0:T], ones, sq.ap[:, c * T:(c + 1) * T], first=c == 0, last=c == 1,
                           after=[t, *ps.free])
        y, z = g.tmp.get(), g.tmp.get()
        v, yy, zz = sq.ap[:, 0:n], y.ap[:, 0:n], z.ap[:, 0:n]
        t1 = g.v_ts(v, ps.ap[:, 0:n], 1.0 / dim, 1e-6, ALU.mult, ALU.add, tok)
        g.ps.put(ps, t1)
        t2 = g.a_act(yy, v, ACT.Ln, t1, *y.free)
        t2 = g.a_act(yy, yy, ACT.Exp, t2, scale=-0.5)
        t3 = g.v_tt(zz, yy, yy, ALU.mult, t2, *z.free)
        t3 = g.v_stt(zz, zz, -0.5, v, ALU.mult, ALU.mult, t3)
        t3 = g.v_stt(zz, zz, 1.5, yy, ALU.add, ALU.mult, t3)
        for c in range(2):
            a = s[:, c * T:(c + 1) * T]
            r = zz[:, (c * T) % n:(c * T) % n + T]
            t4 = g.v_stt(a, a, gcol(c), r, ALU.mult, ALU.mult, t3)
        for x in (sq, y, z):
            g.tmp.put(x, t4, t2)
        return t4

    return finish


def mlstm(g, tx):
    per_k, r, tr = second_norm(g, 1, 1, [tx])
    rc, trc = token_factor(g, r, tr)
    fa = g.fa
    q, k = fa[:, 0:1024], fa[:, 1024:2048]
    V = fa[:, 2048:4096]
    h_ = fa[:, 4096:6144]
    W, AT = fa[:, 6144:6528], fa[:, 6528:6912]
    rows = fa[0:4, 6912:8960]
    em = fa[:, 8960:9216]
    dn = fa[:, 9216:9472]
    base = [g.pe.last(), g.act.last(), g.dve.last()]
    ps = g.ps.get()
    c0 = PARAM_COLS["w_if"]
    for i in range(2):
        for kk in range(8):
            w = g.par[:, c0 + kk * 8 + i * 4:c0 + kk * 8 + i * 4 + 4]
            out = ps.ap[0:4, i * T:(i + 1) * T]
            g.mm(out, w, g.xk(g.hh, kk).bitcast(F32), first=kk == 0, last=False, inc=False, after=[per_k[kk], *ps.free])
            tok = g.mm(out, w, g.xk(g.hl, kk).bitcast(F32), first=False, last=kk == 7)
    G, X1, Lc, A, CM, NM = [rows[:, i * T:(i + 1) * T] for i in (0, 2, 3, 4, 5, 6)]
    ig, fg = rows[:, 0:T], rows[:, T:2 * T]
    t = g.v_tt(v2(rows[:, 0:512]), v2(ps.ap[0:4, :]), bc2(r[0:4, :]), ALU.mult, tok, tr.get(), *base)
    g.ps.put(ps, t)
    for i, a in enumerate((ig, fg)):
        t = g.v_ts(a, a, g.P("ml_b_if", i, 4), None, ALU.add, None, t)
    t = g.a_act(rows[:, 0:512], rows[:, 0:512], ACT.Tanh, t, scale=1.0 / 15)
    t = g.v_ts(rows[:, 0:512], rows[:, 0:512], 15.0, None, ALU.mult, None, t)
    t = g.a_act(X1, fg, ACT.Exp, t, scale=-1.0)
    t = g.v_ts(X1, X1, 1.0, None, ALU.add, None, t)
    t = g.a_act(X1, X1, ACT.Ln, t)
    t = g.dve.op(lambda e: e.tensor_tensor_scan(Lc, g.C("ones", 0, 1, 0, 4).broadcast_to([4, T]), X1, 0.0,
                                                ALU.mult, ALU.add), t)
    t = g.v_tt(A, ig, Lc, ALU.add, t)
    t = g.dve.op(lambda e: e.tensor_tensor_scan(CM, A, A, 0.0, ALU.max, ALU.max), t)
    t = g.v_tt(NM, Lc, CM, ALU.subtract, t)
    ac = g.small[:, 528:536]
    ps = g.ps.get()
    for sb in range(2):
        tok = g.pe.op(lambda e, sb=sb, ps=ps: e.transpose(ps.ap[:, sb * 4:sb * 4 + 4], A[:, sb * 128:(sb + 1) * 128],
                                                   g.C("ident", 0, 4, 0, 4)), t, *ps.free)
    tac = g.v_copy(ac, ps.ap[:, 0:8], tok)
    g.ps.put(ps, tac)
    tq = []
    for n in range(4):
        (ps, tok), = g.proj("ml_in", n, 8, 256, g.hh, g.hl, [])
        dst = (q if n < 2 else k)[:, (n % 2) * 512:(n % 2) * 512 + 512]
        tq.append(evac_scaled(g, dst, ps, tok, r, tr, *base))
    tv = []
    for n in range(2):
        banks = [g.ps.get() for _ in range(2)]
        tok = token_major(g, "ml_in", [4 + 2 * n, 5 + 2 * n], 256, 0, banks, per_k)
        for tb in range(2):
            t = g.v_ts(V[:, tb * 1024 + n * 512:tb * 1024 + (n + 1) * 512], banks[tb].ap[:, :], rc[:, tb:tb + 1], None,
                       ALU.mult, None, tok, trc, *base)
            g.ps.put(banks[tb], t)
            tv.append(t)
    th = []
    for h in range(4):
        ps = g.ps.get()
        s_ = g.C("ident", h, 1, 0, 4).broadcast_to([4, 128])
        tok = g.mm(ps.ap[:, 0:T], s_, CM, after=[tac, *ps.free])
        tok = g.mm(ps.ap[:, T:2 * T], s_, NM)
        free = [g.pe.last(), g.dve.last()]
        t = g.v_ts(W[:, 0:256], ps.ap[:, 0:256], ac[:, h:h + 1], 0.0, ALU.subtract, ALU.max, tok, *base)
        t = g.v_ts(W[:, 256:384], ps.ap[:, 128:256], ac[:, 4 + h:5 + h], 0.0, ALU.subtract, ALU.max, tok, *base)
        te = g.a_act(em, ps.ap[:, T:2 * T], ACT.Exp, tok, t, *free)
        g.ps.put(ps, t, te)
        t = g.a_act(W, W, ACT.Exp, t, scale=-1.0)
        for a in (0, 256):
            t = g.v_tt(W[:, a:a + 128], W[:, a:a + 128], g.C("maskT", 0, 128), ALU.mult, t)
        ps = g.ps.get()
        tok = g.mm(ps.ap[:, 0:256], k[:, h * T:h * T + 128], q[:, h * T:(h + 1) * T], after=[*tq, *ps.free])
        tok = g.mm(ps.ap[:, 256:384], k[:, h * T + 128:(h + 1) * T], q[:, h * T + 128:(h + 1) * T])
        t = g.v_stt(AT, ps.ap[:, 0:384], 128 ** -0.5, W, ALU.mult, ALU.mult, tok, t, *free)
        g.ps.put(ps, t)
        ps, pd = g.ps.get(), g.ps.get()
        g.mm(pd.ap[:, 0:256], g.C("ones", 0, 128), AT[:, 0:256], last=False, inc=False, after=[t, *pd.free])
        tokd = g.mm(pd.ap[:, 128:256], g.C("ones", 0, 128), AT[:, 256:384], first=False)
        for c in range(2):
            a = h * 256 + c * 128
            g.mm(ps.ap[:, c * T:c * T + 256], V[:, a:a + 128], AT[:, 0:256], last=False, inc=False,
                 after=[*tv, *ps.free])
            tok = g.mm(ps.ap[:, c * T + 128:c * T + 256], V[:, 1024 + a:1024 + a + 128], AT[:, 256:384], first=False)
        t = g.a_act(dn, pd.ap[:, 0:256], ACT.Abs, tokd, *free)
        g.ps.put(pd, t)
        t = g.v_tt(dn, dn, em, ALU.max, t, te)
        t = g.dve.op(lambda e: e.reciprocal(dn, dn), t)
        t = g.v_tt(v2(h_[:, 2 * h * T:(2 * h + 2) * T]), v2(ps.ap[:, :]), bc2(dn), ALU.mult, t, tok, *base)
        g.ps.put(ps, t)
        th.append(t)
    zh, zl = g.ra[:, 0:2048], g.ra[:, 2048:4096]
    tz = []
    tz = gated_tail(g, "ml_in", 8, h_, th, 2, 256, lambda n, c: g.P("ml_norm", 2 * n + c), sigmoid_gate, zh, zl, r, tr,
                    base)
    return out_add(g, "ml_out", 0, zh, zl, tz)


def swa(g, tx):
    per_k, r, tr = second_norm(g, 2, 1, [tx])
    fa = g.fa
    q, k = fa[:, 2048:4096], fa[:, 4096:5120]
    V = fa[:, 5120:5632]
    o = fa[:, 5632:7680]
    base = [g.pe.last(), g.act.last(), g.dve.last()]
    tq = []
    gq = g.small[:, 540:541]
    t0 = g.v_ts(gq, g.P("sw_q_norm", 0), 0.125, None, ALU.mult, None, *base)
    end = None
    for n in range(6):
        dst, gain, tg = ((q[:, n * 512:(n + 1) * 512], gq, t0) if n < 4 else
                         (k[:, (n - 4) * 512:(n - 3) * 512], g.P("sw_k_norm", 0), None))
        (ps, tok), = g.proj("sw_in", n, 8, 256, g.hh, g.hl, [], per_k=per_k)
        if end:
            tq.append(end())
        t = evac_scaled(g, dst, ps, tok, r, tr, *base)
        end = norm_heads(g, dst, 1, 64, lambda c, a=gain: a, g.C("ones64", 0, 128), [t, tg])
    banks = [g.ps.get() for _ in range(2)]
    rc, trc = token_factor(g, r, tr)
    tok = token_major(g, "sw_in", [6], 256, 0, banks, per_k)
    tq.append(end())
    tv = []
    for tb in range(2):
        t = g.v_ts(V[:, tb * 256:(tb + 1) * 256], banks[tb].ap[:, 0:256], rc[:, tb:tb + 1], None, ALU.mult, None,
                   tok, trc, *base)
        g.ps.put(banks[tb], t)
        tv.append(t)
    zh, zl = g.ra[:, 0:2048], g.ra[:, 2048:4096]
    tz, held, po = [], {}, {}
    for u in g.sring.bufs:
        u.free = [*u.free, *base]

    def scores(h):
        c, p0, gk = h // 2, 64 * (h % 2), h // 4
        ps = g.ps.get()
        g.mm(ps.ap[:, 0:128], q[p0:p0 + 64, c * T:c * T + 128], k[p0:p0 + 64, gk * T:gk * T + 128],
             after=[*tq, *ps.free], inc=False)
        tok = g.mm(ps.ap[:, 128:384], q[p0:p0 + 64, c * T + 128:(c + 1) * T], k[p0:p0 + 64, gk * T:(gk + 1) * T])
        u = g.sring.get()
        slope = 2.0 ** (-8.0 * (h + 1) / 16)
        held[h] = (u, softmax3(g, u, tok, ps, (g.C("dist3", 0, 384), slope), 1.0, sink=g.P("sw_sinks", h)))

    def scale(h):
        u, state = held[h]
        held[h] = (u, softmax3_scale(g, u, state))

    def turn(h):
        u, ta = held[h]
        pt, tE, tpt = turn3(g, u.ap, [ta])
        g.sring.put(u, tE)
        held[h] = (pt, tpt)

    def values(h):
        c, p0, gk = h // 2, 64 * (h % 2), h // 4
        pt, tpt = held.pop(h)
        if h % 2 == 0:
            po[0] = g.ps.get()
        b = po[0]
        g.mm(b.ap[p0:p0 + 64, 0:256], V[:, gk * 64:(gk + 1) * 64], pt.ap[:, 0:256], last=False, inc=False,
             after=[tpt, *tv, *b.free])
        tok = g.mm(b.ap[p0:p0 + 64, 128:256], V[:, 256 + gk * 64:256 + (gk + 1) * 64], pt.ap[:, 256:384], first=False)
        g.tmp.put(pt, tok)
        if h % 2:
            oo = o[:, c * T:(c + 1) * T]
            t = g.v_copy(oo, b.ap[:, 0:256], tok, *base)
            g.ps.put(b, t)
            tz.append(g.split_act(g.xk(zh, c), g.xk(zl, c), oo, t, *base)[1])

    pipelined(16, [scores, scale, turn, values], lambda: None)
    return out_add(g, "sw_out", 0, zh, zl, tz)


def ple(g, layer, tx):
    per_k, r, tr = second_norm(g, layer, 3, [tx])
    gate = g.fa[:, 2048:4096]
    base = [g.pe.last(), g.act.last(), g.dve.last()]
    pt = g.fa[:, 4096:4608]
    ph, pl = g.ra[:, 0:512], g.ra[:, 512:1024]
    g.sp.dma(lambda e: e.dma_start(pt, g.args["pT"][layer]), g.s_p[1], *base)
    t1, t2 = g.split_act(ph, pl, pt, (g.s_p[1], 16 * (layer + 1)), *base)
    tp = [t1, t2]
    tg = []
    for j in range(4):
        (ps, tok), = g.proj("ple_gate", layer * 4 + j, 8, 256, g.hh, g.hl, [], per_k=per_k)
        s = gate[:, j * 512:(j + 1) * 512]
        t = evac_scaled(g, s, ps, tok, r, tr, *base)
        tg.append(sigmoid(g, s, s, t)[0])
    w = g.weight("ple_proj", layer)
    for j in range(4):
        ps = g.ps.get()
        for c in range(2):
            tok = g.group(w, 2, 1024, ph, pl, (2 * j + c) * 128, ps.ap[:, c * T:(c + 1) * T], [*tp, *ps.free])
        s = gate[:, j * 512:(j + 1) * 512]
        t = g.v_tt(s, s, ps.ap[:, :], ALU.mult, tok, tg[j])
        g.ps.put(ps, t)
        xs = g.x[:, j * 512:(j + 1) * 512]
        t = g.v_tt(xs, xs, s, ALU.add, t, base[1])
    g.done(w, tok)
    return t


STAGES = ["mix0", "ffn0", "mix1", "ffn1"] + [f"{a}{n}" for n in range(4) for a in ("h1_", "mx_", "h2_", "pl_")]


def emit(g, start=0, stop=99):
    t0, tc = load_small(g)
    g.dve.wait(t0)
    g.act.wait(t0)
    g.pe.wait(t0)
    tx = t0
    g.t_sc = exp_silu(g, g.sc[:, 0:8], g.par[:, PARAM_COLS["c"]:PARAM_COLS["c"] + 8], g.small[:, 570:578], [t0])
    for j in range(8):
        modulation_tile(g, 0, j)
    g.dve.wait(tc)
    g.act.wait(tc)
    g.pe.wait(tc)
    g.pool.wait(tc)
    tables(g, t0)
    with ExitStack() as ctx:
        g.scope(ctx, 1, 11392, 8704)
        for lay in range(2):
            mod = g.mod[:, lay * 48:(lay + 1) * 48]
            if start <= 2 * lay < stop:
                tx = mix_first(g, lay, mod)
            if start <= 2 * lay + 1 < stop:
                tx = first_ffn(g, lay, mod)
    with ExitStack() as ctx:
        g.scope(ctx, 2, 15104, 4096)
        for layer in range(4):
            s = 4 + 4 * layer
            if start <= s < stop:
                tx = second_ffn(g, layer, 0, tx)
            if start <= s + 1 < stop:
                tx = [lambda: hgrn(g, layer, layer // 3, tx), lambda: mlstm(g, tx), lambda: swa(g, tx)][layer % 3]()
            if start <= s + 2 < stop:
                tx = second_ffn(g, layer, 1, tx)
            if start <= s + 3 < stop:
                tx = ple(g, layer, tx)
    g.sp.dma(lambda e: e.dma_start(g.args["out"], g.x[:, :]), g.s_out, tx)
    g.sp.wait((g.s_out, 16))


def build(nc: bass.Bass, args, order, start=0, stop=99):
    with ExitStack() as ctx:
        g = Program(nc, ctx, args, order)
        emit(g, start, stop)
        block = ctx.enter_context(nc.Block())

        @block.sync
        def _(eng):
            g.sp.play(eng)

        @block.scalar
        def _(eng):
            g.act.play(eng)

        @block.vector
        def _(eng):
            g.dve.play(eng)

        @block.tensor
        def _(eng):
            g.pe.play(eng)

        @block.gpsimd
        def _(eng):
            g.pool.play(eng)


def cols(v):
    v = np.asarray(v)
    return v.reshape(-1, 128).T


def rows_to(v, n=128):
    a = np.zeros((128, v.shape[1]), np.float32)
    a[:v.shape[0]] = v
    return a


def layout(i):
    par = [cols(i["c"]), cols(i["g_pre_mix"]), cols(i["b_ada"]),
           rows_to(np.stack([i[n][l] for l in range(2) for n in ("da_lam_q1", "da_lam_k1", "da_lam_q2", "da_lam_k2")], 1)),
           cols(i["da_g_subln"]), cols(i["mla_g_cq"]), cols(i["mla_g_ckv"]), cols(i["sc_conv"]), cols(i["cf_conv"]),
           cols(i["cf_conv_b"]), cols(i["cf_ln_g"]), cols(i["cf_ln_b"]), cols(i["g_post_mix"]), cols(i["g_pre_ffn"]),
           cols(i["ffn_conv"]), cols(i["g_post_ffn"]), cols(i["norm_gains_2"]), cols(i["hg_lower_bounds_2"]),
           cols(i["hg_g_norm_2"]), rows_to(np.asarray(i["ml_b_if_2"]).reshape(2, 4).T), cols(i["ml_norm_2"]),
           np.concatenate([np.asarray(i["sw_q_norm_2"]).T] * 2, 0), np.concatenate([np.asarray(i["sw_k_norm_2"]).T] * 2, 0),
           np.broadcast_to(np.asarray(i["sw_sinks_2"]), (128, 16)),
           np.asarray(i["ml_w_if_2"])[0].reshape(8, 128, 8).transpose(1, 0, 2).reshape(128, 64)]
    par = np.concatenate([np.asarray(p) for p in par], 1)
    assert par.shape == (128, NPAR)

    def kn(ws, n, plan=None):
        return np.stack([tiles_kn(w, c) for w in ws for c in (plan or [_span(a, n) for a in range(0, w.shape[1], n)])])

    dup = [sum([_span(1024 + 64 * (2 * a + b // 2), 64) for b in range(4)], []) for a in range(2)]
    gu = [_span(128 * a, 128) + _span(2816 + 128 * a, 128) for a in range(22)]

    def ko(ws):
        return np.stack([np.ascontiguousarray(w[a:a + 256].reshape(2, 128, 1024).transpose(1, 0, 2)).reshape(128, 2048)
                         for w in ws for a in range(0, 2816, 256)])

    out = {
        "params": par, "consts": constants(), "positions": np.asarray(i["positions"]),
        "xT": np.ascontiguousarray(np.asarray(i["x"])[0].T.reshape(8, 128, 256).transpose(1, 0, 2)).reshape(128, 2048),
        "pT": np.ascontiguousarray(np.asarray(i["p_2"])[:, 0].transpose(0, 2, 1).reshape(4, 2, 128, 256)
                                   .transpose(0, 2, 1, 3)).reshape(4, 128, 512),
        "w_ada": kn(i["w_ada"], 256), "w_in": kn(i["w_in"], 0, WIN),
        "w_mc": kn(i["w_in"], 0, [_span(2048, 160)]),
        "da_w_o": kn(i["da_w_o"], 512), "mla_w_o": kn(i["mla_w_o"], 512), "sc_w_o": kn(i["sc_w_o"], 512),
        "cf_w_o": kn(i["cf_w_o"], 512), "mla_w_uq": kn(i["mla_w_uq"], 384), "mla_w_ukv": kn(i["mla_w_ukv"], 1024),
        "w_mix_out": kn(i["w_mix_out"], 256), "w_up": kn(i["w_up"], 0, gu), "w_down": ko(i["w_down"]),
        "w_gu": kn(np.asarray(i["w_ffn_gu_2"]).reshape(8, 1024, 5632), 0, gu),
        "w_dn": ko(np.asarray(i["w_ffn_down_2"]).reshape(8, 2816, 1024)),
        "ple_gate": kn(i["w_ple_gate_2"], 256), "ple_proj": kn(i["w_ple_proj_2"], 1024),
        "hg_in": kn(i["hg_w_in_2"], 256), "hg_out": kn(i["hg_w_out_2"], 256),
        "ml_in": kn(i["ml_w_qkvo_2"], 256), "ml_out": kn(i["ml_w_out_2"], 256),
        "sw_in": kn(i["sw_w_qkv_2"], 0, [_span(256 * a, 256) for a in range(4)] + dup + [_span(1280, 256)]), "sw_out": kn(i["sw_w_o_2"], 256),
    }
    return out


def weight_order(start=0, stop=99):
    out = []

    def add(name, *ns, split=True):
        out.extend((name, n, split) for n in ns)

    def ffn_tiles(up, up0, down, dn0, ada=False):
        for p in range(NF // 2):
            for c in (2 * p, 2 * p + 1):
                add(up, up0 + c)
                if ada:
                    add("w_ada", 24 + c, split=False)
            if p:
                add(down, dn0 + p - 1)
        if ada:
            add("w_ada", 46, 47, split=False)
        add(down, dn0 + NF // 2 - 1)

    def merge_tiles(lay, wo, branch):
        for n in range(2):
            add(wo, lay * 2 + n)
            if branch is not None:
                add("w_in", *[lay * 34 + GATE0 + 4 * branch + 2 * n + i for i in range(2)])

    add("w_ada", *range(8), split=False)
    for lay in range(2):
        if start <= 2 * lay < stop:
            w = lay * 34
            at = 8
            for n in range(MLA0):
                add("w_in", w + n)
                if lay == 0 and n < len(ADA_IN_MIX):
                    add("w_ada", *range(at, at + ADA_IN_MIX[n]), split=False)
                    at += ADA_IN_MIX[n]
            merge_tiles(lay, "sc_w_o", 2)
            add("w_in", w + MLA0, w + MLA0 + 1)
            add("w_mc", lay)
            add("mla_w_uq", 2 * lay, 2 * lay + 1)
            add("mla_w_ukv", lay)
            add("w_in", *range(w + GATE0 + 4, w + GATE0 + 8))
            merge_tiles(lay, "da_w_o", 0)
            merge_tiles(lay, "cf_w_o", 3)
            merge_tiles(lay, "mla_w_o", None)
            add("w_mix_out", *range(4 * lay, 4 * lay + 4))
        if start <= 2 * lay + 1 < stop:
            ffn_tiles("w_up", lay * 22, "w_down", lay * 11, ada=lay == 0)
    for layer in range(4):
        s = 4 + 4 * layer
        j = layer // 3
        if start <= s < stop:
            ffn_tiles("w_gu", layer * 44, "w_dn", layer * 22)
        if start <= s + 1 < stop:
            if layer % 3 == 0:
                for a in (0, 2):
                    add("hg_in", *[16 * j + a + n for n in (0, 1, 4, 5, 8, 9)])
                add("hg_in", *range(16 * j + 12, 16 * j + 16))
                add("hg_out", *range(4 * j, 4 * j + 4))
            elif layer == 1:
                add("ml_in", *range(12))
                add("ml_out", *range(4))
            else:
                add("sw_in", *range(7))
                add("sw_out", *range(4))
        if start <= s + 2 < stop:
            ffn_tiles("w_gu", layer * 44 + 22, "w_dn", layer * 22 + 11)
        if start <= s + 3 < stop:
            add("ple_gate", *range(layer * 4, layer * 4 + 4))
            add("ple_proj", layer)
    return out


def kernel(**inputs):
    import concourse.bacc as _bacc
    from concourse.bass_utils import run_bass_kernel_spmd as _run

    arrays = layout({k: np.asarray(v) for k, v in inputs.items()})
    nc = _bacc.Bacc("TRN2", target_bir_lowering=False, num_devices=1)
    args = {k: nc.dram_tensor(k, v.shape, mybir.dt.from_np(v.dtype), kind="ExternalInput").ap() for k, v in arrays.items()}
    args["out"] = nc.dram_tensor("out", (128, 2048), F32, kind="ExternalOutput").ap()
    build(nc, args, weight_order())
    r = _run(nc, [arrays], core_ids=[0])
    o = r.results[0]["out"]
    return np.ascontiguousarray(o.reshape(128, 8, 256).transpose(1, 0, 2).reshape(1024, 256).T)[None]
```

```python
import math
from contextlib import ExitStack

import numpy as np
import concourse.bass as bass
from concourse import mybir

F32 = mybir.dt.float32
F32R = mybir.dt.float32r
I32 = mybir.dt.int32
ALU = mybir.AluOpType
ACT = mybir.ActivationFunctionType
AX = mybir.AxisListType.X

D = 1024
T = 256
NC = 8
NF = 22
TILE = 2048
NEG = -1e30

PARAM_COLS = {}


def _plan_params():
    at = 0
    for name, n in [("c", 8), ("g_pre_mix", 16), ("b_ada", 96), ("lam", 8), ("da_g_subln", 2),
                    ("mla_g_cq", 6), ("mla_g_ckv", 4), ("sc_conv", 24), ("cf_conv", 248),
                    ("cf_conv_b", 8), ("cf_ln_g", 8), ("cf_ln_b", 8), ("g_post_mix", 16),
                    ("g_pre_ffn", 16), ("ffn_conv", 132), ("g_post_ffn", 16), ("norm_gains", 128),
                    ("hg_lb", 32), ("hg_g_norm", 2), ("ml_b_if", 2), ("ml_norm", 8),
                    ("sw_q_norm", 1), ("sw_k_norm", 1), ("sw_sinks", 16), ("w_if", 64)]:
        PARAM_COLS[name] = at
        at += n
    return at


NPAR = _plan_params()

CONST_COLS = {}


def _plan_consts():
    at = 0
    for name, n in [("ident", 128), ("ones", 128), ("ones64", 128), ("mask3", 384), ("dist3", 384),
                    ("maskT", 128), ("lev", 192), ("rot", 96), ("inv", 1), ("rst", 256)]:
        CONST_COLS[name] = at
        at += n
    return at


NCON = _plan_consts()


def constants():
    c = np.zeros((128, NCON), np.float32)

    def put(name, a):
        c[:a.shape[0], CONST_COLS[name]:CONST_COLS[name] + a.shape[1]] = a

    i = np.arange(128)
    put("ident", np.eye(128, dtype=np.float32))
    put("ones", np.ones((128, 128), np.float32))
    put("ones64", (i[:, None] // 64 == i[None, :] // 64).astype(np.float32))
    causal = np.where(i[None, :] <= i[:, None], 0.0, NEG)
    put("mask3", np.concatenate([causal, np.zeros((128, 128)), causal], 1))
    same = i[:, None] - i[None, :]
    prev = same + 128
    put("dist3", np.concatenate([np.where(same >= 0, same, -NEG * 1e3), np.where(prev < 128, prev, -NEG * 1e3),
                                 np.where(same >= 0, same, -NEG * 1e3)], 1))
    put("maskT", (i[None, :] >= i[:, None]).astype(np.float32))
    s = (i % 32)[:, None]
    t = np.arange(32)[None, :]
    lev = []
    for m in (16, 8, 4, 2, 1):
        lev.append((s // (2 * m) == t // (2 * m)) & (s % (2 * m) < m) & (t % (2 * m) >= m))
    lev.append(s == t)
    put("lev", np.concatenate(lev, 1).astype(np.float32))
    rot = np.zeros((128, 96), np.float32)
    for n in range(16):
        rot[80 + n, 64 + n] = -1.0
        rot[64 + n, 80 + n] = 1.0
    put("rot", rot)
    inv = np.zeros((128, 1), np.float32)
    f = (np.float32(10000.0) ** (-np.arange(16, dtype=np.float32) / np.float32(16))).astype(np.float32)
    inv[64:80, 0] = f
    inv[80:96, 0] = f
    put("inv", inv)
    put("rst", np.tile((np.arange(256) % 64 != 0).astype(np.float32), (128, 1)))
    return c


def tiles_kn(w, cols):
    k = w.shape[0] // 128
    return np.ascontiguousarray(w[:, cols].reshape(k, 128, len(cols)).transpose(1, 0, 2)).reshape(128, -1)


def _span(a, n):
    return list(range(a, a + n))


def plan_win():
    t = []
    for j in range(4):
        t.append(_span(3744 + 128 * j, 128) + _span(3744 + 512 + 128 * j, 128))
    for j in range(6):
        t.append(_span(256 * j, 256))
    for j in range(4):
        t.append(_span(2208 + 128 * j, 128) + _span(2208 + 1024 + 128 * j, 128))
    for j in range(2):
        t.append(_span(2208 + 512 + 256 * j, 256))
    for j in range(2):
        t.append(_span(1536 + 256 * j, 256))
    for j in range(16):
        t.append(_span(4768 + 256 * j, 256))
    return t


WIN = plan_win()
CF0, DA0, SCU0, SCB0, MLA0, GATE0 = 0, 4, 10, 14, 16, 18
TWO_PI = 2.0 * math.pi


class Queue:
    def __init__(self, sem, on=True):
        self.sem, self.n, self.ops, self.seen, self.on = sem, 0, [], {}, on

    def wait(self, *tokens):
        for t in tokens:
            if t is None:
                continue
            if isinstance(t, list):
                self.wait(*t)
                continue
            sem, v = t
            if v > 0 and self.seen.get(sem.name, 0) < v:
                self.seen[sem.name] = v
                self.ops.append(("w", sem, v))

    def op(self, fn, *after):
        self.wait(*after)
        self.n += 1
        self.ops.append(("i", fn, self.sem, 1))
        return (self.sem, self.n)

    def quiet(self, fn, *after):
        self.wait(*after)
        self.ops.append(("q", fn))

    def dma(self, fn, sem, *after):
        self.wait(*after)
        self.ops.append(("i", fn, sem, 16))

    def last(self):
        return (self.sem, self.n)

    def play(self, eng):
        for o in self.ops:
            if o[0] == "w":
                eng.wait_ge(o[1], o[2])
            elif o[0] == "i":
                o[1](eng).then_inc(o[2], o[3])
            else:
                o[1](eng)


class Buf:
    def __init__(self, ap):
        self.ap, self.free = ap, []


class Ring:

    def __init__(self, aps):
        self.bufs = [Buf(a) for a in aps]

    def get(self):
        return self.bufs.pop(0)

    def put(self, buf, *tokens):
        buf.free = [t for t in tokens]
        self.bufs.append(buf)


class Program:
    def __init__(self, nc, ctx, args, order, depth=4):
        self.nc, self.args, self.order, self.asked, self.ready = nc, args, order, 0, []
        self.depth = depth

        def sem(name):
            return ctx.enter_context(nc.semaphore(name))

        def sb(name, n, dt=F32):
            return ctx.enter_context(nc.sbuf_tensor(name, [128, n], dt))

        self.pe, self.act, self.dve, self.pool, self.sp = [Queue(sem("s_" + n)) for n in
                                                           ("pe", "act", "dve", "pool", "sp")]
        self.NL, self.NS = 3, 3
        self.land = sb("land", self.NL * TILE)
        self.whi = sb("whi", self.NS * TILE, F32R)
        self.wlo = sb("wlo", self.NS * TILE, F32R)
        self.s_land = [sem(f"s_land{i}") for i in range(self.NL)]
        self.s_misc = sem("s_misc")
        self.s_con = sem("s_con")
        self.s_out = sem("s_out")
        self.s_p = [sem("s_p0"), sem("s_p1")]
        self.n_p = 0
        self.t_mod = [None, None]
        self.t_rows = None
        self.x_squares = None
        self.pending, self.biases = [], []
        self.sc = sb("sc", 8)
        self.nload = 0
        self.slots, self.rest = list(range(self.NL)), [0] * self.NL
        self.share = False
        self.nsplit = 0
        self.land_free = [[] for _ in range(self.NL)]
        self.land_use = [0] * self.NL
        self.split_free = [[] for _ in range(self.NS)]
        self.x = sb("x", NC * T)
        self.hh = sb("hh", NC * T, F32R)
        self.hl = sb("hl", NC * T, F32R)
        self.par = sb("par", NPAR)
        self.con = sb("con", NCON)
        self.attn = sb("attn", 1152)
        self.sring = Ring([self.attn[:, i * 384:(i + 1) * 384] for i in range(3)])
        self.trig = sb("trig", 512)
        self.mod = sb("mod", 96)
        self.tmps = sb("tmps", 4 * 512)
        self.small = sb("small", 1024)
        self.ps = Ring([ctx.enter_context(nc.psum_tensor(f"ps{i}", [128, 512], F32)) for i in range(8)])
        self.cols = Ring([self.small[:, 600 + i * 16:616 + i * 16] for i in range(4)])
        self.tmp = Ring([self.tmps[:, i * 512:(i + 1) * 512] for i in range(4)])

    def scope(self, ctx, n, fa, ra):
        self.fa = ctx.enter_context(self.nc.sbuf_tensor(f"fa{n}", [128, fa], F32))
        self.ra = ctx.enter_context(self.nc.sbuf_tensor(f"ra{n}", [128, ra], F32R))

    def P(self, name, j, rows=128):
        a = PARAM_COLS[name] + j
        return self.par[0:rows, a:a + 1]

    def C(self, name, a, n, p0=0, p1=128):
        a += CONST_COLS[name]
        return self.con[p0:p1, a:a + n]

    def _prepare(self):
        i = len(self.ready)
        name, n, split = self.order[i]
        s = self._slot()
        self.slots.remove(s)
        self.slots.append(s)
        self.nload += 1
        self.rest[s] = self.nload + (0 if split or n < 8 else 4)
        self.land_use[s] += 1
        src = self.args[name][n]
        w = src.shape[1]
        dst = self.land[:, s * TILE:s * TILE + w]
        self.sp.dma(lambda e, d=dst, a=src: e.dma_start(d, a), self.s_land[s], *self.land_free[s])
        got = (self.s_land[s], 16 * self.land_use[s])
        if not split:
            self.ready.append((dst, None, got, s, None))
            self.land_free[s] = None
            return
        k = self.nsplit % self.NS
        self.nsplit += 1
        hi, lo = self.whi[:, k * TILE:k * TILE + w], self.wlo[:, k * TILE:k * TILE + w]
        t1 = self.act.op(lambda e, o=hi, a=dst: e.activation(o, a, ACT.Copy), got, *self.split_free[k])
        low = self.pool if self.share and self.nsplit % 2 else self.dve
        t2 = low.op(lambda e, o=lo, a=dst, b=hi.bitcast(F32): e.tensor_tensor(o, a, b, ALU.subtract),
                         got, t1, *self.split_free[k])
        self.land_free[s] = [t1, t2]
        self.split_free[k] = None
        self.ready.append((hi, lo, t2, s, k))

    def weight(self, name, n, split=True):
        if name != "w_ada":
            queue_all(self.biases)
            while self.order[self.asked][0] == "w_ada":
                queue_all(self.pending)
                lay, j = divmod(self.order[self.asked][1], 24)
                modulation_tile(self, lay, j, "pool")
        i = self.asked
        self.asked += 1
        assert self.order[i] == (name, n, split)
        while len(self.ready) <= i:
            self._prepare()
        self.prefetch(i)
        return self.ready[i]

    def prefetch(self, i=None):
        top = min((self.asked if i is None else i) + self.depth, len(self.order))
        while len(self.ready) < top and self._room():
            self._prepare()

    def _slot(self):
        for s in self.slots:
            if self.rest[s] <= self.nload and self.land_free[s] is not None:
                return s
        return self.slots[0]

    def _room(self):
        name, n, split = self.order[len(self.ready)]
        return self.land_free[self._slot()] is not None and (
            not split or self.split_free[self.nsplit % self.NS] is not None)

    def done(self, w, token):
        if w[4] is None:
            self.land_free[w[3]] = [token]
        else:
            self.split_free[w[4]] = [token]

    def mm3(self, out, wh, wl, xh, xl, first, last, skip=False, inc=False, after=()):
        pe = self.pe
        pe.wait(*after)
        pe.quiet(lambda e: e.matmul(out, wh, xh, start=first, stop=False, skip_group_check=skip))
        pe.quiet(lambda e: e.matmul(out, wh, xl, start=False, stop=False, skip_group_check=skip))
        fn = lambda e: e.matmul(out, wl, xh, start=False, stop=last, skip_group_check=skip)
        if inc:
            return pe.op(fn)
        pe.quiet(fn)

    def mm(self, out, lhsT, rhs, first=True, last=True, after=(), inc=True, skip=False):
        fn = lambda e: e.matmul(out, lhsT, rhs, start=first, stop=last, skip_group_check=skip)
        self.pe.wait(*after)
        if inc:
            return self.pe.op(fn)
        self.pe.quiet(fn)

    def xk(self, t, k):
        return t[:, k * T:(k + 1) * T]

    def v_tt(self, out, a, b, op, *after):
        return self.dve.op(lambda e: e.tensor_tensor(out, a, b, op), *after)

    def p_tt(self, out, a, b, op, *after):
        return self.pool.op(lambda e: e.tensor_tensor(out, a, b, op), *after)

    def v_ts(self, out, a, s1, s2, op0, op1, *after):
        if op1 is None:
            return self.dve.op(lambda e: e.tensor_scalar(out, a, s1, None, op0), *after)
        return self.dve.op(lambda e: e.tensor_scalar(out, a, s1, s2, op0, op1), *after)

    def v_stt(self, out, a, s, b, op0, op1, *after):
        return self.dve.op(lambda e: e.scalar_tensor_tensor(out, a, s, b, op0, op1), *after)

    def v_copy(self, out, a, *after):
        return self.dve.op(lambda e: e.tensor_copy(out, a), *after)

    def a_act(self, out, a, f, *after, **kw):
        return self.act.op(lambda e: e.activation(out, a, f, **kw), *after)

    def split_act(self, hi, lo, src, *after):
        t1 = self.a_act(hi, src, ACT.Copy, *after)
        return t1, self.v_tt(lo, src, hi.bitcast(F32), ALU.subtract, t1, *after)

    def rsqrt(self, out, v, t):
        b = self.tmp.get()
        n = v.shape[1]
        p = v.shape[0]
        y, z = b.ap[0:p, 0:n], b.ap[0:p, 256:256 + n]
        t1 = self.a_act(y, v, ACT.Ln, t, *b.free)
        t1 = self.a_act(y, y, ACT.Exp, t1, scale=-0.5)
        t2 = self.v_tt(z, y, y, ALU.mult, t1, *b.free)
        t2 = self.v_stt(z, z, -0.5, v, ALU.mult, ALU.mult, t2)
        t2 = self.v_stt(out, z, 1.5, y, ALU.add, ALU.mult, t2)
        self.tmp.put(b, t1, t2)
        return t2

    def stats(self, src, n, dim, eps, out, vbuf, sq, after):
        t1, finish = self.stats_later(src, n, dim, eps, out, vbuf, sq, after)
        return finish(), t1

    def stats_later(self, src, n, dim, eps, out, vbuf, sq, after):
        t1 = self.a_act(sq[:, 0:n * T], src, ACT.Square, *after)
        b = self.tmp.get()
        t2 = self.dve.op(lambda e: e.tensor_reduce(
            b.ap[:, 0:T], sq[:, 0:n * T].rearrange("p (c t) -> p t c", c=n), AX, ALU.add), t1, *b.free)

        def finish():
            ps = self.ps.get()
            t3 = self.mm(ps.ap[:, 0:T], self.C("ones", 0, 128), b.ap[:, 0:T], after=[t2, *ps.free])
            self.tmp.put(b, t3)
            t4 = self.v_ts(vbuf, ps.ap[:, 0:T], 1.0 / dim, eps, ALU.mult, ALU.add, t3, *after)
            self.ps.put(ps, t4)
            return self.rsqrt(out, vbuf, t4)

        return t1, finish

    def group(self, w, kc, width, xh, xl, cols, out, after, m=128, per_k=None):
        wh, wl = w[0], w[1]
        for k in range(kc):
            a = k * width + cols
            ready = [w[2], *after] if k == 0 else []
            if per_k:
                ready = ready + [per_k[k]]
            tok = self.mm3(out, wh[:, a:a + m], wl[:, a:a + m], self.xk(xh, k), self.xk(xl, k),
                           k == 0, k == kc - 1, inc=k == kc - 1, after=ready)
        return tok

    def proj(self, name, n, kc, width, xh, xl, after, per_k=None):
        w = self.weight(name, n)
        out = []
        ng = (width + 127) // 128
        for j in range(0, ng, 2):
            ps = self.ps.get()
            for i in range(j, min(j + 2, ng)):
                tok = self.group(w, kc, width, xh, xl, i * 128, ps.ap[:, (i - j) * T:(i - j + 1) * T],
                                 [*ps.free, *after], per_k=per_k)
            out.append((ps, tok))
        self.done(w, tok)
        return out

    def split_gain(self, gname, g0, n, src, after, free=()):
        toks = []
        for k in range(n):
            s, g = self.xk(src, k), self.P(gname, g0 + k)
            h, l = self.xk(self.hh, k), self.xk(self.hl, k)
            ready = after[k // 2] if len(after) == 4 else after[0]
            t1 = self.a_act(h, s, ACT.Identity, ready, *free, scale=g)
            t2 = self.v_stt(l, s, g, h.bitcast(F32), ALU.mult, ALU.subtract, t1, *free)
            toks.append(t2)
        return toks


class Later:

    def __init__(self, fn):
        self.fn, self.token = fn, None

    def get(self):
        if self.token is None:
            self.token = self.fn()
        return self.token


def bc2(ap):
    return ap.unsqueeze(1).broadcast_to([ap.shape[0], 2, ap.shape[1]])


def v2(ap):
    return ap.rearrange("p (a t) -> p a t", a=2)


def sigmoid(g, out, src, *after):
    t1 = g.a_act(out, src, ACT.Exp, *after, scale=-1.0)
    t = g.v_ts(out, out, 1.0, None, ALU.add, None, t1)
    return g.dve.op(lambda e: e.reciprocal(out, out), t), t1


def tanh_half(g, out, src, *after):
    return g.a_act(out, src, ACT.Tanh, *after, scale=0.5)


def split_half(g, hi, lo, src, *after):
    t1 = g.a_act(hi, src, ACT.Copy, *after, scale=0.5)
    return t1, g.v_stt(lo, src, 0.5, hi.bitcast(F32), ALU.mult, ALU.subtract, t1, *after)


def exp_silu(g, out, src, tmp, after):
    t, _ = sigmoid(g, tmp, src, *after)
    return g.v_tt(out, src, tmp, ALU.mult, t)


def load_small(g):
    a = g.args
    g.sp.dma(lambda e: e.dma_start(g.par[:, :], a["params"]), g.s_misc)
    g.act.dma(lambda e: e.dma_start(g.x[:, :], a["xT"]), g.s_misc)
    g.act.dma(lambda e: e.dma_start(g.con[:, :], a["consts"]), g.s_con, (g.s_land[0], 16))
    return (g.s_misc, 32), (g.s_con, 16)


def modulation_tile(g, lay, j, how):
    w = g.weight("w_ada", lay * 24 + j, split=False)
    wt = w[0]
    w3 = wt.rearrange("p (k n) -> p k n", k=8)
    sc = g.sc[:, 0:8].unsqueeze(2).broadcast_to([128, 8, 256])

    def add_bias(ps, tok):
        a = PARAM_COLS["b_ada"] + lay * 48 + 2 * j
        c = lay * 48 + 2 * j
        t = g.v_tt(g.mod[:, c:c + 2], ps.ap[:, 0:2], g.par[:, a:a + 2], ALU.add, tok)
        g.ps.put(ps, t)
        g.t_mod[lay] = t

    def partitions(rows, t):
        ps = g.ps.get()
        for i in range(2):
            tok = g.mm(ps.ap[:, i:i + 1], rows[:, i * 128:i * 128 + 128], g.C("ones", 0, 1),
                       after=[t, *g.con_tok, *ps.free])
        g.biases.append(lambda: add_bias(ps, tok))
        return tok

    if how == "pe":
        ps = g.ps.get()
        for i in range(2):
            for k in range(8):
                tok = g.mm(ps.ap[:, i:i + 1], wt[:, k * 256 + i * 128:k * 256 + i * 128 + 128], g.sc[:, k:k + 1],
                           first=k == 0, last=k == 7, after=[w[2], g.t_sc, *ps.free] if k == 0 else (), inc=k == 7)
        g.done(w, tok)
        g.biases.append(lambda: add_bias(ps, tok))
    elif how == "dve":
        i = len(g.pending)
        rows = g.attn[:, i * 256:(i + 1) * 256] if i < 4 else g.trig[:, (i - 4) * 256:(i - 3) * 256]
        t = g.v_tt(w3, w3, sc, ALU.mult, w[2], g.t_sc)
        t = g.dve.op(lambda e: e.tensor_reduce(rows, wt.rearrange("p (k n) -> p n k", k=8), AX, ALU.add), t)
        g.done(w, t)
        g.pending.append(lambda: partitions(rows, t))
    else:
        rows = g.small[:, 700:956]
        t = g.p_tt(w3, w3, sc, ALU.mult, w[2], g.t_sc)
        for n in (1024, 512):
            t = g.p_tt(wt[:, 0:n], wt[:, 0:n], wt[:, n:2 * n], ALU.add, t)
        t = g.p_tt(rows, wt[:, 0:256], wt[:, 256:512], ALU.add, t, g.t_rows)
        g.done(w, t)

        def later():
            g.t_rows = partitions(rows, t)

        g.pending.append(later)


def queue_all(fns):
    while fns:
        fns.pop(0)()


def finish_modulation(g):
    queue_all(g.pending)
    queue_all(g.biases)


class Squares:

    def __init__(self, g, sq, *after):
        self.g, self.sq, self.after, self.ps, self.queued, self.n = g, sq, after, g.ps.get(), None, 0

    def _add(self):
        s, t, i = self.queued
        for c in range(2):
            self.token = self.g.mm(self.ps.ap[:, 0:T], self.g.C("ones", 0, 128), s[:, c * T:(c + 1) * T],
                                   first=i == 0 and c == 0, last=i == 3 and c == 1, after=[t, *self.ps.free],
                                   inc=i == 3 and c == 1)
        self.queued = None

    def take(self, src, *after):
        if self.queued:
            self._add()
        s = self.sq[:, self.n * 512:(self.n + 1) * 512]
        t = self.g.a_act(s, src, ACT.Square, *after, *self.after)
        self.queued = (s, t, self.n)
        self.n += 1

    def factor(self, dim, eps, out, vbuf, *after):
        if self.queued:
            self._add()
        t = self.g.v_ts(vbuf, self.ps.ap[:, 0:T], 1.0 / dim, eps, ALU.mult, ALU.add, self.token, *after)
        self.g.ps.put(self.ps, t)
        return self.g.rsqrt(out, vbuf, t)


def modulated(g, gname, lay, mod, shift, scale, after):
    fa = g.fa
    xr, v, r = fa[:, 0:2048], g.small[:, 0:256], g.small[:, 256:512]
    A = g.small[:, 560:568]
    gc = PARAM_COLS[gname] + lay * 8
    finish_modulation(g)
    after = [*after, g.t_mod[lay]]
    t0 = g.v_ts(A, mod[:, scale:scale + 8], 1.0, None, ALU.add, None, *after)
    t0 = g.v_tt(A, A, g.par[:, gc:gc + 8], ALU.mult, t0)
    if g.x_squares is None:
        g.x_squares = Squares(g, fa[:, 2048:4096], *after)
        for p in range(4):
            g.x_squares.take(g.x[:, p * 512:(p + 1) * 512])
    t1 = g.x_squares.factor(D, 1e-6, r, v, *after)
    toks = []
    for p in range(4):
        w = slice(p * 512, (p + 1) * 512)
        t2 = g.v_tt(v2(xr[:, w]), v2(g.x[:, w]), bc2(r), ALU.mult, t1, *after)
        for k in (2 * p, 2 * p + 1):
            s = g.xk(xr, k)
            t3 = g.v_ts(s, s, A[:, k:k + 1], mod[:, shift + k:shift + k + 1], ALU.mult, ALU.add, t2, t0)
            _, t3 = g.split_act(g.xk(g.hh, k), g.xk(g.hl, k), s, t3, g.pe.last())
            toks.append(t3)
    return toks


def evac_y(g, y, banks):
    squares = Squares(g, g.fa[:, 2048:4096], g.pe.last(), g.dve.last())
    for i, (ps, tok) in enumerate(banks):
        s = y[:, i * 512:(i + 1) * 512]
        t = g.v_copy(s, ps.ap[:, :], tok)
        g.ps.put(ps, t)
        squares.take(s, t)
    return squares


def add_normed(g, y, lay, gname, mod, gate, squares):
    v, r = g.small[:, 0:256], g.small[:, 256:512]
    B = g.small[:, 560:568]
    gc = PARAM_COLS[gname] + lay * 8
    finish_modulation(g)
    t0 = g.v_tt(B, mod[:, gate:gate + 8], g.par[:, gc:gc + 8], ALU.mult, g.t_mod[lay], g.dve.last())
    t1 = squares.factor(D, 1e-6, r, v)
    g.x_squares = Squares(g, g.fa[:, 2048:4096], g.pe.last())
    for p in range(4):
        s, xs = y[:, p * 512:(p + 1) * 512], g.x[:, p * 512:(p + 1) * 512]
        t2 = g.v_tt(v2(s), v2(s), bc2(r), ALU.mult, t1)
        for k in (2 * p, 2 * p + 1):
            t3 = g.v_stt(g.xk(g.x, k), g.xk(y, k), B[:, k:k + 1], g.xk(g.x, k), ALU.mult, ALU.add, t2, t0)
        g.x_squares.take(xs, t3)
    return t3


def conv3(g, out, src, name, j, step, after):
    t = g.v_ts(out, src[:, 2:258], g.P(name, j + 2 * step), None, ALU.mult, None, *after)
    t = g.v_stt(out, src[:, 1:257], g.P(name, j + step), out, ALU.mult, ALU.add, t)
    return g.v_stt(out, src[:, 0:256], g.P(name, j), out, ALU.mult, ALU.add, t)


def down_setup(g):
    return [g.ps.get() for _ in range(4)]


def down_pair(g, name, n, acc, yb, ty, first, last):
    w = g.weight(name, n)
    yh, yl = yb.ap
    for c in range(2):
        for m in range(8):
            bank = acc[m // 2]
            a = c * 1024 + m * 128
            f = first and c == 0
            tok = g.mm3(bank.ap[:, (m % 2) * T:(m % 2 + 1) * T], w[0][:, a:a + 128], w[1][:, a:a + 128],
                        g.xk(yh, c), g.xk(yl, c), f and m % 2 == 0, last and c == 1, skip=True,
                        inc=m == 7 or (last and c == 1 and m % 2 == 1),
                        after=[w[2], *ty, *(bank.free if f else [])])
            if last and c == 1 and m % 2 == 1:
                bank.ready = tok
    g.done(w, tok)
    return tok


def ffn(g, up, up0, down, dn0, per_k, chunk):
    acc = down_setup(g)
    R = [Buf((g.ra[:, i * 1024:i * 1024 + 512], g.ra[:, i * 1024 + 512:i * 1024 + 1024])) for i in range(3)]
    for b in R:
        b.free = [g.pe.last()]
    ready = []
    npair = NF // 2

    def do_down(p):
        b, t = ready.pop(0)
        tok = down_pair(g, down, dn0 + p, acc, b, t, p == 0, p == npair - 1)
        b.free = [tok]
        R.append(b)

    for p in range(npair):
        b = R.pop(0)
        toks = []
        for c in range(2):
            (ps, tok), = g.proj(up, up0 + 2 * p + c, 8, 256, g.hh, g.hl, [], per_k=per_k)
            toks.append(chunk(2 * p + c, ps, tok, g.xk(b.ap[0], c), g.xk(b.ap[1], c), b.free))
        ready.append((b, toks))
        if p >= 1:
            do_down(p - 1)
    do_down(npair - 1)
    return acc


def first_ffn(g, lay, mod):
    base = [g.pe.last(), g.act.last(), g.dve.last(), g.t_mod[lay]]
    per_k = modulated(g, "g_pre_ffn", lay, mod, 24, 32, base)
    fa = g.fa
    A = [Buf(fa[:, 4096 + i * 512:4096 + i * 512 + 258]) for i in range(2)]
    S = [Buf(fa[:, 5120 + i * 256:5376 + i * 256]) for i in range(2)]
    for b in A:
        t = g.dve.op(lambda e, b=b: e.memset(b.ap[:, 0:2], 0.0), *base)
        b.free = [t]

    def chunk(j, ps, tok, yh, yl, free):
        a, s = A[j % 2].ap, S[j % 2].ap
        t = g.v_copy(a[:, 2:258], ps.ap[:, 0:T], tok, *A[j % 2].free)
        o = g.tmp.get()
        c1 = o.ap[:, 0:T]
        t = conv3(g, c1, a, "ffn_conv", lay * 66 + j, 22, [t, *o.free])
        A[j % 2].free = [t]
        t1 = g.a_act(s, c1, ACT.Silu, t)
        t2 = g.v_tt(o.ap[:, T:2 * T], s, ps.ap[:, T:2 * T], ALU.mult, t1, tok)
        g.ps.put(ps, t2)
        t3, t4 = g.split_act(yh, yl, o.ap[:, T:2 * T], t2, *free)
        g.tmp.put(o, t3, t4)
        return t4

    acc = ffn(g, "w_up", lay * 22, "w_down", lay * 11, per_k, chunk)
    y = fa[:, 0:2048]
    return add_normed(g, y, lay, "g_post_ffn", mod, 40, evac_y(g, y, [(b, b.ready) for b in acc]))


def softmax3(g, u, tps, ps, bias, scale, sink=None):
    b = g.cols.get()
    S = u.ap[:, 0:384]
    mx, nm, sm, es = b.ap[:, 0:2], b.ap[:, 2:4], b.ap[:, 4:6], b.ap[:, 8:10]
    if isinstance(bias, tuple):
        t = g.v_stt(S, bias[0], -bias[1], ps.ap[:, 0:384], ALU.mult, ALU.add, tps, *u.free)
    else:
        t = g.v_tt(S, ps.ap[:, 0:384], bias, ALU.add, tps, *u.free)
    g.ps.put(ps, t)
    t1 = g.dve.op(lambda e: e.tensor_reduce(mx[:, 0:1], S[:, 0:128], AX, ALU.max), t, *b.free)
    t1 = g.dve.op(lambda e: e.tensor_reduce(mx[:, 1:2], S[:, 128:384], AX, ALU.max), t, *b.free)
    if sink is not None:
        t1 = g.v_ts(mx, mx, sink, None, ALU.max, None, t1)
    t1 = g.v_ts(nm, mx, -scale, None, ALU.mult, None, t1)
    if sink is not None:
        t3 = g.v_ts(es, nm, sink, None, ALU.add, None, t1)
    g.a_act(S[:, 0:128], S[:, 0:128], ACT.Exp, t1, bias=nm[:, 0:1], scale=scale, accum_out=sm[:, 0:1])
    t2 = g.a_act(S[:, 128:384], S[:, 128:384], ACT.Exp, t1, bias=nm[:, 1:2], scale=scale, accum_out=sm[:, 1:2])
    if sink is not None:
        t2 = g.a_act(es, es, ACT.Exp, t3)
    return b, t2, sink is not None


def softmax3_end(g, state):
    b, t, sink = state
    sm, rs, es = b.ap[:, 4:6], b.ap[:, 6:8], b.ap[:, 8:10]
    if sink:
        t = g.v_tt(sm, sm, es, ALU.add, t)
    return rs, g.dve.op(lambda e: e.reciprocal(rs, sm), t)


def softmax3_scale(g, u, state):
    rs, t = softmax3_end(g, state)
    S = u.ap[:, 0:384]
    t1 = g.v_ts(S[:, 0:128], S[:, 0:128], rs[:, 0:1], None, ALU.mult, None, t)
    t2 = g.a_act(S[:, 128:384], S[:, 128:384], ACT.Copy, t, scale=rs[:, 1:2])
    g.cols.put(state[0], t1, t2)
    return [t1, t2]


def turn3(g, E, t):
    ps = g.ps.get()
    b = g.tmp.get()
    for i in range(3):
        tok = g.pe.op(lambda e, i=i: e.transpose(ps.ap[:, i * 128:(i + 1) * 128], E[:, i * 128:(i + 1) * 128],
                                                 g.C("ident", 0, 128)), *t, *ps.free)
    t1 = g.a_act(b.ap[:, 0:384], ps.ap[:, 0:384], ACT.Copy, tok, *b.free)
    g.ps.put(ps, t1)
    return b, tok, t1


def pipelined(n, stages, step):
    last = len(stages) - 1
    for h in range(n + last):
        for i in range(last, -1, -1):
            if 0 <= h - i < n:
                stages[i](h - i)
        step()


def mix_first(g, lay, mod):
    fa, ra = g.fa, g.ra
    base = [g.pe.last(), g.act.last(), g.dve.last(), g.t_mod[lay]]

    lam_init = 0.8 - 0.6 * math.exp(-0.3 * lay)
    pl = g.small[:, 512:520]
    lc = PARAM_COLS["lam"] + lay * 4
    q = g.par[0:64, lc:lc + 4]
    tl = g.v_tt(pl[0:64, 0:1], q[:, 0:1], q[:, 1:2], ALU.mult, *base)
    tl = g.v_tt(pl[0:64, 1:2], q[:, 2:3], q[:, 3:4], ALU.mult, *base)
    gsub = pl[:, 5:6]
    tsub = g.v_ts(gsub, g.P("da_g_subln", lay), 1.0 - lam_init, None, ALU.mult, None, *base)
    nlam = pl[:, 4:5]

    per_k = modulated(g, "g_pre_mix", lay, mod, 0, 8, base)

    merged, Gb = fa[:, 0:2048], fa[:, 2048:4096]
    qT, kT, V = fa[:, 4096:5120], fa[:, 5120:6144], fa[:, 6144:7168]
    SCz, ya = fa[:, 7168:8200], fa[:, 8200:9224]
    cfu, cfv = fa[:, 9224:10368], fa[:, 10368:11392]
    cc, krb = fa[:, 2048:3328], fa[:, 3328:3584]
    Zh = [ra[:, i * 2048:i * 2048 + 1024] for i in range(3)]
    Zl = [ra[:, i * 2048 + 1024:i * 2048 + 2048] for i in range(3)]
    ch, cl = ra[:, 6144:7424], ra[:, 7424:8704]

    cu = cfu.rearrange("p (c t) -> p c t", c=4)
    tcu = []
    t0 = g.dve.op(lambda e: e.memset(cu[:, :, 0:30], 0.0), *per_k)
    def conv_steps():
        for j in range(4):
            o = cfv[:, j * T:(j + 1) * T]
            t = g.v_ts(o, cu[:, j, 0:256], g.P("cf_conv", lay * 124 + j), g.P("cf_conv_b", lay * 4 + j),
                       ALU.mult, ALU.add, tcu[j], t0)
            for n in range(1, 31):
                t = g.v_stt(o, cu[:, j, n:n + 256], g.P("cf_conv", lay * 124 + 4 * n + j), o,
                            ALU.mult, ALU.add, t)
                if n % 6 == 0:
                    yield
            g.cf_tok = t

    conv = conv_steps()
    for j in range(4):
        (ps, tok), = g.proj("w_in", lay * 34 + CF0 + j, 8, 256, g.hh, g.hl, [], per_k=per_k)
        b = g.tmp.get()
        t1 = tanh_half(g, b.ap[:, 0:T], ps.ap[:, T:2 * T], tok, *b.free)
        t1 = g.v_ts(b.ap[:, 0:T], b.ap[:, 0:T], 0.5, 0.5, ALU.mult, ALU.add, t1)
        t2 = g.v_tt(cu[:, j, 30:286], ps.ap[:, 0:T], b.ap[:, 0:T], ALU.mult, tok, t1)
        g.ps.put(ps, t1, t2)
        g.tmp.put(b, t2)
        tcu.append(t2)
        if j:
            next(conv)

    ps = g.ps.get()
    tl = g.mm(ps.ap[:, 0:2], g.C("ones", 0, 128, 0, 64), pl[0:64, 0:2], after=[tl, *ps.free])
    tl = g.a_act(pl[:, 2:4], ps.ap[:, 0:2], ACT.Exp, tl, *base)
    g.ps.put(ps, tl)
    tl = g.v_tt(pl[:, 4:5], pl[:, 3:4], pl[:, 2:3], ALU.subtract, tl)
    tlam = g.v_ts(pl[:, 4:5], pl[:, 4:5], -lam_init, None, ALU.add, None, tl)

    tq = []
    for j in range(4):
        (ps, tok), = g.proj("w_in", lay * 34 + DA0 + j, 8, 256, g.hh, g.hl, [])
        dst = (qT if j < 2 else kT)[:, (j % 2) * 512:(j % 2) * 512 + 512]
        t = g.a_act(dst, ps.ap[:, :], ACT.Copy, tok, *per_k)
        g.ps.put(ps, t)
        tq.append(t)
        next(conv)
        next(conv)
    tv = []
    pv = [g.ps.get() for _ in range(2)]
    for j in range(2):
        w = g.weight("w_in", lay * 34 + DA0 + 4 + j)
        for tb in range(2):
            for k in range(8):
                xh = g.hh[:, k * T + tb * 128:k * T + tb * 128 + 128]
                xl = g.hl[:, k * T + tb * 128:k * T + tb * 128 + 128]
                wh, wl = w[0][:, k * 256:(k + 1) * 256], w[1][:, k * 256:(k + 1) * 256]
                tok = g.mm3(pv[tb].ap[:, j * 256:(j + 1) * 256], xh, xl, wh, wl, k == 0, k == 7, inc=k == 7,
                            after=[w[2], *pv[tb].free])
        g.done(w, tok)
        next(conv)
        next(conv)
    if lay == 0:
        tables(g)
    for tb in range(2):
        t = g.a_act(V[:, tb * 512:(tb + 1) * 512], pv[tb].ap[:, :], ACT.Copy, tok)
        g.ps.put(pv[tb], t)
        tv.append(t)

    st = {}

    def sc_proj():
        z = SCz.rearrange("p (c t) -> p c t", c=4)
        st["z0"] = g.dve.op(lambda e: e.memset(z[:, :, 0:2], 0.0), *per_k)
        for j in range(4):
            (ps, tok), = g.proj("w_in", lay * 34 + SCU0 + j, 8, 256, g.hh, g.hl, [])
            b = g.tmp.get()
            t = g.a_act(b.ap[:, 0:T], ps.ap[:, 0:T], ACT.Copy, tok, *b.free)
            t = g.v_tt(z[:, j, 2:258], ps.ap[:, T:2 * T], b.ap[:, 0:T], ALU.mult, tok, t)
            g.ps.put(ps, t)
            g.tmp.put(b, t)
            st["z"] = t
            yield
        for j in range(2):
            (ps, tok), = g.proj("w_in", lay * 34 + SCB0 + j, 8, 256, g.hh, g.hl, [])
            for i in range(2):
                c = 2 * j + i
                b = g.tmp.get()
                t = conv3(g, b.ap[:, 0:T], z[:, c, :], "sc_conv", lay * 12 + c, 4, [st["z0"], st["z"], *b.free])
                t = g.v_tt(b.ap[:, 0:T], b.ap[:, 0:T], ps.ap[:, i * T:(i + 1) * T], ALU.mult, tok, t)
                t1, t2 = g.split_act(g.xk(Zh[0], c), g.xk(Zl[0], c), b.ap[:, 0:T], t)
                g.tmp.put(b, t1, t2)
            g.ps.put(ps, t)
            st["yc"] = t2
            yield

    def mla_proj():
        for j in range(2):
            (ps, tok), = g.proj("w_in", lay * 34 + MLA0 + j, 8, 256, g.hh, g.hl, [])
            t = g.a_act(cc[:, j * 512:(j + 1) * 512], ps.ap[:, :], ACT.Copy, tok, *per_k)
            g.ps.put(ps, t)
            yield
        w = g.weight("w_mc", lay)
        ps = g.ps.get()
        tok = g.group(w, 8, 160, g.hh, g.hl, 0, ps.ap[:, 0:T], ps.free)
        tok = g.group(w, 8, 160, g.hh, g.hl, 64, ps.ap[0:96, T:2 * T], [], m=96)
        g.done(w, tok)
        t = g.a_act(cc[:, 1024:1280], ps.ap[:, 0:T], ACT.Copy, tok)
        kr = st["kr"] = krb
        t2 = g.a_act(kr[0:96, 0:T], ps.ap[0:96, T:2 * T], ACT.Copy, tok, *per_k)
        g.ps.put(ps, t2)
        st["cc"], st["krt"] = t, t2
        yield

    def mla_norms():
        tz = st["tz"] = []
        for a, n, dim, gn, gl in ((0, 3, 384, "mla_g_cq", 3), (3, 2, 256, "mla_g_ckv", 2)):
            src = cc[:, a * T:(a + n) * T]
            sqb = merged[:, a * T:(a + n) * T]
            v_, r_ = g.small[:, 0:256], g.small[:, 256:512]
            _, finish = g.stats_later(src, n, dim, 1e-6, r_, v_, sqb, [st["cc"], g.dve.last(), *per_k])
            yield
            t1 = finish()
            for k in range(n):
                s = cc[:, (a + k) * T:(a + k + 1) * T]
                t2 = g.v_stt(s, s, g.P(gn, lay * gl + k), r_, ALU.mult, ALU.mult, t1)
                _, t3 = g.split_act(g.xk(ch, a + k), g.xk(cl, a + k), s, t2, *per_k)
                tz.append(t3)
            yield

    def merge(branch, z, wo, tz, gate_saved=None):
        zh, zl = z
        for n in range(2):
            gated = []
            if branch == 2:
                for i in range(2):
                    (pg, tg), = g.proj("w_in", lay * 34 + GATE0 + 8 + 2 * n + i, 8, 256, g.hh, g.hl, [])
                    m = merged[:, (2 * n + i) * 512:(2 * n + i + 1) * 512]
                    gated.append(tanh_half(g, m, pg.ap[:, :], tg, *per_k, *st["tz"]))
                    g.ps.put(pg, gated[-1])
                    yield
            held = g.weight(wo, lay * 2 + n)
            for i in range(2):
                pair = 2 * n + i
                dst = merged[:, pair * 512:(pair + 1) * 512]
                ps = g.ps.get()
                for c in range(2):
                    tok = g.group(held, 4, 512, zh, zl, i * 256 + c * 128, ps.ap[:, c * T:(c + 1) * T],
                                  [*ps.free, *tz])
                if i == 1:
                    g.done(held, tok)
                if branch == 2:
                    b, sg, ts = None, dst, gated[i]
                elif gate_saved is None:
                    (pg, tg), = g.proj("w_in", lay * 34 + GATE0 + branch * 4 + pair, 8, 256, g.hh, g.hl, [])
                    b = g.tmp.get()
                    ts = tanh_half(g, b.ap[:, :], pg.ap[:, :], tg, *b.free)
                    g.ps.put(pg, ts)
                    sg = b.ap[:, :]
                else:
                    b, sg, ts = None, gate_saved[0][:, pair * 512:(pair + 1) * 512], gate_saved[1]
                if branch == 2:
                    t = g.v_stt(dst, sg, 1.0, ps.ap[:, :], ALU.add, ALU.mult, tok, ts, *per_k)
                    st[("merged", pair)] = t
                    if b:
                        g.tmp.put(b, t)
                else:
                    o = g.tmp.get()
                    t = g.v_stt(o.ap[:, :], sg, 1.0, ps.ap[:, :], ALU.add, ALU.mult, tok, ts, *o.free)
                    t2 = g.v_tt(dst, dst, o.ap[:, :], ALU.add, t, st[("merged", pair)])
                    st[("merged", pair)] = t2
                    if branch == 1:
                        for k in (2 * pair, 2 * pair + 1):
                            tm.append(split_half(g, g.xk(g.hh, k), g.xk(g.hl, k), g.xk(merged, k), t2, hfree)[1])
                    g.tmp.put(o, t2)
                    if b:
                        g.tmp.put(b, t)
                g.ps.put(ps, t)
                yield

    def gates_b():
        for j in range(4):
            (pg, tg), = g.proj("w_in", lay * 34 + GATE0 + 4 + j, 8, 256, g.hh, g.hl, [])
            st["gb"] = tanh_half(g, Gb[:, j * 512:(j + 1) * 512], pg.ap[:, :], tg, *per_k)
            g.ps.put(pg, st["gb"])
            yield

    def chain(*gens):
        for x in gens:
            yield from (x() if callable(x) else x)

    def alternate(a, b):
        its = [a, b]
        while its:
            it = its.pop(0)
            try:
                next(it)
                its.append(it)
            except StopIteration:
                continue
            yield

    def fill(it, other=iter(())):
        def step(n=1):
            next(other, None)
            for _ in range(n):
                next(it, None)
        return step

    def drain(it):
        for _ in it:
            pass

    work = chain(mla_proj, lambda: alternate(mla_norms(), sc_proj()),
                 lambda: merge(2, (Zh[0], Zl[0]), "sc_w_o", [st["yc"]]))
    step = fill(work, conv)
    tya, held = [], {}

    def da_scores(h):
        hs = []
        for m in range(2):
            ps = g.ps.get()
            p0 = 64 * m
            tok = g.mm(ps.ap[:, 0:128], qT[p0:p0 + 64, h * T:h * T + 128], kT[p0:p0 + 64, h * T:h * T + 128],
                       after=[*tq, *ps.free], inc=False)
            tok = g.mm(ps.ap[:, 128:384], qT[p0:p0 + 64, h * T + 128:h * T + 256], kT[p0:p0 + 64, h * T:h * T + 256])
            u = (g.tmp if m else g.sring).get()
            hs.append((u, softmax3(g, u, tok, ps, g.C("mask3", 0, 384), 0.125)))
        held[h] = hs

    def da_combine(h):
        (u1, st1), (u2, st2) = held[h]
        s1, s2 = u1.ap, u2.ap
        r1, t1 = softmax3_end(g, st1)
        r2, t2 = softmax3_end(g, st2)
        t2 = g.v_ts(r2, r2, nlam, None, ALU.mult, None, t2, tlam)
        for a, n, i in ((0, 128, 0), (128, 256, 1)):
            ta = g.a_act(s1[:, a:a + n], s1[:, a:a + n], ACT.Copy, t1, scale=r1[:, i:i + 1])
            ta = g.v_stt(s1[:, a:a + n], s2[:, a:a + n], r2[:, i:i + 1], s1[:, a:a + n], ALU.mult, ALU.add, ta, t2)
        g.cols.put(st1[0], ta)
        g.cols.put(st2[0], ta)
        g.tmp.put(u2, ta)
        held[h] = (u1, ta)

    def turn(h):
        u, ta = held[h]
        pt, tE, tpt = turn3(g, u.ap, [ta])
        g.sring.put(u, tE)
        held[h] = (pt, tpt)

    def da_values(h):
        pt, tpt = held.pop(h)
        ps = g.ps.get()
        g.mm(ps.ap[:, 0:256], V[:, h * 128:(h + 1) * 128], pt.ap[:, 0:256], last=False, after=[tpt, *tv, *ps.free],
             inc=False)
        tok = g.mm(ps.ap[:, 128:256], V[:, 512 + h * 128:512 + (h + 1) * 128], pt.ap[:, 256:384], first=False)
        g.tmp.put(pt, tok)
        t = g.a_act(ya[:, h * T:(h + 1) * T], ps.ap[:, 0:T], ACT.Copy, tok, *per_k)
        g.ps.put(ps, t)
        tya.append(t)

    def ya_norm(pair):
        w = slice(pair * 512, (pair + 1) * 512)
        end = norm_heads(g, ya[:, w], 1, 128, lambda c: gsub, g.C("ones", 0, 128),
                         [*tya[2 * pair:2 * pair + 2], tsub])
        yield
        t = end()
        _, t = g.split_act(Zh[1][:, w], Zl[1][:, w], ya[:, w], t, *per_k)
        st[("ya", pair)] = t
        yield

    pipelined(4, [da_scores, da_combine, turn, da_values], lambda: step(2))
    norms = [ya_norm(0), ya_norm(1)]
    for x in norms:
        next(x)
    drain(work)
    drain(norms[0])
    tz = st["tz"]

    mq, mk, mv = fa[:, 4096:6144], fa[:, 7168:9216], fa[:, 6144:7168]
    free = [g.pe.last(), g.dve.last(), g.act.last()]
    tmq = []
    cos, sin = g.trig[64:96, 0:256], g.trig[64:96, 256:512]

    def rope(dst, n, t, free):
        ps = g.ps.get()
        for i in range(n):
            tok = g.mm(ps.ap[0:96, i * T:(i + 1) * T], g.C("rot", 0, 96, 0, 96), dst[0:96, i * T:(i + 1) * T],
                       after=[t, *ps.free])
        b = g.tmp.get()
        o = b.ap[64:96, 0:n * T]
        d = dst[64:96, 0:n * T]
        cs, sn = (cos, sin) if n == 1 else (bc2(cos), bc2(sin))
        f = (lambda a: a) if n == 1 else v2
        t1 = g.v_tt(f(o), f(ps.ap[64:96, 0:n * T]), sn, ALU.mult, tok, *b.free, *g.trig_tok)
        g.ps.put(ps, t1)
        t2 = g.v_tt(f(d), f(d), cs, ALU.mult, tok)
        t3 = g.v_tt(d, d, o, ALU.add, t1, t2)
        g.tmp.put(b, t3)
        return t3

    turned = None
    for n in range(2):
        w = g.weight("mla_w_uq", lay * 2 + n)
        for i in range(2):
            ps = g.ps.get()
            for c in range(2):
                tok = g.group(w, 3, 384, ch, cl, (2 * i + c) * 96, ps.ap[0:96, c * T:(c + 1) * T],
                              [*ps.free, *tz], m=96)
            h = 4 * n + 2 * i
            t = g.a_act(mq[0:96, h * T:(h + 2) * T], ps.ap[0:96, :], ACT.Copy, tok, *free)
            g.ps.put(ps, t)
            if turned:
                tmq.append(rope(*turned))
            turned = (mq[:, h * T:(h + 2) * T], 2, t, free)
            next(conv, None)
        g.done(w, tok)
    drain(norms[1])
    tza = [st[("ya", 0)], st[("ya", 1)]]
    tmq.append(rope(*turned))
    t = rope(krb, 1, st["krt"], [])
    free = [g.pe.last(), g.dve.last(), g.act.last()]
    tkr = g.v_copy(mk[64:96, :].rearrange("p (h t) -> p h t", h=8),
                   krb[64:96, 0:T].unsqueeze(1).broadcast_to([32, 8, T]), t, *free)
    w = g.weight("mla_w_ukv", lay)
    c0h, c0l = ch[:, 3 * T:5 * T], cl[:, 3 * T:5 * T]
    tmk = []
    for i in range(4):
        ps = g.ps.get()
        for c in range(2):
            tok = g.group(w, 2, 1024, c0h, c0l, (2 * i + c) * 128, ps.ap[:, c * T:(c + 1) * T], ps.free)
        t = g.a_act(mk[0:64, 2 * i * T:(2 * i + 2) * T], ps.ap[0:64, :], ACT.Copy, tok, *free)
        g.ps.put(ps, t)
        tmk.append(t)
        next(conv, None)
    tmv = []
    for tb in range(2):
        ps = g.ps.get()
        for k in range(2):
            xh, xl = [c0[:, k * T + tb * 128:k * T + tb * 128 + 128] for c0 in (c0h, c0l)]
            wh, wl = [a[:, k * 1024:(k + 1) * 1024].rearrange("p (h c) -> p h c", h=8)[:, :, 64:128] for a in (w[0], w[1])]
            tok = g.mm3(ps.ap[:, :].rearrange("p (h c) -> p h c", h=8), xh, xl, wh, wl, k == 0, k == 1, inc=k == 1,
                        after=ps.free)
        t = g.a_act(mv[:, tb * 512:(tb + 1) * 512], ps.ap[:, :], ACT.Copy, tok, *free)
        g.ps.put(ps, t)
        tmv.append(t)
    g.done(w, tok)
    drain(conv)

    def cf_finish():
        sm, ve = g.small[:, 0:256], g.small[:, 256:512]
        b = g.tmp.get()
        t = g.dve.op(lambda e: e.tensor_reduce(b.ap[:, 0:T], cfv.rearrange("p (c t) -> p t c", c=4), AX, ALU.add),
                     g.cf_tok, *b.free)
        ps = g.ps.get()
        t = g.mm(ps.ap[:, 0:T], g.C("ones", 0, 128), b.ap[:, 0:T], after=[t, *ps.free])
        g.tmp.put(b, t)
        t = g.v_ts(sm, ps.ap[:, 0:T], 1.0 / 512, None, ALU.mult, None, t, g.act.last())
        g.ps.put(ps, t)
        for j in range(4):
            o = cfv[:, j * T:(j + 1) * T]
            t1 = g.v_tt(o, o, sm, ALU.subtract, t)
        yield
        t2, _ = g.stats(cfv, 4, 512, 1e-5, sm, ve, cfu, [t1, g.dve.last()])
        for j in range(4):
            o = cfv[:, j * T:(j + 1) * T]
            t3 = g.v_tt(o, o, sm, ALU.mult, t2)
            t3 = g.v_ts(o, o, g.P("cf_ln_g", lay * 4 + j), g.P("cf_ln_b", lay * 4 + j), ALU.mult, ALU.add, t3)
            u = cfu[:, j * T:(j + 1) * T]
            t4 = tanh_half(g, u, o, t3)
            t3 = g.v_stt(o, u, 1.0, o, ALU.add, ALU.mult, t4)
            _, t4 = split_half(g, g.xk(Zh[2], j), g.xk(Zl[2], j), o, t3, *per_k)
        st["cf"] = t4
        yield

    work = chain(lambda: alternate(gates_b(), cf_finish()), lambda: merge(0, (Zh[1], Zl[1]), "da_w_o", tza),
                 lambda: merge(3, (Zh[2], Zl[2]), "cf_w_o", [st["cf"]]))
    step = fill(work)
    tyb = []
    sc = 96 ** -0.5
    trn = [g.pe.last(), g.dve.last()]
    for u in g.sring.bufs:
        u.free = trn
    po = {}

    def mla_scores(h):
        ps = g.ps.get()
        g.mm(ps.ap[:, 0:128], mq[0:96, h * T:h * T + 128], mk[0:96, h * T:h * T + 128],
             after=[*tmq, *tmk, tkr, *ps.free], inc=False)
        tok = g.mm(ps.ap[:, 128:384], mq[0:96, h * T + 128:(h + 1) * T], mk[0:96, h * T:(h + 1) * T])
        u = g.sring.get()
        held[h] = (u, softmax3(g, u, tok, ps, g.C("mask3", 0, 384), sc))

    def scale(h):
        u, state = held[h]
        held[h] = (u, softmax3_scale(g, u, state))

    def mla_values(h):
        pt, tpt = held.pop(h)
        p0 = 64 * (h % 2)
        if h % 2 == 0:
            po[0] = g.ps.get()
        o = po[0]
        g.mm(o.ap[p0:p0 + 64, 0:256], mv[:, h * 64:(h + 1) * 64], pt.ap[:, 0:256], last=False,
             after=[tpt, *tmv, *o.free], inc=False)
        tok = g.mm(o.ap[p0:p0 + 64, 128:256], mv[:, 512 + h * 64:512 + (h + 1) * 64], pt.ap[:, 256:384], first=False)
        g.tmp.put(pt, tok)
        if h % 2:
            c = h // 2
            b = g.tmp.get()
            t = g.a_act(b.ap[:, 0:T], o.ap[:, 0:T], ACT.Copy, tok, *b.free)
            g.ps.put(o, t)
            t1, t2 = g.split_act(g.xk(Zh[0], c), g.xk(Zl[0], c), b.ap[:, 0:T], t, *trn)
            g.tmp.put(b, t1, t2)
            tyb.extend([t1, t2])

    pipelined(8, [mla_scores, scale, turn, mla_values], step)
    drain(work)
    tm, hfree = [], g.pe.last()
    drain(merge(1, (Zh[0], Zl[0]), "mla_w_o", tyb, gate_saved=(Gb, st["gb"])))

    y = fa[:, 4096:6144]
    g.dve.wait(g.pe.last())
    g.act.wait(g.pe.last(), g.dve.last())

    def mixed():
        for j in range(4):
            yield g.proj("w_mix_out", lay * 4 + j, 8, 256, g.hh, g.hl, [], per_k=tm)[0]

    return add_normed(g, y, lay, "g_post_mix", mod, 16, evac_y(g, y, mixed()))


def tables(g):
    pi = g.tmp.get()
    raw = pi.ap[64:96, 0:T].bitcast(I32)
    g.sp.dma(lambda e: e.dma_start(raw, g.args["positions"].broadcast_to([32, T])), g.s_p[0], *pi.free)
    g.n_p += 1
    p = pi.ap[64:96, T:2 * T]
    t = g.v_copy(p, raw, (g.s_p[0], 16))
    t = g.v_ts(p, p, g.C("inv", 0, 1, 64, 96), None, ALU.mult, None, t)
    b = g.tmp.get()
    n, z = b.ap[64:96, 0:T], b.ap[64:96, T:2 * T]
    g.dve.wait(*b.free)
    big = 12582912.0
    c1 = 6.28125
    c2 = float(np.float32(TWO_PI - c1))
    c3 = float(TWO_PI - c1 - float(np.float32(TWO_PI - c1)))
    for i, shift in ((0, 0.25), (1, 0.0)):
        t = g.v_ts(n, p, 1.0 / TWO_PI, shift, ALU.mult, ALU.add, t)
        t = g.v_ts(n, n, big, None, ALU.add, None, t)
        t = g.v_ts(n, n, big, None, ALU.subtract, None, t)
        t = g.v_stt(z, n, -c1, p, ALU.mult, ALU.add, t)
        t = g.v_stt(z, n, -c2, z, ALU.mult, ALU.add, t)
        t = g.v_stt(z, n, -c3, z, ALU.mult, ALU.add, t)
        if i == 0:
            t = g.v_ts(z, z, math.pi / 2, None, ALU.add, None, t)
        t = g.v_ts(z, z, 3.1415925, -3.1415925, ALU.min, ALU.max, t)
        t = g.a_act(g.trig[64:96, i * T:(i + 1) * T], z, ACT.Sin, t)
    g.tmp.put(pi, t)
    g.tmp.put(b, t)
    g.trig_tok = [t]


def second_norm(g, layer, which, after):
    v, r = g.small[:, 0:256], g.small[:, 256:512]
    after = after if isinstance(after, list) else [after]
    per_k = g.split_gain("norm_gains", (layer * 4 + which) * 8, 8, g.x, after, [g.pe.last()])
    sq = g.fa[:, 13056:15104]
    _, finish = g.stats_later(g.x[:, :], 8, D, 1e-6, r, v, sq, [*after, g.pe.last(), g.act.last(), g.dve.last()])
    return per_k, r, Later(finish)


def second_ffn(g, layer, half, tx):
    per_k, r, tr = second_norm(g, layer, 2 * half, tx)

    def chunk(j, ps, tok, yh, yl, free):
        tr.get()
        a = g.tmp.get()
        t = g.v_tt(v2(a.ap[:, :]), v2(ps.ap[:, :]), bc2(r), ALU.mult, tok, tr.get(), *a.free)
        g.ps.put(ps, t)
        b = g.tmp.get()
        t1 = g.a_act(b.ap[:, 0:T], a.ap[:, 0:T], ACT.Silu, t, *b.free)
        t2 = g.v_tt(b.ap[:, T:2 * T], b.ap[:, 0:T], a.ap[:, T:2 * T], ALU.mult, t1)
        g.tmp.put(a, t2)
        t3, t4 = g.split_act(yh, yl, b.ap[:, T:2 * T], t2, *free)
        g.tmp.put(b, t3, t4)
        return t4

    i = layer * 2 + half
    acc = ffn(g, "w_gu", i * 22, "w_dn", i * 11, per_k, chunk)
    la = g.act.last()
    tx = []
    for n, b in enumerate(acc):
        s = g.x[:, n * 512:(n + 1) * 512]
        tx.append(g.v_stt(s, b.ap[:, :], 0.5, s, ALU.mult, ALU.add, b.ready, la))
        g.ps.put(b, tx[-1])
    return tx


def out_add(g, name, n0, zh, zl, tz):
    la = g.act.last()
    tx = []
    for j in range(4):
        (ps, tok), = g.proj(name, n0 + j, 8, 256, zh, zl, [], per_k=tz)
        s = g.x[:, j * 512:(j + 1) * 512]
        tx.append(g.v_tt(s, s, ps.ap[:, :], ALU.add, tok, la))
        g.ps.put(ps, tx[-1])
    return tx


def evac_scaled(g, out, ps, tok, r, tr, *after):
    t = g.v_tt(v2(out), v2(ps.ap[:, :]), bc2(r), ALU.mult, tok, tr.get(), *after)
    g.ps.put(ps, t)
    return t


def token_factor(g, r, tr):
    rc = g.small[:, 520:522]
    ps = g.ps.get()
    for tb in range(2):
        tok = g.pe.op(lambda e, tb=tb: e.transpose(ps.ap[:, tb * 128:(tb + 1) * 128], r[:, tb * 128:(tb + 1) * 128],
                                                   g.C("ident", 0, 128)), tr.get(), *ps.free)
    for tb in range(2):
        t = g.v_copy(rc[:, tb:tb + 1], ps.ap[:, tb * 128:tb * 128 + 1], tok)
    g.ps.put(ps, t)
    return rc, t


def token_major(g, name, ns, width, j0, banks, per_k):
    for j, n in enumerate(ns, j0):
        w = g.weight(name, n)
        for tb in range(2):
            ps = banks[tb]
            for k in range(8):
                a = k * T + tb * 128
                tok = g.mm3(ps.ap[:, j * width:(j + 1) * width], g.hh[:, a:a + 128], g.hl[:, a:a + 128],
                            w[0][:, k * width:(k + 1) * width], w[1][:, k * width:(k + 1) * width],
                            k == 0, k == 7, inc=k == 7, after=[w[2], *ps.free, per_k[k]])
        g.done(w, tok)
    return tok


def hgrn(g, layer, j, tx):
    per_k, r, tr = second_norm(g, layer, 1, tx)
    fa = g.fa
    G = [None, None]
    G[0] = [fa[:, 0:1024], fa[:, 1024:2048], fa[:, 2048:3072], fa[:, 3072:4096]]
    G[1] = [fa[:, 4096:5120], fa[:, 5120:6144], fa[:, 6144:7168], fa[:, 7168:8192]]
    Qa, Ka = fa[:, 8192:9216], fa[:, 9216:10240]
    DD = [fa[:, 10240:11264], g.attn[:, 128:1152]]
    AT = fa[:, 11264:12800]
    A32 = fa[:, 12800:13056]
    o = fa[:, 13056:15104]
    base = [g.pe.last(), g.act.last(), g.dve.last()]
    L = g.attn[:, 0:96]
    lb, oml, zf = L[:, 64:72], L[:, 72:80], L[:, 80:88]
    if layer == 0:
        tl = g.dve.op(lambda e: e.memset(lb, 0.0), *base)
        tl = g.dve.op(lambda e: e.memset(oml, 1.0), *base)
        tl = g.dve.op(lambda e: e.memset(zf, 1.0), *base)
    else:
        c = PARAM_COLS["hg_lb"]
        raw = g.par[:, c:c + 32]
        mx, s = L[:, 88:96], L[:, 32:40]
        t = g.dve.op(lambda e: e.tensor_reduce(mx, raw.rearrange("p (l c) -> p c l", l=4), AX, ALU.max), *base)
        t = g.v_tt(L[:, 0:32].rearrange("p (l c) -> p l c", l=4), raw.rearrange("p (l c) -> p l c", l=4),
                   mx.unsqueeze(1).broadcast_to([128, 4, 8]), ALU.subtract, t)
        t = g.a_act(L[:, 0:32], L[:, 0:32], ACT.Exp, t)
        t = g.v_tt(s, L[:, 8:16], L[:, 16:24], ALU.add, t)
        t = g.v_tt(s, s, L[:, 24:32], ALU.add, t) if layer == 3 else t
        t = g.v_tt(L[:, 40:48], s, L[:, 0:8], ALU.add, t)
        t = g.dve.op(lambda e: e.reciprocal(L[:, 48:56], L[:, 40:48]), t)
        t = g.v_tt(lb, s, L[:, 48:56], ALU.mult, t)
        t = g.v_tt(oml, L[:, 0:8], L[:, 48:56], ALU.mult, t)
        tl = g.v_ts(zf, lb, 2.0 ** -60, None, ALU.is_lt, None, t)
    t_at = g.pool.op(lambda e: e.memset(AT, 0.0), *base)
    AT4 = AT.rearrange("p (h c) -> p h c", h=4)
    st = [{}, {}]
    tO = []

    def project(gr):
        q, k, b, V = G[gr]
        x = st[gr]
        x["q"], x["b"], x["v"] = [], [], []
        for n in range(2):
            (ps, tok), = g.proj("hg_in", j * 16 + gr * 2 + n, 8, 256, g.hh, g.hl, [], per_k=per_k)
            a = g.tmp.get()
            t = evac_scaled(g, a.ap[:, :], ps, tok, r, tr, *a.free)
            u = g.tmp.get()
            t = tanh_half(g, u.ap[:, :], a.ap[:, :], t, *u.free)
            t = g.v_stt(q[:, n * 512:(n + 1) * 512], u.ap[:, :], 1.0, a.ap[:, :], ALU.add, ALU.mult, t, *base)
            g.tmp.put(a, t)
            g.tmp.put(u, t)
            x["q"].append(t)
            yield
        for n in range(2):
            (ps, tok), = g.proj("hg_in", j * 16 + 4 + gr * 2 + n, 8, 256, g.hh, g.hl, [], per_k=per_k)
            f = g.tmp.get()
            t = evac_scaled(g, f.ap[:, :], ps, tok, r, tr, *f.free)
            e_ = g.tmp.get()
            tc = g.v_ts(e_.ap[:, :], f.ap[:, :], -80.0, None, ALU.max, None, t, *e_.free)
            t = g.a_act(e_.ap[:, :], e_.ap[:, :], ACT.Exp, tc, scale=-1.0)
            tf = g.v_ts(f.ap[:, :], f.ap[:, :], 60 * math.log(2.0), 0.0, ALU.add, ALU.min, tc)
            s = g.tmp.get()
            ts = g.v_ts(s.ap[:, :], e_.ap[:, :], 1.0, None, ALU.add, None, t, *s.free)
            ts = g.dve.op(lambda e, s=s: e.reciprocal(s.ap[:, :], s.ap[:, :]), ts)
            for c in range(2):
                hd = gr * 4 + n * 2 + c
                w = slice(c * T, (c + 1) * T)
                kk = k[:, (2 * n + c) * T:(2 * n + c + 1) * T]
                t = g.v_stt(kk, e_.ap[:, w], oml[:, hd:hd + 1], s.ap[:, w], ALU.mult, ALU.mult, ts, tl, *base)
                tu = g.v_ts(s.ap[:, w], s.ap[:, w], oml[:, hd:hd + 1], lb[:, hd:hd + 1], ALU.mult, ALU.add, t)
            tu = g.v_ts(s.ap[:, :], s.ap[:, :], 2.0 ** -60, None, ALU.max, None, tu)
            tu = g.a_act(s.ap[:, :], s.ap[:, :], ACT.Ln, tu)
            for c in range(2):
                hd = gr * 4 + n * 2 + c
                w = slice(c * T, (c + 1) * T)
                tw = g.v_stt(f.ap[:, w], f.ap[:, w], zf[:, hd:hd + 1], s.ap[:, w], ALU.mult, ALU.add, tu, tf)
                bb = b[:, (2 * n + c) * T:(2 * n + c + 1) * T]
                tw = g.dve.op(lambda e, bb=bb, ff=f.ap[:, w]: e.tensor_tensor_scan(
                    bb, g.C("rst", 0, 256), ff, 0.0, ALU.mult, ALU.add), tw, *base)
            for x_ in (f, e_, s):
                g.tmp.put(x_, tw, t)
            x["b"].append(tw)
            x["k"] = t
            yield
        rc, trc = token_factor(g, r, tr) if gr == 0 else st[0]["rc"]
        x["rc"] = (rc, trc)
        banks = [g.ps.get() for _ in range(2)]
        for n in range(2):
            tok = token_major(g, "hg_in", [j * 16 + 8 + gr * 2 + n], 256, n, banks, per_k)
            if n == 0:
                yield
        for tb in range(2):
            t = g.v_ts(V[:, tb * 512:(tb + 1) * 512], banks[tb].ap[:, :], rc[:, tb:tb + 1], None, ALU.mult, None,
                       tok, trc, *base)
            g.ps.put(banks[tb], t)
            x["v"].append(t)
        yield

    def v3(a, n):
        return a.rearrange("p (n m) -> p n m", m=n)

    def scan(gr):
        nonlocal t_at
        q, k, b, V = G[gr]
        x = st[gr]
        tb_, tq = x["b"], x["q"]
        free = [g.pe.last(), g.act.last(), g.dve.last()]
        b64 = v3(b, 64)
        last = b64[:, :, 63:64].broadcast_to([128, 16, 64])
        t = g.a_act(Qa, b, ACT.Exp, *tb_, *free)
        tQ = g.v_tt(Qa, Qa, q, ALU.mult, t, *tq)
        t = g.p_tt(v3(Ka, 64), last, b64, ALU.subtract, *free, *tb_)
        t = g.a_act(Ka, Ka, ACT.Exp, t)
        tK = g.p_tt(Ka, Ka, k, ALU.mult, t, x["k"])
        eb = g.cols.get()
        tE = g.a_act(eb.ap[:, 0:16].unsqueeze(2), b64[:, :, 63:64], ACT.Exp, *tb_, *eb.free)
        levels = (32, 16, 8, 4, 2, 1, 0)
        made = {}
        dfree = [list(free), list(free)]

        def make(lv):
            m = levels[lv]
            if m == 0:
                made[lv] = (k, q, [x["k"], *tq])
                return
            Dv = DD[lv % 2]
            b3, d3, qq, kk = v3(b, 2 * m), v3(Dv, 2 * m), v3(q, 2 * m), v3(k, 2 * m)
            n = 1024 // (2 * m)
            ref = b3[:, :, m - 1:m].broadcast_to([128, n, m])
            t1 = g.v_tt(d3[:, :, m:2 * m], b3[:, :, m:2 * m], ref, ALU.subtract, *dfree[lv % 2], *tb_)
            t2 = g.p_tt(d3[:, :, 0:m], ref, b3[:, :, 0:m], ALU.subtract, *dfree[lv % 2], *tb_)
            t = g.a_act(Dv, Dv, ACT.Exp, t1, t2)
            made[lv] = (Dv, d3, qq, kk, m, t)

        def finish_make(lv):
            if levels[lv] == 0:
                return
            Dv, d3, qq, kk, m, t = made[lv]
            t1 = g.v_tt(d3[:, :, m:2 * m], d3[:, :, m:2 * m], qq[:, :, m:2 * m], ALU.mult, t)
            t2 = g.p_tt(d3[:, :, 0:m], d3[:, :, 0:m], kk[:, :, 0:m], ALU.mult, t)
            made[lv] = (Dv, Dv, [t1, t2])

        make(0)
        make(1)
        yield
        ps = g.ps.get()
        for h in range(4):
            for sb in range(2):
                a = h * T + sb * 128
                tok = g.mm(ps.ap[0:64, h * 128 + sb * 64:h * 128 + sb * 64 + 64], Ka[:, a:a + 64], Qa[:, a + 64:a + 128],
                           after=[tQ, tK, *ps.free], inc=h == 3)
        tA = []
        for sb in range(2):
            t = g.a_act(AT4[0:64, :, sb * 256 + 64:sb * 256 + 128],
                        ps.ap[0:64, :].rearrange("p (h s t) -> p h s t", h=4, s=2)[:, :, sb, :], ACT.Copy, tok, t_at)
            tA.append(t)
        g.ps.put(ps, t)
        q3 = v3(Qa, 64).rearrange("p (h c) m -> p h c m", c=4)
        k3 = v3(Ka, 64).rearrange("p (h c) m -> p h c m", c=4)
        e4 = eb.ap[:, 0:16].rearrange("p (h c) -> p h c", c=4)
        t1 = g.v_tt(q3[:, :, 3, :], q3[:, :, 3, :], e4[:, :, 2:3].broadcast_to([128, 4, 64]), ALU.mult, tok, tE)
        t2 = g.v_tt(k3[:, :, 0, :], k3[:, :, 0, :], e4[:, :, 1:2].broadcast_to([128, 4, 64]), ALU.mult, tok, tE)
        g.cols.put(eb, t2)
        finish_make(0)
        yield
        ps = g.ps.get()
        for h in range(4):
            tok = g.mm(ps.ap[:, h * 128:(h + 1) * 128], Ka[:, h * T:h * T + 128], Qa[:, h * T + 128:h * T + 256],
                       after=[t1, t2, *ps.free], inc=h == 3)
        t = g.a_act(AT4[:, :, 128:256], ps.ap[:, :].rearrange("p (h t) -> p h t", h=4), ACT.Copy, tok, t_at)
        tA.append(t)
        g.ps.put(ps, t)
        tacc = None
        for lv, m in enumerate(levels):
            lhs, rhs, ready = made.pop(lv)
            ps = g.ps.get()
            if m == 32:
                for h in range(4):
                    for c in range(4):
                        a = h * T + c * 64
                        p0 = 64 * (c % 2)
                        col = h * 64 + (c // 2) * 32
                        tok = g.mm(ps.ap[p0:p0 + 32, col:col + 32], lhs[:, a:a + 32], rhs[:, a + 32:a + 64],
                                   after=[*ready, *ps.free], inc=h == 3 and c == 3)
            else:
                for h in range(4):
                    for jb in range(8):
                        a = h * T + jb * 32
                        p0 = 32 * (jb % 4)
                        col = h * 64 + (jb // 4) * 32
                        tok = g.mm(ps.ap[p0:p0 + 32, col:col + 32], lhs[:, a:a + 32], rhs[:, a:a + 32],
                                   after=[*ready, *ps.free], inc=h == 3 and jb == 7)
            dfree[lv % 2] = [tok]
            if lv + 1 < len(levels):
                finish_make(lv + 1)
            if lv + 2 < len(levels):
                make(lv + 2)
            if m == 32:
                for c in range(2):
                    p0 = 64 * c
                    for sb in range(2):
                        t = g.a_act(AT4[p0:p0 + 32, :, sb * 256 + p0 + 32:sb * 256 + p0 + 64],
                                    ps.ap[p0:p0 + 32, 0:256].rearrange("p (h s t) -> p h s t", h=4, s=2)[:, :, sb, :],
                                    ACT.Copy, tok, t_at)
                        tA.append(t)
                g.ps.put(ps, t)
            else:
                mask = g.C("lev", (lv - 1) * 32, 32).unsqueeze(1).broadcast_to([128, 8, 32])
                pv = ps.ap[:, 0:256].rearrange("p (n t) -> p n t", t=32)
                av = A32.rearrange("p (n t) -> p n t", t=32)
                if lv == 1:
                    tacc = g.v_tt(av, pv, mask, ALU.mult, tok, *tA, *free)
                    g.ps.put(ps, tacc)
                else:
                    a = g.tmp.get()
                    t = g.v_tt(a.ap[:, 0:256].rearrange("p (n t) -> p n t", t=32), pv, mask, ALU.mult, tok, *a.free)
                    g.ps.put(ps, t)
                    tacc = g.v_tt(A32, A32, a.ap[:, 0:256], ALU.add, t, tacc)
                    g.tmp.put(a, tacc)
            yield
        for c in range(4):
            p0 = 32 * c
            for sb in range(2):
                t = g.a_act(AT4[p0:p0 + 32, :, sb * 256 + p0:sb * 256 + p0 + 32],
                            A32[p0:p0 + 32, :].rearrange("p (h s t) -> p h s t", h=4, s=2)[:, :, sb, :],
                            ACT.Copy, tacc, t_at)
        tA.append(t)
        yield
        for hp in range(2):
            ps = g.ps.get()
            for c in range(2):
                h = 2 * hp + c
                g.mm(ps.ap[:, c * T:c * T + 256], V[:, h * 128:(h + 1) * 128], AT4[:, h, 0:256], last=False,
                     after=[*tA, *x["v"], *ps.free], inc=False)
                tok = g.mm(ps.ap[:, c * T + 128:c * T + 256], V[:, 512 + h * 128:512 + (h + 1) * 128],
                           AT4[:, h, 256:384], first=False)
            hh = gr * 4 + 2 * hp
            t = g.v_ts(o[:, hh * T:(hh + 2) * T], ps.ap[:, :], 0.5, None, ALU.mult, None, tok, *base)
            g.ps.put(ps, t)
            tO.append(t)
        t_at = tok
        yield

    og = fa[:, 0:2048]
    tg = []

    def gates():
        dead = [g.pe.last(), g.act.last(), g.dve.last(), g.pool.last()]
        for n in range(4):
            (ps, tok), = g.proj("hg_in", j * 16 + 12 + n, 8, 256, g.hh, g.hl, [])
            s = og[:, n * 512:(n + 1) * 512]
            tg.append(silu_gate(g, s, evac_scaled(g, s, ps, tok, r, tr, *dead)))
            yield

    zh, zl = g.ra[:, 0:2048], g.ra[:, 2048:4096]
    tz = []

    for _ in project(0):
        pass
    g.share = False
    other = project(1)
    for i, _ in enumerate(scan(0)):
        next(other, None)
    for _ in other:
        pass
    other = gates()
    for i, _ in enumerate(scan(1)):
        if i % 4 == 2:
            next(other, None)
    norms = HeadNorms(g, 128, g.C("ones", 0, 128), fa[:, 2048:4096], fa[:, 4096:6144], g.pe.last(), g.act.last(),
                      g.dve.last(), g.pool.last())
    for n in range(4):
        tO[n] = norms.begin(o[:, n * 512:(n + 1) * 512], None, tO[n])
    g.share = True
    while len(tg) < 3:
        next(other)
    norms.products()
    factors = list(norms.factors())
    next(other)
    for n, (v, t) in enumerate(factors):
        w = slice(n * 512, (n + 1) * 512)
        t1 = g.v_stt(o[:, w], o[:, w], g.P("hg_g_norm", j), og[:, w], ALU.mult, ALU.mult, tg[n], tO[n])
        t = g.v_tt(o[:, w], o[:, w], v, ALU.mult, t1, t)
        t1, t2 = split_half(g, zh[:, w], zl[:, w], o[:, w], t, *base)
        tz.extend([t2, t2])
    return out_add(g, "hg_out", j * 4, zh, zl, tz)


def silu_gate(g, og, t):
    u = g.tmp.get()
    t = tanh_half(g, u.ap[:, :], og, t, *u.free)
    t = g.v_stt(og, u.ap[:, :], 1.0, og, ALU.add, ALU.mult, t)
    g.tmp.put(u, t)
    return t


def norm_heads(g, s, per, dim, gcol, ones, after):
    sq = g.tmp.get()
    t = g.a_act(sq.ap[:, :], s, ACT.Square, *after, *sq.free)

    def finish():
        n = 512 // per
        ps = g.ps.get()
        for c in range(2):
            if per == 1:
                tok = g.mm(ps.ap[:, c * T:(c + 1) * T], ones, sq.ap[:, c * T:(c + 1) * T], after=[t, *ps.free])
            else:
                tok = g.mm(ps.ap[:, 0:T], ones, sq.ap[:, c * T:(c + 1) * T], first=c == 0, last=c == 1,
                           after=[t, *ps.free])
        y, z = g.tmp.get(), g.tmp.get()
        v, yy, zz = sq.ap[:, 0:n], y.ap[:, 0:n], z.ap[:, 0:n]
        t1 = g.v_ts(v, ps.ap[:, 0:n], 1.0 / dim, 1e-6, ALU.mult, ALU.add, tok)
        g.ps.put(ps, t1)
        t2 = g.a_act(yy, v, ACT.Ln, t1, *y.free)
        t2 = g.a_act(yy, yy, ACT.Exp, t2, scale=-0.5)
        t3 = g.v_tt(zz, yy, yy, ALU.mult, t2, *z.free)
        t3 = g.v_stt(zz, zz, -0.5, v, ALU.mult, ALU.mult, t3)
        t3 = g.v_stt(zz, zz, 1.5, yy, ALU.add, ALU.mult, t3)
        for c in range(2):
            a = s[:, c * T:(c + 1) * T]
            r = zz[:, (c * T) % n:(c * T) % n + T]
            t4 = g.v_stt(a, a, gcol(c), r, ALU.mult, ALU.mult, t3)
        for x in (sq, y, z):
            g.tmp.put(x, t4, t2)
        return t4

    return finish


class HeadNorms:

    def __init__(self, g, dim, ones, sq, y, *after):
        self.g, self.dim, self.ones, self.after, self.items = g, dim, ones, after, []
        self.sq, self.y = sq, y

    def begin(self, s, gain, *after):
        i = len(self.items)
        v = self.sq[:, i * 512:(i + 1) * 512]
        t = self.g.a_act(v, s, ACT.Square, *after, *self.after)
        self.items.append([s, gain, v, self.y[:, i * 512:(i + 1) * 512], t])
        return t

    def products(self):
        g = self.g
        for x in self.items:
            ps = g.ps.get()
            for c in range(2):
                tok = g.mm(ps.ap[:, c * T:(c + 1) * T], self.ones, x[2][:, c * T:(c + 1) * T], after=[x[4], *ps.free])
            x[4] = g.v_ts(x[2], ps.ap[:, :], 1.0 / self.dim, 1e-6, ALU.mult, ALU.add, tok)
            g.ps.put(ps, x[4])
            x[4] = g.a_act(x[3], x[2], ACT.Ln, x[4], *self.after)

    def factors(self):
        g = self.g
        for x in self.items:
            x[4] = g.a_act(x[3], x[3], ACT.Exp, x[4], scale=-0.5)
        for s, gain, v, y, t in self.items:
            b = g.tmp.get()
            t1 = g.a_act(b.ap[:, :], y, ACT.Square, t, *b.free)
            t1 = g.v_stt(v, b.ap[:, :], -0.5, v, ALU.mult, ALU.mult, t1)
            g.tmp.put(b, t1)
            yield v, g.v_stt(v, v, 1.5, y, ALU.add, ALU.mult, t1)

    def finish(self):
        for x, (v, t) in zip(self.items, self.factors()):
            yield self.g.v_stt(x[0], x[0], x[1], v, ALU.mult, ALU.mult, t)


def mlstm(g, tx):
    per_k, r, tr = second_norm(g, 1, 1, tx)
    fa = g.fa
    q, k = fa[:, 0:1024], fa[:, 1024:2048]
    V = fa[:, 2048:4096]
    h_ = fa[:, 4096:6144]
    rows = fa[0:4, 6144:8192]
    B = [[fa[:, 8192 + i * 1280:8192 + i * 1280 + 384], fa[:, 8576 + i * 1280:8576 + i * 1280 + 384],
          fa[:, 8960 + i * 1280:8960 + i * 1280 + 256], fa[:, 9216 + i * 1280:9216 + i * 1280 + 256]] for i in range(2)]
    og = fa[:, 10752:12800]
    base = [g.pe.last(), g.act.last(), g.dve.last()]
    tq = []

    def project(n):
        (ps, tok), = g.proj("ml_in", n, 8, 256, g.hh, g.hl, [], per_k=per_k)
        dst = (q if n < 2 else k)[:, (n % 2) * 512:(n % 2) * 512 + 512]
        tq.append(evac_scaled(g, dst, ps, tok, r, tr, *base))

    project(0)
    ps = g.ps.get()
    c0 = PARAM_COLS["w_if"]
    for i in range(2):
        for kk in range(8):
            w = g.par[:, c0 + kk * 8 + i * 4:c0 + kk * 8 + i * 4 + 4]
            out = ps.ap[0:4, i * T:(i + 1) * T]
            g.mm(out, w, g.xk(g.hh, kk).bitcast(F32), first=kk == 0, last=False, inc=False, after=[per_k[kk], *ps.free])
            tok = g.mm(out, w, g.xk(g.hl, kk).bitcast(F32), first=False, last=kk == 7)
    G, X1, Lc, A, CM, NM = [rows[:, i * T:(i + 1) * T] for i in (0, 2, 3, 4, 5, 6)]
    ig, fg = rows[:, 0:T], rows[:, T:2 * T]
    t = g.v_tt(v2(rows[:, 0:512]), v2(ps.ap[0:4, :]), bc2(r[0:4, :]), ALU.mult, tok, tr.get(), *base)
    g.ps.put(ps, t)
    for i, a in enumerate((ig, fg)):
        t = g.v_ts(a, a, g.P("ml_b_if", i, 4), None, ALU.add, None, t)
    t = g.a_act(rows[:, 0:512], rows[:, 0:512], ACT.Tanh, t, scale=1.0 / 15)
    t = g.v_ts(rows[:, 0:512], rows[:, 0:512], 15.0, None, ALU.mult, None, t)
    t = g.a_act(X1, fg, ACT.Exp, t, scale=-1.0)
    t = g.v_ts(X1, X1, 1.0, None, ALU.add, None, t)
    t = g.a_act(X1, X1, ACT.Ln, t)
    t = g.dve.op(lambda e: e.tensor_tensor_scan(Lc, g.C("ones", 0, 1, 0, 4).broadcast_to([4, T]), X1, 0.0,
                                                ALU.mult, ALU.add), t)
    t = g.v_tt(A, ig, Lc, ALU.add, t)
    t = g.dve.op(lambda e: e.tensor_tensor_scan(CM, A, A, 0.0, ALU.max, ALU.max), t)
    trow = g.v_tt(NM, Lc, CM, ALU.subtract, t)
    for n in range(1, 4):
        project(n)
    rc, trc = token_factor(g, r, tr)
    ac = g.small[:, 528:536]
    ps = g.ps.get()
    for sb in range(2):
        tok = g.pe.op(lambda e, sb=sb, ps=ps: e.transpose(ps.ap[:, sb * 4:sb * 4 + 4], A[:, sb * 128:(sb + 1) * 128],
                                                          g.C("ident", 0, 4, 0, 4)), trow, *ps.free)
    tac = g.v_copy(ac, ps.ap[:, 0:8], tok)
    g.ps.put(ps, tac)
    free = [list(base), list(base)]
    held = {}

    def weights(h):
        W, AT, em, dn = B[h % 2]
        ps = g.ps.get()
        s_ = g.C("ident", h, 1, 0, 4).broadcast_to([4, 128])
        tok = g.mm(ps.ap[:, 0:T], s_, CM, after=[tac, *ps.free])
        tok = g.mm(ps.ap[:, T:2 * T], s_, NM)
        t = g.v_ts(W[:, 0:256], ps.ap[:, 0:256], ac[:, h:h + 1], 0.0, ALU.subtract, ALU.max, tok, *free[h % 2])
        t = g.v_ts(W[:, 256:384], ps.ap[:, 128:256], ac[:, 4 + h:5 + h], 0.0, ALU.subtract, ALU.max, tok)
        te = g.a_act(em, ps.ap[:, T:2 * T], ACT.Exp, tok, t, *free[h % 2])
        g.ps.put(ps, t, te)
        t = g.a_act(W, W, ACT.Exp, t, scale=-1.0)
        for a in (0, 256):
            t1 = g.v_tt(W[:, a:a + 128], W[:, a:a + 128], g.C("maskT", 0, 128), ALU.mult, t)
        held[h] = (t1, te)

    weights(0)
    tv = []
    for n in range(2):
        banks = [g.ps.get() for _ in range(2)]
        tok = token_major(g, "ml_in", [4 + 2 * n, 5 + 2 * n], 256, 0, banks, per_k)
        for tb in range(2):
            t = g.v_ts(V[:, tb * 1024 + n * 512:tb * 1024 + (n + 1) * 512], banks[tb].ap[:, :], rc[:, tb:tb + 1], None,
                       ALU.mult, None, tok, trc, *base)
            g.ps.put(banks[tb], t)
            tv.append(t)
    tgate = []

    def gates():
        for n in range(4):
            (ps, tok), = g.proj("ml_in", 8 + n, 8, 256, g.hh, g.hl, [])
            s = og[:, n * 512:(n + 1) * 512]
            tgate.append(tanh_half(g, s, s, evac_scaled(g, s, ps, tok, r, tr, *base)))
            yield

    def scores(h):
        W, AT, em, dn = B[h % 2]
        tw, te = held[h]
        ps = g.ps.get()
        tok = g.mm(ps.ap[:, 0:256], k[:, h * T:h * T + 128], q[:, h * T:(h + 1) * T], after=[*tq, *ps.free])
        tok = g.mm(ps.ap[:, 256:384], k[:, h * T + 128:(h + 1) * T], q[:, h * T + 128:(h + 1) * T])
        t = g.v_stt(AT, ps.ap[:, 0:384], 128 ** -0.5, W, ALU.mult, ALU.mult, tok, tw, *free[h % 2])
        g.ps.put(ps, t)
        if h < 3:
            weights(h + 1)
        held[h] = (t, te)

    def values(h):
        W, AT, em, dn = B[h % 2]
        ta, te = held[h]
        ps, pd = g.ps.get(), g.ps.get()
        g.mm(pd.ap[:, 0:256], g.C("ones", 0, 128), AT[:, 0:256], last=False, inc=False, after=[ta, *pd.free])
        tokd = g.mm(pd.ap[:, 128:256], g.C("ones", 0, 128), AT[:, 256:384], first=False)
        for c in range(2):
            a = h * 256 + c * 128
            g.mm(ps.ap[:, c * T:c * T + 256], V[:, a:a + 128], AT[:, 0:256], last=False, inc=False,
                 after=[*tv, *ps.free])
            tok = g.mm(ps.ap[:, c * T + 128:c * T + 256], V[:, 1024 + a:1024 + a + 128], AT[:, 256:384], first=False)
        t1 = g.a_act(dn, pd.ap[:, 0:256], ACT.Abs, tokd, *free[h % 2])
        g.ps.put(pd, t1)
        t = g.v_tt(dn, dn, em, ALU.max, t1, te)
        t = g.dve.op(lambda e: e.reciprocal(dn, dn), t)
        s = h_[:, 2 * h * T:(2 * h + 2) * T]
        t = g.v_tt(v2(s), v2(ps.ap[:, :]), bc2(dn), ALU.mult, t, tok, *base)
        g.ps.put(ps, t)
        free[h % 2] = [tok, t, t1]
        held[h] = norm_heads(g, s, 2, 256, lambda c: g.P("ml_norm", 2 * h + c), g.C("ones", 0, 128), [t])

    zh, zl = g.ra[:, 0:2048], g.ra[:, 2048:4096]
    tz = []

    def tail(h):
        w = slice(h * 512, (h + 1) * 512)
        t = g.v_stt(h_[:, w], og[:, w], 1.0, h_[:, w], ALU.add, ALU.mult, tgate[h], held.pop(h)())
        t1, t2 = split_half(g, zh[:, w], zl[:, w], h_[:, w], t, *base)
        tz.extend([t2, t2])

    work = gates()
    turn = [0]

    def step():
        turn[0] += 1
        if turn[0] > 2:
            next(work, None)

    pipelined(4, [scores, values, lambda h: None, tail], step)
    return out_add(g, "ml_out", 0, zh, zl, tz)


def swa(g, tx):
    per_k, r, tr = second_norm(g, 2, 1, tx)
    fa = g.fa
    q, k = fa[:, 2048:4096], fa[:, 4096:5120]
    V = fa[:, 5120:5632]
    o = fa[:, 5632:7680]
    base = [g.pe.last(), g.act.last(), g.dve.last()]
    tq = []
    gq = g.small[:, 540:541]
    t0 = g.v_ts(gq, g.P("sw_q_norm", 0), 0.125, None, ALU.mult, None, *base)
    norms = HeadNorms(g, 64, g.C("ones64", 0, 128), fa[:, 7680:10752], fa[:, 10752:13824], *base)
    for n in range(6):
        dst, gain, tg = ((q[:, n * 512:(n + 1) * 512], gq, t0) if n < 4 else
                         (k[:, (n - 4) * 512:(n - 3) * 512], g.P("sw_k_norm", 0), None))
        (ps, tok), = g.proj("sw_in", n, 8, 256, g.hh, g.hl, [], per_k=per_k)
        norms.begin(dst, gain, evac_scaled(g, dst, ps, tok, r, tr, *base), tg)
    banks = [g.ps.get() for _ in range(2)]
    rc, trc = token_factor(g, r, tr)
    norms.products()
    tok = token_major(g, "sw_in", [6], 256, 0, banks, per_k)
    tq = list(norms.finish())
    tv = []
    for tb in range(2):
        t = g.v_ts(V[:, tb * 256:(tb + 1) * 256], banks[tb].ap[:, 0:256], rc[:, tb:tb + 1], None, ALU.mult, None,
                   tok, trc, *base)
        g.ps.put(banks[tb], t)
        tv.append(t)
    zh, zl = g.ra[:, 0:2048], g.ra[:, 2048:4096]
    tz, held, po = [], {}, {}
    for u in g.sring.bufs:
        u.free = [*u.free, *base]

    def scores(h):
        c, p0, gk = h // 2, 64 * (h % 2), h // 4
        ps = g.ps.get()
        g.mm(ps.ap[:, 0:128], q[p0:p0 + 64, c * T:c * T + 128], k[p0:p0 + 64, gk * T:gk * T + 128],
             after=[*tq, *ps.free], inc=False)
        tok = g.mm(ps.ap[:, 128:384], q[p0:p0 + 64, c * T + 128:(c + 1) * T], k[p0:p0 + 64, gk * T:(gk + 1) * T])
        u = g.sring.get()
        slope = 2.0 ** (-8.0 * (h + 1) / 16)
        held[h] = (u, softmax3(g, u, tok, ps, (g.C("dist3", 0, 384), slope), 1.0, sink=g.P("sw_sinks", h)))

    def scale(h):
        u, state = held[h]
        held[h] = (u, softmax3_scale(g, u, state))

    def turn(h):
        u, ta = held[h]
        pt, tE, tpt = turn3(g, u.ap, [ta])
        g.sring.put(u, tE)
        held[h] = (pt, tpt)

    def values(h):
        c, p0, gk = h // 2, 64 * (h % 2), h // 4
        pt, tpt = held.pop(h)
        if h % 2 == 0:
            po[0] = g.ps.get()
        b = po[0]
        g.mm(b.ap[p0:p0 + 64, 0:256], V[:, gk * 64:(gk + 1) * 64], pt.ap[:, 0:256], last=False, inc=False,
             after=[tpt, *tv, *b.free])
        tok = g.mm(b.ap[p0:p0 + 64, 128:256], V[:, 256 + gk * 64:256 + (gk + 1) * 64], pt.ap[:, 256:384], first=False)
        g.tmp.put(pt, tok)
        if h % 2:
            oo = o[:, c * T:(c + 1) * T]
            t = g.v_copy(oo, b.ap[:, 0:256], tok, *base)
            g.ps.put(b, t)
            tz.append(g.split_act(g.xk(zh, c), g.xk(zl, c), oo, t, *base)[1])

    pipelined(16, [scores, scale, turn, values], lambda: None)
    return out_add(g, "sw_out", 0, zh, zl, tz)


def ple(g, layer, tx):
    before = [g.pe.last(), g.act.last(), g.dve.last()]
    per_k, r, tr = second_norm(g, layer, 3, tx)
    gate = g.fa[:, 2048:4096]
    base = [g.pe.last(), g.act.last(), g.dve.last()]
    pt = g.fa[:, 4096:4608]
    ph, pl = g.ra[:, 0:512], g.ra[:, 512:1024]
    tg = []
    for j in range(4):
        (ps, tok), = g.proj("ple_gate", layer * 4 + j, 8, 256, g.hh, g.hl, [], per_k=per_k)
        s = gate[:, j * 512:(j + 1) * 512]
        t = evac_scaled(g, s, ps, tok, r, tr, *base)
        tg.append(tanh_half(g, s, s, t))
        if j == 0:
            g.sp.dma(lambda e: e.dma_start(pt, g.args["pT"][layer]), g.s_p[1], *before)
        if j == 2:
            tp = g.split_act(ph, pl, pt, (g.s_p[1], 16 * (layer + 1)), *base)
    w = g.weight("ple_proj", layer)
    tx_new = []
    for j in range(4):
        ps = g.ps.get()
        for c in range(2):
            tok = g.group(w, 2, 1024, ph, pl, (2 * j + c) * 128, ps.ap[:, c * T:(c + 1) * T], [*tp, *ps.free])
        s = gate[:, j * 512:(j + 1) * 512]
        t = g.v_stt(s, s, 1.0, ps.ap[:, :], ALU.add, ALU.mult, tok, tg[j])
        g.ps.put(ps, t)
        xs = g.x[:, j * 512:(j + 1) * 512]
        tx_new.append(g.v_stt(xs, s, 0.5, xs, ALU.mult, ALU.add, t, base[1]))
    g.done(w, tok)
    return tx_new


STAGES = ["mix0", "ffn0", "mix1", "ffn1"] + [f"{a}{n}" for n in range(4) for a in ("h1_", "mx_", "h2_", "pl_")]


def emit(g, start=0, stop=99):
    t0, tc = load_small(g)
    g.dve.wait(t0)
    g.act.wait(t0)
    g.pe.wait(t0)
    tx = t0
    g.t_sc = exp_silu(g, g.sc[:, 0:8], g.par[:, PARAM_COLS["c"]:PARAM_COLS["c"] + 8], g.small[:, 570:578], [t0])
    g.con_tok = [tc]
    g.depth, depth = 1, g.depth
    for j in range(8):
        modulation_tile(g, 0, j, ("dve", "pe", "dve", "dve", "pe", "dve", "dve", "dve")[j])
    finish_modulation(g)
    g.depth = depth
    g.prefetch()
    g.dve.wait(tc)
    g.act.wait(tc)
    g.pe.wait(tc)
    g.pool.wait(tc)
    with ExitStack() as ctx:
        g.scope(ctx, 1, 11392, 8704)
        for lay in range(2):
            mod = g.mod[:, lay * 48:(lay + 1) * 48]
            if start <= 2 * lay < stop:
                tx = mix_first(g, lay, mod)
            if start <= 2 * lay + 1 < stop:
                tx = first_ffn(g, lay, mod)
    with ExitStack() as ctx:
        g.scope(ctx, 2, 15104, 4096)
        for layer in range(4):
            s = 4 + 4 * layer
            if start <= s < stop:
                tx = second_ffn(g, layer, 0, tx)
            if start <= s + 1 < stop:
                g.share = True
                tx = [lambda: hgrn(g, layer, layer // 3, tx), lambda: mlstm(g, tx), lambda: swa(g, tx)][layer % 3]()
                g.share = False
            if start <= s + 2 < stop:
                tx = second_ffn(g, layer, 1, tx)
            if start <= s + 3 < stop:
                tx = ple(g, layer, tx)
    g.sp.dma(lambda e: e.dma_start(g.args["out"], g.x[:, :]), g.s_out, *(tx if isinstance(tx, list) else [tx]))
    g.sp.wait((g.s_out, 16))


def build(nc: bass.Bass, args, order, start=0, stop=99):
    with ExitStack() as ctx:
        g = Program(nc, ctx, args, order)
        emit(g, start, stop)
        block = ctx.enter_context(nc.Block())

        @block.sync
        def _(eng):
            g.sp.play(eng)

        @block.scalar
        def _(eng):
            g.act.play(eng)

        @block.vector
        def _(eng):
            g.dve.play(eng)

        @block.tensor
        def _(eng):
            g.pe.play(eng)

        @block.gpsimd
        def _(eng):
            g.pool.play(eng)


def cols(v):
    v = np.asarray(v)
    return v.reshape(-1, 128).T


def rows_to(v, n=128):
    a = np.zeros((128, v.shape[1]), np.float32)
    a[:v.shape[0]] = v
    return a


def layout(i):
    par = [cols(i["c"]), cols(i["g_pre_mix"]), cols(i["b_ada"]),
           rows_to(np.stack([i[n][l] for l in range(2) for n in ("da_lam_q1", "da_lam_k1", "da_lam_q2", "da_lam_k2")], 1)),
           cols(i["da_g_subln"]), cols(i["mla_g_cq"]), cols(i["mla_g_ckv"]), cols(i["sc_conv"]), cols(i["cf_conv"]),
           cols(i["cf_conv_b"]), cols(i["cf_ln_g"]), cols(i["cf_ln_b"]), cols(i["g_post_mix"]), cols(i["g_pre_ffn"]),
           cols(i["ffn_conv"]), cols(i["g_post_ffn"]), cols(i["norm_gains_2"]), cols(i["hg_lower_bounds_2"]),
           cols(i["hg_g_norm_2"]), rows_to(np.asarray(i["ml_b_if_2"]).reshape(2, 4).T), cols(i["ml_norm_2"]),
           np.concatenate([np.asarray(i["sw_q_norm_2"]).T] * 2, 0), np.concatenate([np.asarray(i["sw_k_norm_2"]).T] * 2, 0),
           np.broadcast_to(np.asarray(i["sw_sinks_2"]), (128, 16)),
           np.asarray(i["ml_w_if_2"])[0].reshape(8, 128, 8).transpose(1, 0, 2).reshape(128, 64)]
    par = np.concatenate([np.asarray(p) for p in par], 1)
    assert par.shape == (128, NPAR)

    def kn(ws, n, plan=None):
        return np.stack([tiles_kn(w, c) for w in ws for c in (plan or [_span(a, n) for a in range(0, w.shape[1], n)])])

    dup = [sum([_span(1024 + 64 * (2 * a + b // 2), 64) for b in range(4)], []) for a in range(2)]
    gu = [_span(128 * a, 128) + _span(2816 + 128 * a, 128) for a in range(22)]

    def ko(ws):
        return np.stack([np.ascontiguousarray(w[a:a + 256].reshape(2, 128, 1024).transpose(1, 0, 2)).reshape(128, 2048)
                         for w in ws for a in range(0, 2816, 256)])

    out = {
        "params": par, "consts": constants(), "positions": np.asarray(i["positions"]),
        "xT": np.ascontiguousarray(np.asarray(i["x"])[0].T.reshape(8, 128, 256).transpose(1, 0, 2)).reshape(128, 2048),
        "pT": np.ascontiguousarray(np.asarray(i["p_2"])[:, 0].transpose(0, 2, 1).reshape(4, 2, 128, 256)
                                   .transpose(0, 2, 1, 3)).reshape(4, 128, 512),
        "w_ada": kn(i["w_ada"], 256), "w_in": kn(i["w_in"], 0, WIN),
        "w_mc": kn(i["w_in"], 0, [_span(2048, 160)]),
        "da_w_o": kn(i["da_w_o"], 512), "mla_w_o": kn(i["mla_w_o"], 512), "sc_w_o": kn(i["sc_w_o"], 512),
        "cf_w_o": kn(i["cf_w_o"], 512), "mla_w_uq": kn(i["mla_w_uq"], 384), "mla_w_ukv": kn(i["mla_w_ukv"], 1024),
        "w_mix_out": kn(i["w_mix_out"], 256), "w_up": kn(i["w_up"], 0, gu), "w_down": ko(i["w_down"]),
        "w_gu": kn(np.asarray(i["w_ffn_gu_2"]).reshape(8, 1024, 5632), 0, gu),
        "w_dn": ko(np.asarray(i["w_ffn_down_2"]).reshape(8, 2816, 1024)),
        "ple_gate": kn(i["w_ple_gate_2"], 256), "ple_proj": kn(i["w_ple_proj_2"], 1024),
        "hg_in": kn(i["hg_w_in_2"], 256), "hg_out": kn(i["hg_w_out_2"], 256),
        "ml_in": kn(i["ml_w_qkvo_2"], 256), "ml_out": kn(i["ml_w_out_2"], 256),
        "sw_in": kn(i["sw_w_qkv_2"], 0, [_span(256 * a, 256) for a in range(4)] + dup + [_span(1280, 256)]), "sw_out": kn(i["sw_w_o_2"], 256),
    }
    return out


def weight_order(start=0, stop=99):
    out = []

    def add(name, *ns, split=True):
        out.extend((name, n, split) for n in ns)

    def ride(start, every, tiles):
        rest = out[start:]
        del out[start:]
        tiles = list(tiles)
        for i, t in enumerate(rest):
            out.append(t)
            if tiles and i % every == 0 and i < len(rest) - 1:
                add("w_ada", tiles.pop(0), split=False)
        assert not tiles

    def ffn_tiles(up, up0, down, dn0):
        for p in range(NF // 2):
            for c in (2 * p, 2 * p + 1):
                add(up, up0 + c)
            if p:
                add(down, dn0 + p - 1)
        add(down, dn0 + NF // 2 - 1)

    def merge_tiles(lay, wo, branch):
        for n in range(2):
            if branch != 2:
                add(wo, lay * 2 + n)
            if branch is not None:
                add("w_in", *[lay * 34 + GATE0 + 4 * branch + 2 * n + i for i in range(2)])
            if branch == 2:
                add(wo, lay * 2 + n)

    add("w_ada", *range(8), split=False)
    for lay in range(2):
        if start <= 2 * lay < stop:
            w = lay * 34
            first = len(out)
            add("w_in", *range(w, w + SCU0), w + MLA0, w + MLA0 + 1)
            add("w_mc", lay)
            add("w_in", *range(w + SCU0, w + MLA0))
            merge_tiles(lay, "sc_w_o", 2)
            add("mla_w_uq", 2 * lay, 2 * lay + 1)
            add("mla_w_ukv", lay)
            add("w_in", *range(w + GATE0 + 4, w + GATE0 + 8))
            merge_tiles(lay, "da_w_o", 0)
            merge_tiles(lay, "cf_w_o", 3)
            merge_tiles(lay, "mla_w_o", None)
            add("w_mix_out", *range(4 * lay, 4 * lay + 4))
            ride(first, *((3, range(8, 25)) if lay == 0 else (4, range(36, 48))))
        if start <= 2 * lay + 1 < stop:
            first = len(out)
            ffn_tiles("w_up", lay * 22, "w_down", lay * 11)
            if lay == 0:
                ride(first, 3, range(25, 36))
    for layer in range(4):
        s = 4 + 4 * layer
        j = layer // 3
        if start <= s < stop:
            ffn_tiles("w_gu", layer * 44, "w_dn", layer * 22)
        if start <= s + 1 < stop:
            if layer % 3 == 0:
                for a in (0, 2):
                    add("hg_in", *[16 * j + a + n for n in (0, 1, 4, 5, 8, 9)])
                add("hg_in", *range(16 * j + 12, 16 * j + 16))
                add("hg_out", *range(4 * j, 4 * j + 4))
            elif layer == 1:
                add("ml_in", *range(12))
                add("ml_out", *range(4))
            else:
                add("sw_in", *range(7))
                add("sw_out", *range(4))
        if start <= s + 2 < stop:
            ffn_tiles("w_gu", layer * 44 + 22, "w_dn", layer * 22 + 11)
        if start <= s + 3 < stop:
            add("ple_gate", *range(layer * 4, layer * 4 + 4))
            add("ple_proj", layer)
    return out


def kernel(**inputs):
    import concourse.bacc as _bacc
    from concourse.bass_utils import run_bass_kernel_spmd as _run

    arrays = layout({k: np.asarray(v) for k, v in inputs.items()})
    nc = _bacc.Bacc("TRN2", target_bir_lowering=False, num_devices=1)
    args = {k: nc.dram_tensor(k, v.shape, mybir.dt.from_np(v.dtype), kind="ExternalInput").ap() for k, v in arrays.items()}
    args["out"] = nc.dram_tensor("out", (128, 2048), F32, kind="ExternalOutput").ap()
    build(nc, args, weight_order())
    r = _run(nc, [arrays], core_ids=[0])
    o = r.results[0]["out"]
    return np.ascontiguousarray(o.reshape(128, 8, 256).transpose(1, 0, 2).reshape(1024, 256).T)[None]
```
